# Optimizing a Trainium2 kernel written in Bass

```python
import math
import jax, jax.numpy as jnp
from jax import lax
import numpy as np

D_MODEL = 1024
BATCH = 1
SEQ = 1024
DEPTH = 2

RET_HEADS = 4
RET_DK = 128
RET_DV = 256
RET_CHUNK = 128
RET_THETA = 10000.0
DIL_HEADS = 8
DIL_HD = 64
DIL_PAIRS = ((128, 1), (512, 4), (2048, 16))
DIL_BLOCK = 128
ROPE_THETA = 500000.0
ROPE_DIMS = DIL_HD // 4
GDN_HEADS = 8
GDN_DK = 128
GDN_DV = 128
GDN_CHUNK = 64
GDN_CONV = 4
D_FF = 2816
FFN_CONV = 3
DN_ALPHA = (2.0 * DEPTH) ** 0.25
DN_BETA = (8.0 * DEPTH) ** -0.25
EPS = 1e-5
N_EVEN = (DEPTH + 1) // 2
N_ODD = DEPTH // 2

RET_QK_W = RET_HEADS * RET_DK
RET_V_W = RET_HEADS * RET_DV
DIL_W = DIL_HEADS * DIL_HD
EV_IN = 2 * RET_QK_W + 2 * RET_V_W + 3 * DIL_W
EV_MIX = RET_V_W + DIL_W
GDN_W = GDN_HEADS * GDN_DK
OD_IN = 4 * GDN_W + 2 * GDN_HEADS

kernel_name = "hybrid_retention_dilated_gdn_deepnorm"

F32 = jnp.float32

def _layernorm(x, g, b):
    xf = x.astype(F32)
    mu = jnp.mean(xf, -1, keepdims=True)
    var = jnp.mean(jnp.square(xf - mu), -1, keepdims=True)
    return ((xf - mu) * lax.rsqrt(var + EPS) * g.astype(F32) + b.astype(F32)).astype(x.dtype)

def _rms(xf):
    return xf * lax.rsqrt(jnp.mean(xf * xf, -1, keepdims=True) + EPS)

def _l2norm(xf):
    return xf * lax.rsqrt(jnp.sum(xf * xf, -1, keepdims=True) + 1e-6)

def _heads(t, n_heads):
    b, s, w = t.shape
    return t.reshape(b, s, n_heads, w // n_heads).transpose(0, 2, 1, 3)

def _merge(t):
    b, h, s, d = t.shape
    return t.transpose(0, 2, 1, 3).reshape(b, s, h * d)

def _rotary(x, positions, n_rot, theta):
    half = n_rot // 2
    inv = jnp.power(theta, -jnp.arange(half, dtype=F32) * 2.0 / n_rot)
    ang = positions.astype(F32)[:, None, :, None] * inv
    cos, sin = jnp.cos(ang), jnp.sin(ang)
    xf = x.astype(F32)
    x1, x2 = xf[..., :half], xf[..., half:n_rot]
    out = jnp.concatenate([x1 * cos - x2 * sin, x2 * cos + x1 * sin, xf[..., n_rot:]], -1)
    return out.astype(x.dtype)

def _causal_dwconv(x, w):
    k_w = w.shape[0]
    s = x.shape[1]
    xp = jnp.pad(x, ((0, 0), (k_w - 1, 0), (0, 0)))
    return sum(xp[:, j:j + s] * w[j] for j in range(k_w))

def _retention(q, k, v):
    b, h, s, dk = q.shape
    dv = v.shape[-1]
    c = RET_CHUNK
    n = s // c
    lg = jnp.log1p(-jnp.power(2.0, -5.0 - jnp.arange(h, dtype=F32)))
    idx = jnp.arange(c, dtype=F32)
    rel = idx[:, None] - idx[None, :]
    dmat = jnp.where(rel >= 0, jnp.exp(jnp.maximum(rel, 0.0) * lg[:, None, None]), 0.0)
    zeta = jnp.exp((c - 1 - idx) * lg[:, None])
    xi = jnp.exp((idx + 1) * lg[:, None])
    g_chunk = jnp.exp(c * lg)
    qc = q.reshape(b, h, n, c, dk)
    kc = k.reshape(b, h, n, c, dk)
    vc = v.reshape(b, h, n, c, dv)
    scores = jnp.einsum('bhnid,bhnjd->bhnij', qc, kc) * dmat[None, :, None]
    o_intra = jnp.einsum('bhnij,bhnje->bhnie', scores, vc)
    kv = jnp.einsum('bhnjd,bhnje->bhnde', kc * zeta[None, :, None, :, None], vc)

    def step(r_state, kv_n):
        return r_state * g_chunk[None, :, None, None] + kv_n, r_state

    _, r_prev = lax.scan(step, jnp.zeros((b, h, dk, dv), F32), jnp.moveaxis(kv, 2, 0))
    r_prev = jnp.moveaxis(r_prev, 0, 2)
    o_inter = jnp.einsum('bhnid,bhnde->bhnie', qc, r_prev) * xi[None, :, None, :, None]
    return (o_intra + o_inter).reshape(b, h, s, dv)

def _dilated_branch(q, k, v, window, dilation):
    b, h, s, hd = q.shape
    L = s // dilation
    wd = window // dilation
    qb_sz = DIL_BLOCK
    nb = -(-L // qb_sz)
    lp = nb * qb_sz

    def sub(t):
        t = t.reshape(b, h, L, dilation, hd).transpose(0, 1, 3, 2, 4)
        return jnp.pad(t, ((0, 0), (0, 0), (0, 0), (0, lp - L), (0, 0)))

    def band(t):
        tb = t.reshape(b, h, dilation, nb, qb_sz, hd)
        prev = jnp.pad(tb, ((0, 0), (0, 0), (0, 0), (1, 0), (0, 0), (0, 0)))[:, :, :, :nb]
        return jnp.concatenate([prev, tb], axis=4)

    qs = sub(q).reshape(b, h, dilation, nb, qb_sz, hd)
    kb = band(sub(k))
    vb = band(sub(v))
    qpos = jnp.arange(nb)[:, None] * qb_sz + jnp.arange(qb_sz)[None, :]
    kpos = jnp.arange(nb)[:, None] * qb_sz - qb_sz + jnp.arange(2 * qb_sz)[None, :]
    dist = qpos[:, :, None] - kpos[:, None, :]
    mask = (dist >= 0) & (dist <= wd) & (kpos[:, None, :] >= 0)
    sc = jnp.einsum('bhrnqd,bhrnkd->bhrnqk', qs, kb).astype(F32) * (hd ** -0.5)
    sc = jnp.where(mask, sc, -jnp.inf)
    m = jnp.max(sc, -1)
    p = jnp.exp(sc - m[..., None])
    l = jnp.sum(p, -1)
    o = jnp.einsum('bhrnqk,bhrnkd->bhrnqd', p, vb.astype(F32)) / l[..., None]

    def unsub(t):
        tail = t.shape[5:]
        t = t.reshape(b, h, dilation, lp, *tail)[:, :, :, :L]
        t = jnp.moveaxis(t, 2, 3)
        return t.reshape(b, h, s, *tail)

    return unsub(o), unsub(m), unsub(l)

def _dilated_attention(q, k, v):
    outs = [_dilated_branch(q, k, v, w, r) for (w, r) in DIL_PAIRS]
    m_all = jnp.stack([m for (_, m, _) in outs])
    m_max = jnp.max(m_all, 0)
    wts = jnp.stack([l * jnp.exp(m - m_max) for (_, m, l) in outs])
    o_all = jnp.stack([o for (o, _, _) in outs])
    return jnp.sum(wts[..., None] * o_all, 0) / jnp.sum(wts, 0)[..., None]

def _even_mixer(x, positions, w_in, w_out):
    hproj = x @ w_in
    sizes = (RET_QK_W, RET_QK_W, RET_V_W, RET_V_W, DIL_W, DIL_W, DIL_W)
    offs = [0]
    for sz in sizes:
        offs.append(offs[-1] + sz)
    qa, ka, va, ga, qb, kb, vb = [hproj[..., offs[i]:offs[i + 1]] for i in range(len(sizes))]
    qa = _rotary(_heads(qa, RET_HEADS), positions, RET_DK, RET_THETA).astype(F32)
    ka = _rotary(_heads(ka, RET_HEADS), positions, RET_DK, RET_THETA).astype(F32) * (RET_DK ** -0.5)
    ya = _rms(_retention(qa, ka, _heads(va, RET_HEADS).astype(F32)))
    ya = (_merge(ya) * jax.nn.silu(ga.astype(F32))).astype(x.dtype)
    qb = _rotary(_heads(qb, DIL_HEADS), positions, ROPE_DIMS, ROPE_THETA)
    kb = _rotary(_heads(kb, DIL_HEADS), positions, ROPE_DIMS, ROPE_THETA)
    yb = _merge(_dilated_attention(qb, kb, _heads(vb, DIL_HEADS))).astype(x.dtype)
    return jnp.concatenate([ya, yb], -1) @ w_out

def _gated_delta_rule(q, k, v, beta, g):
    b, h, s, dk = q.shape
    dv = v.shape[-1]
    c = GDN_CHUNK
    n = s // c
    ch = lambda t: t.reshape(b, h, n, c, *t.shape[3:])
    q, k, v, beta, g = ch(q), ch(k), ch(v), ch(beta), ch(g)
    gc = jnp.cumsum(g, -1)
    tri = jnp.tril(jnp.ones((c, c), bool))
    strict = jnp.tril(jnp.ones((c, c), bool), -1)
    diff = gc[..., :, None] - gc[..., None, :]
    decay = jnp.where(tri, jnp.exp(jnp.where(tri, diff, 0.0)), 0.0)
    kb = k * beta[..., None]
    a_mat = jnp.eye(c, dtype=F32) + jnp.where(strict, jnp.einsum('bhnid,bhnjd->bhnij', kb, k) * decay, 0.0)
    rhs = jnp.concatenate([v * beta[..., None], kb * jnp.exp(gc)[..., None]], -1)
    sol = lax.linalg.triangular_solve(a_mat, rhs, left_side=True, lower=True, unit_diagonal=True)
    u, w = sol[..., :dv], sol[..., dv:]
    attn = jnp.where(tri, jnp.einsum('bhnid,bhnjd->bhnij', q, k) * decay, 0.0)
    glast = gc[..., -1]
    k_dec = k * jnp.exp(glast[..., None] - gc)[..., None]
    q_dec = q * jnp.exp(gc)[..., None]

    def step(state, inp):
        qd_n, u_n, w_n, attn_n, kd_n, gl_n = inp
        v_new = u_n - jnp.einsum('bhcd,bhde->bhce', w_n, state)
        o_n = jnp.einsum('bhcd,bhde->bhce', qd_n, state) + jnp.einsum('bhij,bhje->bhie', attn_n, v_new)
        state = state * jnp.exp(gl_n)[..., None, None] + jnp.einsum('bhcd,bhce->bhde', kd_n, v_new)
        return state, o_n

    xs = tuple(jnp.moveaxis(t, 2, 0) for t in (q_dec, u, w, attn, k_dec, glast))
    _, o = lax.scan(step, jnp.zeros((b, h, dk, dv), F32), xs)
    return jnp.moveaxis(o, 0, 2).reshape(b, h, s, dv)

def _odd_mixer(x, w_in, conv_w, a_log, dt_bias, norm_w, w_out):
    hproj = x @ w_in
    qkv = jax.nn.silu(_causal_dwconv(hproj[..., :3 * GDN_W], conv_w))
    gate = hproj[..., 3 * GDN_W:4 * GDN_W]
    b_raw = hproj[..., 4 * GDN_W:4 * GDN_W + GDN_HEADS].astype(F32)
    a_raw = hproj[..., 4 * GDN_W + GDN_HEADS:].astype(F32)
    q = _l2norm(_heads(qkv[..., :GDN_W], GDN_HEADS).astype(F32)) * (GDN_DK ** -0.5)
    k = _l2norm(_heads(qkv[..., GDN_W:2 * GDN_W], GDN_HEADS).astype(F32))
    v = _heads(qkv[..., 2 * GDN_W:], GDN_HEADS).astype(F32)
    beta = jax.nn.sigmoid(b_raw).transpose(0, 2, 1)
    g = (-jnp.exp(a_log.astype(F32)) * jax.nn.softplus(a_raw + dt_bias.astype(F32))).transpose(0, 2, 1)
    o = _rms(_gated_delta_rule(q, k, v, beta, g)) * norm_w.astype(F32)
    o = (_merge(o) * jax.nn.silu(gate.astype(F32))).astype(x.dtype)
    return o @ w_out

def _conv_ffn(x, w_up, conv_w, conv_b, w_down):
    hproj = _causal_dwconv(x @ w_up, conv_w) + conv_b
    gate, val = hproj[..., :D_FF], hproj[..., D_FF:]
    return (jax.nn.silu(gate) * val) @ w_down

def setup_inputs(seed: int = 0) -> dict:
    key = jax.random.key(seed)
    ks = jax.random.split(key, 20)
    nrm = lambda kk, shape, scale: jax.random.normal(kk, shape, F32) * scale
    x = nrm(ks[0], (BATCH, SEQ, D_MODEL), 1.0)
    start = jax.random.randint(ks[1], (BATCH, 1), 0, 4096, dtype=jnp.int32)
    positions = start + jnp.arange(SEQ, dtype=jnp.int32)[None, :]
    ev_w_in = nrm(ks[2], (N_EVEN, D_MODEL, EV_IN), D_MODEL ** -0.5)
    ev_w_out = nrm(ks[3], (N_EVEN, EV_MIX, D_MODEL), EV_MIX ** -0.5 * DN_BETA)
    od_w_in = nrm(ks[4], (N_ODD, D_MODEL, OD_IN), D_MODEL ** -0.5)
    od_conv_w = nrm(ks[5], (N_ODD, GDN_CONV, 3 * GDN_W), GDN_CONV ** -0.5)
    od_a_log = jnp.log(jax.random.uniform(ks[6], (N_ODD, GDN_HEADS), F32, 1.0, 16.0))
    dt = jnp.exp(jax.random.uniform(ks[7], (N_ODD, GDN_HEADS), F32, math.log(1e-3), math.log(1e-1)))
    od_dt_bias = dt + jnp.log(-jnp.expm1(-dt))
    od_norm_w = 1.0 + nrm(ks[8], (N_ODD, GDN_DV), 0.02)
    od_w_out = nrm(ks[9], (N_ODD, GDN_W, D_MODEL), GDN_W ** -0.5 * DN_BETA)
    ffn_w_up = nrm(ks[10], (DEPTH, D_MODEL, 2 * D_FF), D_MODEL ** -0.5)
    ffn_conv_w = nrm(ks[11], (DEPTH, FFN_CONV, 2 * D_FF), FFN_CONV ** -0.5)
    ffn_conv_b = nrm(ks[12], (DEPTH, 2 * D_FF), 0.01)
    ffn_w_down = nrm(ks[13], (DEPTH, D_FF, D_MODEL), D_FF ** -0.5 * DN_BETA)
    ln1_g = 1.0 + nrm(ks[14], (DEPTH, D_MODEL), 0.02)
    ln1_b = nrm(ks[15], (DEPTH, D_MODEL), 0.01)
    ln2_g = 1.0 + nrm(ks[16], (DEPTH, D_MODEL), 0.02)
    ln2_b = nrm(ks[17], (DEPTH, D_MODEL), 0.01)
    return {"x": x, "positions": positions, "ev_w_in": ev_w_in, "ev_w_out": ev_w_out,
            "od_w_in": od_w_in, "od_conv_w": od_conv_w, "od_a_log": od_a_log,
            "od_dt_bias": od_dt_bias, "od_norm_w": od_norm_w, "od_w_out": od_w_out,
            "ffn_w_up": ffn_w_up, "ffn_conv_w": ffn_conv_w, "ffn_conv_b": ffn_conv_b,
            "ffn_w_down": ffn_w_down, "ln1_g": ln1_g, "ln1_b": ln1_b,
            "ln2_g": ln2_g, "ln2_b": ln2_b}

def reference(x, positions, ev_w_in, ev_w_out, od_w_in, od_conv_w, od_a_log, od_dt_bias,
              od_norm_w, od_w_out, ffn_w_up, ffn_conv_w, ffn_conv_b, ffn_w_down,
              ln1_g, ln1_b, ln2_g, ln2_b):
    for layer in range(DEPTH):
        j = layer // 2
        if layer % 2 == 0:
            mix = _even_mixer(x, positions, ev_w_in[j], ev_w_out[j])
        else:
            mix = _odd_mixer(x, od_w_in[j], od_conv_w[j], od_a_log[j], od_dt_bias[j],
                             od_norm_w[j], od_w_out[j])
        x = _layernorm(DN_ALPHA * x + mix, ln1_g[layer], ln1_b[layer])
        ffn = _conv_ffn(x, ffn_w_up[layer], ffn_conv_w[layer], ffn_conv_b[layer], ffn_w_down[layer])
        x = _layernorm(DN_ALPHA * x + ffn, ln2_g[layer], ln2_b[layer])
    return x


_drawn_inputs = setup_inputs


def setup_inputs(seed=0):
    import zlib

    import numpy as np

    out = dict(_drawn_inputs(seed))
    spreads = {}
    factors = {'od_norm_w': 24.525, 'ffn_conv_b': 8.0, 'ln1_b': 3.571, 'ln2_b': 3.768}
    for name, (base, spread) in spreads.items():
        noise = np.random.default_rng([zlib.crc32(name.encode()), seed]).standard_normal(out[name].shape)
        drawn = base * np.exp(spread * noise) if base else spread * noise
        out[name] = __import__('jax').numpy.asarray(drawn.astype(out[name].dtype))
    for name, factor in factors.items():
        out[name] = (out[name] * factor).astype(out[name].dtype)
    return out
```

```python
from contextlib import ExitStack

import numpy as np

import concourse.bass as bass
import concourse.mybir as mybir
from concourse.alu_op_type import AluOpType as ALU

P = 128
SEQ = 1024
D = 1024
TT = SEQ // P
KD = D // P
NB = 512
HALF_T = TT // 2
HALF = SEQ // 2

RET_HEADS, RET_DK, RET_DV = 4, 128, 256
DIL_HEADS, DIL_HD = 8, 64
DIL_PAIRS = ((128, 1), (512, 4), (2048, 16))
ROPE_DIMS = DIL_HD // 4
EV_IN = 2 * RET_HEADS * RET_DK + 2 * RET_HEADS * RET_DV + 3 * DIL_HEADS * DIL_HD
EV_MIX = RET_HEADS * RET_DV + DIL_HEADS * DIL_HD
RET_IN = 2 * RET_HEADS * RET_DK + 2 * RET_HEADS * RET_DV
GDN_HEADS, GDN_DK, GDN_DV, GDN_CONV = 8, 128, 128, 4
GDN_W = GDN_HEADS * GDN_DK
D_FF = 2816
KF = D_FF // P
FFN_CONV = 3
DN_ALPHA = (2.0 * 2) ** 0.25
EPS = 1e-5

ACT = mybir.ActivationFunctionType
AX = mybir.AxisListType
F32 = mybir.dt.float32
F32R = mybir.dt.float32r
I32 = mybir.dt.int32
ds = bass.ds


class Scope:

    def __init__(self, nc, ctx, prefix):
        self.nc, self.ctx, self.prefix, self.sems = nc, ctx, prefix, []
        ctx.callback(self.clear)

    def sbuf(self, name, shape, dt=F32, side=None):
        return self.ctx.enter_context(self.nc.sbuf_tensor(f"{self.prefix}_{name}", shape, dt, side=side))

    def psum(self, name, shape, dt=F32):
        return self.ctx.enter_context(self.nc.psum_tensor(f"{self.prefix}_{name}", shape, dt))

    def sem(self, name):
        self.sems.append(self.nc.alloc_semaphore(name=f"{self.prefix}_{name}"))
        return self.sems[-1]

    def clear(self):
        if self.sems:
            self.nc.clear_and_free_semaphores(self.sems)
            self.nc.all_engine_barrier()


def f32(ap):
    return ap.bitcast(F32)


def transpose_phase(nc, name, src, k_tiles, ident, hi, lo):
    with ExitStack() as ctx:
        sc = Scope(nc, ctx, name)
        rows = sc.sbuf("rows", [P, 2, k_tiles * P])
        turned = sc.psum("turned", [P, 2, 4, NB] if k_tiles > 4 else [P, 2, 1, NB])
        rows_in = [sc.sem(f"rows_in{s}") for s in range(2)]
        turned_ready = sc.sem("turned_ready")
        hi_ready = sc.sem("hi_ready")
        lo_ready = sc.sem("lo_ready")
        done = hi_ready if lo is None else lo_ready

        def psum_view(s):
            return turned[:, s].rearrange("p b n -> p (b n)")[:, 0:k_tiles * P].rearrange("p (k t) -> p k t", t=P)

        block = ctx.enter_context(nc.Block())

        @block.sync
        def _(sp):
            with sp.Fori(0, TT // 2) as i:
                for s in range(2):
                    sp.wait_ge(turned_ready, 2 * i + s + 1)
                    sp.dma_start(rows[:, s], src[ds((2 * i + s) * P, P), :]).then_inc(rows_in[s], 16)

        @block.tensor
        def _(pe):
            pe.sem_inc(turned_ready, 2)
            with pe.Fori(0, TT // 2) as i:
                for s in range(2):
                    pe.wait_ge(rows_in[s], 16 * i + 16)
                    pe.wait_ge(done, 2 * i + s + 1)
                    for k in range(k_tiles):
                        mm = pe.transpose(psum_view(s)[:, k], rows[:, s, k * P:(k + 1) * P], ident[:])
                    mm.then_inc(turned_ready, 1)

        @block.scalar
        def _(act):
            if lo is None:
                act.sem_inc(hi_ready, 2)
            with act.Fori(0, TT // 2) as i:
                for s in range(2):
                    act.wait_ge(turned_ready, 2 * i + s + 3)
                    act.copy(hi[:, :, ds((2 * i + s) * P, P)], psum_view(s)).then_inc(hi_ready, 1)

        if lo is not None:
            @block.vector
            def _(dve):
                dve.sem_inc(lo_ready, 2)
                with dve.Fori(0, TT // 2) as i:
                    for s in range(2):
                        dve.wait_ge(hi_ready, 2 * i + s + 1)
                        tok = ds((2 * i + s) * P, P)
                        dve.tensor_tensor(lo[:, :, tok], psum_view(s), f32(hi[:, :, tok]),
                                          ALU.subtract).then_inc(lo_ready, 1)


def project_tokens(nc, name, xhi, xlo, w, n_tiles, out, col0):
    with ExitStack() as ctx:
        sc = Scope(nc, ctx, name)
        w_raw = sc.sbuf("w_raw", [P, KD, NB])
        w_hi = sc.sbuf("w_hi", [P, KD, NB], F32R)
        w_lo = sc.sbuf("w_lo", [P, KD, NB], F32R)
        stage = sc.sbuf("stage", [P, 2, HALF_T, NB])
        acc = sc.psum("acc", [P, 2, HALF_T, NB])
        w_in = [sc.sem(f"w_in{s}") for s in range(2)]
        hi_ready = sc.sem("hi_ready")
        lo_ready = sc.sem("lo_ready")
        w_used = sc.sem("w_used")
        half_done = sc.sem("half_done")
        acc_free = sc.sem("acc_free")
        stored = [sc.sem(f"stored{s}") for s in range(2)]
        KH = KD // 2

        block = ctx.enter_context(nc.Block())

        @block.sync
        def _(sp):
            with sp.Fori(0, n_tiles) as n:
                for s in range(2):
                    sp.wait_ge(lo_ready, KD * n + KH * (s + 1))
                    sp.dma_start(w_raw[:, s * KH:(s + 1) * KH, :],
                                 w[ds(n, 1), :, s * KH:(s + 1) * KH, :].rearrange("a p k n -> p (a k) n")
                                 ).then_inc(w_in[s], 16)

        @block.scalar
        def _(act):
            act.sem_inc(acc_free, 2)
            act.sem_inc(stored[0], 16)
            act.sem_inc(stored[1], 16)

            def split_hi(n):
                for k in range(KD):
                    if k % KH == 0:
                        act.wait_ge(w_in[k // KH], 16 * n + 16)
                    act.wait_ge(w_used, KD * n + k + 1)
                    act.copy(w_hi[:, k], w_raw[:, k]).then_inc(hi_ready, 1)

            def store_half(n, h):
                if h == 0:
                    act.wait_ge(half_done, n + 1)
                else:
                    act.wait_ge(w_used, KD * (n + 2))
                act.wait_ge(stored[h], 16 * n + 16)
                act.copy(stage[:, h], acc[:, h]).then_inc(acc_free, 1)
                act.wait_ge(acc_free, 2 * n + h + 3)
                rows = out[h * HALF:(h + 1) * HALF, ds(col0 + n * NB, NB)]
                act.dma_start(rows.rearrange("(t p) n -> p t n", p=P), stage[:, h]).then_inc(stored[h], 16)

            split_hi(0)
            if n_tiles > 1:
                with act.Fori(0, n_tiles - 1) as n:
                    store_half(n, 0)
                    split_hi(n + 1)
                    store_half(n, 1)
            store_half(n_tiles - 1, 0)
            store_half(n_tiles - 1, 1)
            for h in range(2):
                act.wait_ge(stored[h], 16 * n_tiles + 16)

        @block.vector
        def _(dve):
            dve.sem_inc(lo_ready, KD)
            with dve.Fori(0, n_tiles) as n:
                for k in range(KD):
                    dve.wait_ge(hi_ready, KD * n + k + 1)
                    dve.tensor_tensor(w_lo[:, k], w_raw[:, k], f32(w_hi[:, k]), ALU.subtract).then_inc(lo_ready, 1)

        @block.tensor
        def _(pe):
            pe.sem_inc(w_used, KD)
            with pe.Fori(0, n_tiles) as n:
                for h in range(2):
                    pe.wait_ge(acc_free, 2 * n + h + 1)
                    for k in range(KD):
                        if h == 0:
                            pe.wait_ge(lo_ready, KD * (n + 1) + k + 1)
                        for t in range(HALF_T):
                            tok = slice(h * HALF + t * P, h * HALF + (t + 1) * P)
                            pe.matmul(acc[:, h, t], xhi[:, k, tok], w_hi[:, k], start=(k == 0), stop=False)
                            pe.matmul(acc[:, h, t], xhi[:, k, tok], w_lo[:, k], start=False, stop=False)
                            mm = pe.matmul(acc[:, h, t], xlo[:, k, tok], w_hi[:, k],
                                           start=False, stop=(k == KD - 1))
                        if h == 1:
                            mm.then_inc(w_used, 1)
                    if h == 0:
                        mm.then_inc(half_done, 1)


def ffn_up(nc, name, xhi, xlo, w, taps_dram, h):
    with ExitStack() as ctx:
        sc = Scope(nc, ctx, name)
        w_raw = sc.sbuf("w_raw", [P, 2, KD, P])
        w_hi = sc.sbuf("w_hi", [P, 2, 2, KD, P], F32R)
        w_lo = sc.sbuf("w_lo", [P, 2, 2, KD, P], F32R)
        conv = sc.sbuf("conv", [P, 2, SEQ])
        taps = sc.sbuf("taps", [P, KF, 2, FFN_CONV + 1])
        acc = sc.psum("acc", [P, 2, 2, SEQ])
        taps_in = sc.sem("taps_in")
        w_in = sc.sem("w_in")
        hi_ready = sc.sem("hi_ready")
        lo_ready = sc.sem("lo_ready")
        prod_done = sc.sem("prod_done")
        tap_done = sc.sem("tap_done")
        tap_added = sc.sem("tap_added")
        gate_done = sc.sem("gate_done")
        acc_free = sc.sem("acc_free")
        h_done = sc.sem("h_done")

        def tap(j, part, c):
            return taps[:, ds(j, 1), part, c:c + 1].rearrange("p a c -> p (a c)")

        block = ctx.enter_context(nc.Block())

        @block.sync
        def _(sp):
            sp.dma_start(taps[:], taps_dram).then_inc(taps_in, 16)
            with sp.Fori(0, KF) as j:
                sp.wait_ge(lo_ready, j + 1)
                sp.dma_start(w_raw[:], w[ds(j, 1)].rearrange("a p g k n -> p (a g) k n")).then_inc(w_in, 16)

        @block.tensor
        def _(pe):
            pe.sem_inc(prod_done, 4)
            with pe.Fori(0, KF // 2) as i:
                for s in range(2):
                    j = 2 * i + s
                    pe.wait_ge(lo_ready, j + 2)
                    pe.wait_ge(acc_free, j + 1)
                    for g in range(2):
                        for k in range(KD):
                            for ww, xx in ((w_hi, xhi), (w_hi, xlo), (w_lo, xhi)):
                                for hf in range(2):
                                    tok = slice(hf * HALF, (hf + 1) * HALF)
                                    mm = pe.matmul(acc[:, s, g, tok], ww[:, s, g, k], xx[:, k, tok],
                                                   start=(k == 0 and ww is w_hi and xx is xhi),
                                                   stop=(k == KD - 1 and ww is w_lo))
                        mm.then_inc(prod_done, 1)

        @block.scalar
        def _(act):
            def split_hi(j, s):
                act.wait_ge(w_in, 16 * j + 16)
                act.wait_ge(prod_done, 2 * j + 2)
                act.copy(w_hi[:, s], w_raw[:]).then_inc(hi_ready, 1)

            def last_tap(j, s):
                act.wait_ge(h_done, j + 1)
                for g in range(2):
                    act.wait_ge(prod_done, 2 * j + g + 5)
                    act.activation(conv[:, g], acc[:, s, g], ACT.Identity, bias=tap(j, g, FFN_CONV),
                                   scale=tap(j, g, FFN_CONV - 1)).then_inc(tap_done, 1)
                act.wait_ge(gate_done, 2 * j + 1)
                act.activation(conv[:, 0], conv[:, 0], ACT.Silu).then_inc(gate_done, 1)

            act.wait_ge(taps_in, 16)
            split_hi(0, 0)
            with act.Fori(0, KF // 2 - 1) as i:
                for s in range(2):
                    split_hi(2 * i + s + 1, 1 - s)
                    last_tap(2 * i + s, s)
            split_hi(KF - 1, 1)
            last_tap(KF - 2, 0)
            last_tap(KF - 1, 1)

        @block.vector
        def _(dve):
            dve.sem_inc(lo_ready, 1)
            dve.sem_inc(acc_free, 2)
            dve.sem_inc(h_done, 1)
            def split_lo(j, s):
                dve.wait_ge(hi_ready, j + 1)
                dve.tensor_tensor(w_lo[:, s], w_raw[:], f32(w_hi[:, s]), ALU.subtract).then_inc(lo_ready, 1)

            def other_taps(j, s):
                for g in range(2):
                    dve.wait_ge(tap_done, 2 * j + g + 1)
                    c = conv[:, g]
                    dve.scalar_tensor_tensor(out=c[:, 1:SEQ], in0=acc[:, s, g, 0:SEQ - 1], scalar=tap(j, g, 1),
                                             in1=c[:, 1:SEQ], op0=ALU.mult, op1=ALU.add).then_inc(tap_added, 1)
                    dve.wait_ge(tap_added, 2 * j + g + 1)
                    last = dve.scalar_tensor_tensor(out=c[:, 2:SEQ], in0=acc[:, s, g, 0:SEQ - 2],
                                                    scalar=tap(j, g, 0), in1=c[:, 2:SEQ],
                                                    op0=ALU.mult, op1=ALU.add)
                    last.then_inc(gate_done if g == 0 else acc_free, 1)
                dve.wait_ge(gate_done, 2 * j + 2)
                dve.wait_ge(acc_free, j + 3)
                dve.tensor_tensor(h[:, ds(j, 1), :].rearrange("p a t -> p (a t)"), conv[:, 0], conv[:, 1],
                                  ALU.mult).then_inc(h_done, 1)

            dve.wait_ge(taps_in, 16)
            split_lo(0, 0)
            with dve.Fori(0, KF // 2 - 1) as i:
                for s in range(2):
                    split_lo(2 * i + s + 1, 1 - s)
                    other_taps(2 * i + s, s)
            split_lo(KF - 1, 1)
            other_taps(KF - 2, 0)
            other_taps(KF - 1, 1)


def project_out(nc, name, a, k_tiles, w, resid, gain, bias, ident, out, hi=None, lo=None):
    with ExitStack() as ctx:
        sc = Scope(nc, ctx, name)
        w_raw = sc.sbuf("w_raw", [P, 2, D])
        w_hi = sc.sbuf("w_hi", [P, 2, D], F32R)
        w_lo = sc.sbuf("w_lo", [P, 2, D], F32R)
        a_hi = sc.sbuf("a_hi", [P, 2, HALF], F32R)
        a_lo = sc.sbuf("a_lo", [P, 2, HALF], F32R)
        y = sc.sbuf("y", [P, TT, D])
        gain_b = sc.sbuf("gain_b", [P, D])
        bias_b = sc.sbuf("bias_b", [P, D])
        stats = sc.sbuf("stats", [P, TT, 2, 6])
        mean_var = sc.sbuf("mean_var", [P, TT, 2])
        rstd = sc.sbuf("rstd", [P, TT, 1])
        power = sc.sbuf("power", [P, 1])
        acc = sc.psum("acc", [P, HALF_T, 2, NB])
        w_in = [sc.sem(f"w_in{s}") for s in range(2)]
        resid_in = sc.sem("resid_in")
        affine_in = sc.sem("affine_in")
        power_set = sc.sem("power_set")
        hi_ready = sc.sem("hi_ready")
        lo_ready = sc.sem("lo_ready")
        step_done = sc.sem("step_done")
        summed = sc.sem("summed")
        stats_done = sc.sem("stats_done")
        moments = sc.sem("moments")
        rstd_ready = sc.sem("rstd_ready")
        centred = sc.sem("centred")
        finished = sc.sem("finished")
        turned = sc.sem("turned")
        hi_copied = sc.sem("hi_copied")
        lo_copied = sc.sem("lo_copied")
        stored = sc.sem("stored")
        KP = k_tiles // 2
        PEELED = 8

        def sums(t):
            return acc[:, t % HALF_T].rearrange("p b n -> p (b n)")

        def turned_ps(t):
            return sums(t).rearrange("p (k t) -> p k t", t=P)

        block = ctx.enter_context(nc.Block())

        @block.sync
        def _(sp):
            def load(step, k, s):
                sp.wait_ge(lo_ready, 2 * step + 1)
                sp.dma_start(w_raw[:, s], w[ds(k, 1)].rearrange("a p n -> (a p) n")).then_inc(w_in[s], 16)

            load(0, 0, 0)
            load(1, 1, 1)
            for k in range(2, 6):
                load(k, k, k % 2)
                for t in (2 * k - 4, 2 * k - 3):
                    sp.dma_start(y[:, t], resid[t * P:(t + 1) * P, :]).then_inc(resid_in, 16)
            sp.dma_start(gain_b[:], gain.broadcast_to([P, D])).then_inc(affine_in, 16)
            sp.dma_start(bias_b[:], bias.broadcast_to([P, D])).then_inc(affine_in, 16)
            for hf in range(2):
                with sp.Fori(3 - 3 * hf, KP) as i:
                    for s in range(2):
                        load(hf * k_tiles + 2 * i + s, 2 * i + s, s)
            for t in range(TT):
                sp.wait_ge(finished, t + 1)
                sp.dma_start(out[t * P:(t + 1) * P, :], y[:, t]).then_inc(stored, 16)
            sp.wait_ge(stored, 16 * TT)

        @block.scalar
        def _(act):
            for hf in range(2):
                with act.Fori(0, KP) as i:
                    for s in range(2):
                        step = hf * k_tiles + 2 * i + s
                        act.wait_ge(w_in[s], 16 * (hf * KP + i) + 16)
                        act.wait_ge(step_done, step + 1)
                        act.copy(w_hi[:, s], w_raw[:, s]).then_inc(hi_ready, 1)
                        act.copy(a_hi[:, s], a[:, ds(2 * i + s, 1), hf * HALF:(hf + 1) * HALF]
                                 .rearrange("p a t -> p (a t)")).then_inc(hi_ready, 1)
            if hi is not None:
                for t in range(TT):
                    act.wait_ge(turned, t + 1)
                    act.copy(hi[:, :, t * P:(t + 1) * P], turned_ps(t)).then_inc(hi_copied, 1)

        @block.tensor
        def _(pe):
            pe.sem_inc(step_done, 2)

            def products(step, s, hf, first, last):
                pe.wait_ge(lo_ready, 2 * step + 6)
                for t in range(HALF_T):
                    if first and hf == 1:
                        pe.wait_ge(summed, t + 1)
                    tok = slice(t * P, (t + 1) * P)
                    for aa, ww in ((a_hi, w_hi), (a_hi, w_lo), (a_lo, w_hi)):
                        for n in range(2):
                            mm = pe.matmul(acc[:, t, n], aa[:, s, tok], ww[:, s, n * NB:(n + 1) * NB],
                                           start=(first and aa is a_hi and ww is w_hi),
                                           stop=(last and aa is a_lo))
                mm.then_inc(step_done, 1)

            for hf in range(2):
                base = hf * k_tiles
                products(base, 0, hf, True, False)
                products(base + 1, 1, hf, False, False)
                with pe.Fori(1, KP - 1) as i:
                    for s in range(2):
                        products(base + 2 * i + s, s, hf, False, False)
                products(base + k_tiles - 2, 0, hf, False, False)
                products(base + k_tiles - 1, 1, hf, False, True)
            if hi is not None:
                for t in range(TT):
                    pe.wait_ge(finished, t + 1)
                    if t < HALF_T:
                        pe.wait_ge(summed, HALF_T + t + 1)
                    else:
                        pe.wait_ge(lo_copied, t - HALF_T + 1)
                    for k in range(KD):
                        mm = pe.transpose(turned_ps(t)[:, k], y[:, t, k * P:(k + 1) * P], ident[:])
                    mm.then_inc(turned, 1)

        @block.vector
        def _(dve):
            dve.sem_inc(lo_ready, 4)
            dve.memset(power[:], -0.5).then_inc(power_set, 1)

            def split_lo(hf, k, s):
                step = hf * k_tiles + k
                dve.wait_ge(hi_ready, 2 * step + 1)
                dve.tensor_tensor(w_lo[:, s], w_raw[:, s], f32(w_hi[:, s]), ALU.subtract).then_inc(lo_ready, 1)
                dve.wait_ge(hi_ready, 2 * step + 2)
                dve.tensor_tensor(a_lo[:, s], a[:, ds(k, 1), hf * HALF:(hf + 1) * HALF].rearrange("p a t -> p (a t)"),
                                  f32(a_hi[:, s]), ALU.subtract).then_inc(lo_ready, 1)

            def add_resid(t):
                dve.scalar_tensor_tensor(out=y[:, t], in0=y[:, t], scalar=DN_ALPHA, in1=sums(t),
                                         op0=ALU.mult, op1=ALU.add).then_inc(summed, 1)

            def tile_moments(t):
                dve.wait_ge(summed, t + 1)
                for b in range(2):
                    dve.bn_stats(stats[:, t, b], y[:, t, b * NB:(b + 1) * NB]).then_inc(stats_done, 1)
                dve.wait_ge(stats_done, 2 * t + 2)
                dve.bn_aggr(mean_var[:, t], stats[:, t].rearrange("p b c -> p (b c)")).then_inc(moments, 1)

            def centre(t):
                dve.wait_ge(moments, t + 1)
                dve.scalar_tensor_tensor(out=y[:, t], in0=y[:, t], scalar=mean_var[:, t, 0:1], in1=gain_b[:],
                                         op0=ALU.subtract, op1=ALU.mult).then_inc(centred, 1)

            def finish(t):
                dve.wait_ge(centred, t + 1)
                dve.wait_ge(rstd_ready, 2 * t + 2)
                dve.scalar_tensor_tensor(out=y[:, t], in0=y[:, t], scalar=rstd[:, t], in1=bias_b[:],
                                         op0=ALU.mult, op1=ALU.add).then_inc(finished, 1)

            def turned_lo(t):
                if hi is not None:
                    tok = slice(t * P, (t + 1) * P)
                    dve.wait_ge(hi_copied, t + 1)
                    dve.tensor_tensor(lo[:, :, tok], turned_ps(t), f32(hi[:, :, tok]), ALU.subtract).then_inc(lo_copied, 1)

            with dve.Fori(0, KP) as i:
                for s in range(2):
                    split_lo(0, 2 * i + s, s)
            split_lo(1, 0, 0)
            dve.wait_ge(step_done, 2 + k_tiles)
            dve.wait_ge(resid_in, 16 * TT)
            dve.wait_ge(affine_in, 32)
            for t in range(HALF_T):
                add_resid(t)
            for k in range(1, PEELED):
                split_lo(1, k, k % 2)
                if k <= 2:
                    tile_moments(2 * k - 2)
                    tile_moments(2 * k - 1)
                elif k <= 2 + HALF_T:
                    centre(k - 3)
                    finish(k - 3)
            if KP > PEELED // 2:
                with dve.Fori(PEELED // 2, KP) as i:
                    for s in range(2):
                        split_lo(1, 2 * i + s, s)
            dve.wait_ge(step_done, 2 + 2 * k_tiles)
            add_resid(HALF_T)
            for t in range(HALF_T, TT):
                if t + 1 < TT:
                    add_resid(t + 1)
                tile_moments(t)
            for t in range(HALF_T, TT):
                centre(t)
                turned_lo(t - HALF_T)
                finish(t)
            for t in range(HALF_T, TT):
                turned_lo(t)

        @block.gpsimd
        def _(pool):
            pool.wait_ge(power_set, 1)
            for t in range(TT):
                pool.wait_ge(moments, t + 1)
                pool.tensor_scalar(rstd[:, t], mean_var[:, t, 1:2], EPS, None, ALU.add).then_inc(rstd_ready, 1)
                pool.wait_ge(rstd_ready, 2 * t + 1)
                pool.tensor_tensor(rstd[:, t], rstd[:, t], power[:], ALU.pow).then_inc(rstd_ready, 1)


ROT_A = RET_DK // 2
ROT_B = ROPE_DIMS // 2
ROT = ROT_A + ROT_B
TWO_PI_1 = 6.28125
TWO_PI_2 = float(np.array([np.float32(2 * np.pi - 6.28125)]).view(np.int32).__and__(-4096).view(np.float32)[0])
TWO_PI_3 = float(2 * np.pi - TWO_PI_1 - TWO_PI_2)
ROUND = 1.5 * 2.0 ** 23


def inverse_frequencies():
    def steps(theta, n_rot):
        half = np.arange(n_rot // 2, dtype=np.float32)
        return np.power(np.float32(theta), -half * np.float32(2) / np.float32(n_rot))

    return np.concatenate([steps(10000.0, RET_DK), steps(500000.0, ROPE_DIMS)])[None]


def rotary_tables(nc, positions, inv_freq, cos, sin):
    with ExitStack() as ctx:
        sc = Scope(nc, ctx, "rotary")
        pos_i = sc.sbuf("pos_i", [P, TT], I32)
        pos = sc.sbuf("pos", [P, TT])
        inv = sc.sbuf("inv", [P, ROT])
        ang = sc.sbuf("ang", [P, TT, ROT])
        turns = sc.sbuf("turns", [P, TT, ROT])
        loaded = sc.sem("loaded")
        step = sc.sem("step")
        reduced = sc.sem("reduced")
        tables_done = sc.sem("tables_done")
        block = ctx.enter_context(nc.Block())

        @block.sync
        def _(sp):
            sp.dma_start(pos_i[:], positions).then_inc(loaded, 16)
            sp.dma_start(inv[:], inv_freq.broadcast_to([P, ROT])).then_inc(loaded, 16)

        @block.vector
        def _(dve):
            count = [0]

            def then_wait(op):
                count[0] += 1
                op.then_inc(step, 1)
                dve.wait_ge(step, count[0])

            dve.wait_ge(loaded, 32)
            then_wait(dve.tensor_copy(pos[:], pos_i[:]))
            then_wait(dve.tensor_tensor(ang[:], pos[:].unsqueeze(2).broadcast_to([P, TT, ROT]),
                                        inv[:].unsqueeze(1).broadcast_to([P, TT, ROT]), ALU.mult))
            for table, quarter in ((sin, 0.0), (cos, 0.25)):
                then_wait(dve.tensor_scalar(turns[:], ang[:], 1.0 / (2 * np.pi), quarter, ALU.mult, ALU.add))
                then_wait(dve.tensor_scalar(turns[:], turns[:], ROUND, None, ALU.add))
                then_wait(dve.tensor_scalar(turns[:], turns[:], -ROUND, None, ALU.add))
                then_wait(dve.scalar_tensor_tensor(out=table[:], in0=turns[:], scalar=-TWO_PI_1, in1=ang[:],
                                                   op0=ALU.mult, op1=ALU.add))
                then_wait(dve.scalar_tensor_tensor(out=table[:], in0=turns[:], scalar=-TWO_PI_2, in1=table[:],
                                                   op0=ALU.mult, op1=ALU.add))
                then_wait(dve.scalar_tensor_tensor(out=table[:], in0=turns[:], scalar=-TWO_PI_3, in1=table[:],
                                                   op0=ALU.mult, op1=ALU.add))
                then_wait(dve.tensor_scalar(table[:], table[:], quarter * 2 * np.pi, None, ALU.add))
                then_wait(dve.tensor_scalar(turns[:], table[:], 1.0 / (2 * np.pi), ROUND, ALU.mult, ALU.add))
                then_wait(dve.tensor_scalar(turns[:], turns[:], -ROUND, None, ALU.add))
                then_wait(dve.scalar_tensor_tensor(out=table[:], in0=turns[:], scalar=-2 * np.pi, in1=table[:],
                                                   op0=ALU.mult, op1=ALU.add))
                then_wait(dve.tensor_scalar(table[:], table[:], 3.1415925, None, ALU.min))
                dve.tensor_scalar(table[:], table[:], -3.1415925, None, ALU.max).then_inc(reduced, 1)

        @block.scalar
        def _(act):
            for n, table in enumerate((sin, cos)):
                act.wait_ge(reduced, n + 1)
                act.activation(table[:], table[:], ACT.Sin).then_inc(tables_done, 1)


def retention_constants():
    h = np.arange(RET_HEADS, dtype=np.float64)
    lg = np.log1p(-(2.0 ** (-5.0 - h)))
    idx = np.arange(P, dtype=np.float64)
    rel = idx[None, :] - idx[:, None]
    scale = RET_DK ** -0.5
    mask = np.where(rel[:, None, :] >= 0, np.exp(np.maximum(rel, 0)[:, None, :] * lg[None, :, None]), 0.0) * scale
    xi = np.exp((idx[:, None] + 1) * lg[None, :])
    zeta = np.exp((P - 1 - idx[:, None]) * lg[None, :]) * scale
    return mask.astype(np.float32), np.concatenate([xi, zeta], 1).astype(np.float32), [float(x) for x in np.exp(P * lg)]


def by_chunks(eng, body):
    body(0, 0, False, True, True)
    body(1, 1, True, True, True)
    with eng.Fori(1, TT // 2 - 1) as i:
        for s in range(2):
            body(2 * i + s, s, True, True, True)
    body(TT - 2, 0, True, True, False)
    body(TT - 1, 1, True, False, False)


def retention(nc, hp, mask_dram, factor_dram, chunk_decay, ident, cos, sin, a):
    H, W = RET_HEADS, RET_HEADS * RET_DK
    V0, G0, B0 = 2 * W, 2 * W + H * RET_DV, RET_IN
    NBH = 2 * DIL_HEADS
    with ExitStack() as ctx:
        sc = Scope(nc, ctx, "ret")
        qk = sc.sbuf("qk", [P, 2, 2 * W])
        small = sc.sbuf("small", [P, 2, NBH * DIL_HD])
        vg = sc.sbuf("vg", [P, 2, 2 * H * RET_DV])
        rot = sc.sbuf("rot", [P, 2, 2 * H, RET_DK])
        scaled = sc.sbuf("scaled", [P, 2 * H, RET_DK])
        prod = sc.sbuf("prod", [P, 4, 2 * H, ROT_A])
        prod_b = sc.sbuf("prod_b", [P, 4, NBH, ROT_B])
        feat = sc.sbuf("feat", [P, 3 * H, P])
        scores = sc.sbuf("scores", [P, H, P])
        state = sc.sbuf("state", [P, 2, H, RET_DV])
        gate = sc.sbuf("gate", [P, 2, H, RET_DV])
        y = sc.sbuf("y", [P, H, RET_DV])
        squares = sc.sbuf("squares", [P, H, RET_DV])
        sumsq = sc.sbuf("sumsq", [P, 2, H])
        rstd = sc.sbuf("rstd", [P, 2, H])
        power = sc.sbuf("power", [P, H])
        eps = sc.sbuf("eps", [P, H])
        mask = sc.sbuf("mask", [P, H, P])
        factor = sc.sbuf("factor", [P, 2 * H])
        bank = sc.psum("bank", [P, 8, NB])
        t_ps = bank[:, 0:3].rearrange("p b n -> p (b n)").rearrange("p (h t) -> p h t", t=P)
        s_ps = bank[:, 3].rearrange("p (h t) -> p h t", t=P)
        o_ps = bank[:, 4:6].rearrange("p b n -> p (b n)").rearrange("p (h e) -> p h e", e=RET_DV)
        kv_ps = bank[:, 6:8].rearrange("p b n -> p (b n)").rearrange("p (h e) -> p h e", e=RET_DV)
        consts_in = sc.sem("consts_in")
        power_set = sc.sem("power_set")
        qk_in = [sc.sem(f"qk_in{s}") for s in range(2)]
        vg_in = [sc.sem(f"vg_in{s}") for s in range(2)]
        qk_stored = [sc.sem(f"qk_stored{s}") for s in range(2)]
        cos_done = sc.sem("cos_done")
        sin_done = sc.sem("sin_done")
        rot_done = sc.sem("rot_done")
        scaled_done = sc.sem("scaled_done")
        slot_seen = sc.sem("slot_seen")
        qk_prod = sc.sem("qk_prod")
        qk_rot = sc.sem("qk_rot")
        turned = sc.sem("turned")
        feat_ready = sc.sem("feat_ready")
        scores_done = sc.sem("scores_done")
        masked = sc.sem("masked")
        kv_done = sc.sem("kv_done")
        state_ready = sc.sem("state_ready")
        o_done = sc.sem("o_done")
        squared = sc.sem("squared")
        gate_ready = sc.sem("gate_ready")
        rstd_step = sc.sem("rstd_step")
        y_done = sc.sem("y_done")
        y_turned = sc.sem("y_turned")
        y_copied = sc.sem("y_copied")
        block = ctx.enter_context(nc.Block())

        @block.sync
        def _(sp):
            sp.dma_start(mask[:], mask_dram).then_inc(consts_in, 16)
            sp.dma_start(factor[:], factor_dram).then_inc(consts_in, 16)

            def load_qk(n, s):
                sp.dma_start(qk[:, s], hp[ds(n * P, P), 0:2 * W]).then_inc(qk_in[s], 16)
                sp.dma_start(small[:, s], hp[ds(n * P, P), B0:B0 + NBH * DIL_HD]).then_inc(qk_in[s], 16)

            def load_vg(n, s):
                sp.dma_start(vg[:, s], hp[ds(n * P, P), V0:V0 + 2 * H * RET_DV]).then_inc(vg_in[s], 16)

            def store_small(n, s, two):
                sp.wait_ge(qk_rot, 2 + 2 * n + 2)
                sp.dma_start(hp[ds(n * P, P), B0:B0 + NBH * DIL_HD], small[:, s]).then_inc(qk_stored[s], 16)
                if two:
                    sp.wait_ge(cos_done, 2 * n + 2)
                    sp.sem_inc(slot_seen, 1)
                    sp.wait_ge(sin_done, 2 * n + 2)
                    sp.wait_ge(qk_stored[s], 8 * (n - s) + 16)
                    load_qk(n + 2, s)

            def body(n, s):
                if n + 1 < TT if isinstance(n, int) else True:
                    sp.wait_ge(o_done, n + 1)
                    sp.wait_ge(gate_ready, n + 1)
                    load_vg(n + 1, 1 - s)
                    store_small(n + 1, 1 - s, n + 3 < TT if isinstance(n, int) else True)

            load_qk(0, 0)
            load_qk(1, 1)
            load_vg(0, 0)
            store_small(0, 0, True)
            with sp.Fori(0, TT // 2 - 2) as i:
                for s in range(2):
                    body(2 * i + s, s)
            for n in range(TT - 4, TT):
                body(n, n % 2)
            for s in range(2):
                sp.wait_ge(qk_stored[s], 16 * (TT // 2))

        @block.vector
        def _(dve):
            dve.sem_inc(rot_done, 2)
            dve.sem_inc(masked, 1)
            dve.sem_inc(y_done, 8)
            dve.memset(state[:, 0].rearrange("p h e -> p (h e)"), 0.0).then_inc(state_ready, 4)
            dve.memset(power[:], -0.5).then_inc(power_set, 1)
            dve.memset(eps[:], EPS).then_inc(power_set, 1)
            dve.wait_ge(consts_in, 32)

            def rotate(n, s):
                heads = qk[:, s].rearrange("p (h d) -> p h d", d=RET_DK)
                c = cos[:, ds(n, 1), 0:ROT_A].broadcast_to([P, 2 * H, ROT_A])
                dve.wait_ge(qk_in[s], 16 * (n - s) + 32)
                dve.wait_ge(rot_done, 2 + 2 * n)
                dve.tensor_tensor(prod[:, 0], heads[:, :, 0:ROT_A], c, ALU.mult).then_inc(cos_done, 1)
                dve.tensor_tensor(prod[:, 1], heads[:, :, ROT_A:RET_DK], c, ALU.mult).then_inc(cos_done, 1)
                dve.wait_ge(cos_done, 2 * n + 2)
                dve.wait_ge(sin_done, 2 * n + 2)
                dve.wait_ge(scaled_done, 2 + n - 1)
                dve.wait_ge(turned, 2 + n - 1)
                dve.tensor_tensor(rot[:, s, :, 0:ROT_A], prod[:, 0], prod[:, 2], ALU.subtract).then_inc(rot_done, 1)
                dve.tensor_tensor(rot[:, s, :, ROT_A:RET_DK], prod[:, 1], prod[:, 3], ALU.add).then_inc(rot_done, 1)

            def output(n, s):
                dve.wait_ge(rstd_step, 2 * n + 2)
                dve.wait_ge(gate_ready, 1 + n + 1)
                dve.wait_ge(y_turned, 1 + n)
                for h in range(H):
                    dve.scalar_tensor_tensor(out=y[:, h], in0=o_ps[:, h], scalar=rstd[:, s, h:h + 1],
                                             in1=gate[:, s, h], op0=ALU.mult, op1=ALU.mult).then_inc(y_done, 1)

            def body(n, s, prev, one, two):
                if prev:
                    output(n - 1, 1 - s)
                dve.wait_ge(scores_done, n + 1)
                dve.tensor_tensor(scores[:], s_ps, mask[:], ALU.mult).then_inc(masked, 1)
                dve.wait_ge(kv_done, 1 + n + 1)
                dve.wait_ge(state_ready, 4 + 4 * n)
                for h in range(H):
                    dve.scalar_tensor_tensor(out=state[:, 1 - s, h], in0=state[:, s, h], scalar=chunk_decay[h],
                                             in1=kv_ps[:, h], op0=ALU.mult, op1=ALU.add).then_inc(state_ready, 1)
                if one:
                    rotate(n + 1, 1 - s)

            rotate(0, 0)
            by_chunks(dve, body)
            output(TT - 1, 1)

        @block.gpsimd
        def _(pool):
            pool.sem_inc(scaled_done, 2)
            pool.sem_inc(qk_rot, 2)
            pool.wait_ge(consts_in, 32)
            pool.wait_ge(power_set, 2)

            def rotate(n, s):
                heads = qk[:, s].rearrange("p (h d) -> p h d", d=RET_DK)
                sn = sin[:, ds(n, 1), 0:ROT_A].broadcast_to([P, 2 * H, ROT_A])
                pool.wait_ge(qk_in[s], 16 * (n - s) + 32)
                pool.wait_ge(rot_done, 2 + 2 * n)
                pool.tensor_tensor(prod[:, 2], heads[:, :, ROT_A:RET_DK], sn, ALU.mult).then_inc(sin_done, 1)
                pool.tensor_tensor(prod[:, 3], heads[:, :, 0:ROT_A], sn, ALU.mult).then_inc(sin_done, 1)
                pairs = small[:, s].rearrange("p (h d) -> p h d", d=DIL_HD)
                d1, d2 = pairs[:, :, 0:ROT_B], pairs[:, :, ROT_B:ROPE_DIMS]
                cb = cos[:, ds(n, 1), ROT_A:ROT].broadcast_to([P, NBH, ROT_B])
                sb = sin[:, ds(n, 1), ROT_A:ROT].broadcast_to([P, NBH, ROT_B])
                pool.wait_ge(qk_rot, 2 + 2 * n)
                for m, (xx, tt) in enumerate(((d1, cb), (d2, cb), (d2, sb), (d1, sb))):
                    pool.tensor_tensor(prod_b[:, m], xx, tt, ALU.mult).then_inc(qk_prod, 1)
                pool.wait_ge(qk_prod, 4 * n + 4)
                pool.tensor_tensor(d1, prod_b[:, 0], prod_b[:, 2], ALU.subtract).then_inc(qk_rot, 1)
                pool.tensor_tensor(d2, prod_b[:, 1], prod_b[:, 3], ALU.add).then_inc(qk_rot, 1)
                pool.wait_ge(rot_done, 2 + 2 * n + 2)
                pool.wait_ge(kv_done, 1 + n)
                pool.tensor_tensor(scaled[:], rot[:, s], factor[:].unsqueeze(2).broadcast_to([P, 2 * H, RET_DK]),
                                   ALU.mult).then_inc(scaled_done, 1)

            def output_norm(n, s):
                pool.wait_ge(squared, 4 + 4 * n + 4)
                pool.tensor_tensor(rstd[:, s], sumsq[:, s], eps[:], ALU.add).then_inc(rstd_step, 1)
                pool.wait_ge(rstd_step, 2 * n + 1)
                pool.tensor_tensor(rstd[:, s], rstd[:, s], power[:], ALU.pow).then_inc(rstd_step, 1)

            def body(n, s, prev, one, two):
                if prev:
                    output_norm(n - 1, 1 - s)
                if one:
                    rotate(n + 1, 1 - s)

            rotate(0, 0)
            by_chunks(pool, body)
            output_norm(TT - 1, 1)

        @block.tensor
        def _(pe):
            pe.sem_inc(turned, 2)
            pe.sem_inc(kv_done, 1)
            pe.sem_inc(y_turned, 1)
            pe.sem_inc(o_done, 1)

            def output(n):
                pe.wait_ge(y_done, 8 + 4 * n + 4)
                for c in range(2 * H):
                    mm = pe.transpose(t_ps[:, c], y[:, c // 2, (c % 2) * P:(c % 2 + 1) * P], ident[:])
                mm.then_inc(y_turned, 1)

            def body(n, s, prev, one, two):
                pe.wait_ge(rot_done, 2 + 2 * n + 2)
                pe.wait_ge(y_copied, n + 1)
                for h in range(2 * H):
                    pe.transpose(t_ps[:, h], rot[:, s, h], ident[:])
                pe.wait_ge(scaled_done, 2 + n + 1)
                for h in range(H):
                    mm = pe.transpose(t_ps[:, 2 * H + h], scaled[:, h], ident[:])
                mm.then_inc(turned, 1)
                pe.wait_ge(state_ready, 4 + 4 * n)
                pe.wait_ge(vg_in[s], 8 * (n - s) + 16)
                for h in range(H):
                    v = vg[:, s, h * RET_DV:(h + 1) * RET_DV]
                    mm = pe.matmul(kv_ps[:, h], scaled[:, H + h], v, start=True, stop=True)
                mm.then_inc(kv_done, 1)
                pe.wait_ge(feat_ready, n + 1)
                pe.wait_ge(masked, 1 + n)
                for h in range(H):
                    mm = pe.matmul(s_ps[:, h], feat[:, H + h], feat[:, h], start=True, stop=True)
                mm.then_inc(scores_done, 1)
                if prev:
                    output(n - 1)
                pe.wait_ge(masked, 1 + n + 1)
                pe.wait_ge(y_done, 8 + 4 * n)
                for h in range(H):
                    v = vg[:, s, h * RET_DV:(h + 1) * RET_DV]
                    pe.matmul(o_ps[:, h], feat[:, 2 * H + h], state[:, s, h], start=True, stop=False)
                    mm = pe.matmul(o_ps[:, h], scores[:, h], v, start=False, stop=True)
                mm.then_inc(o_done, 1)

            by_chunks(pe, body)
            output(TT - 1)

        @block.scalar
        def _(act):
            act.sem_inc(squared, 4)
            act.sem_inc(y_copied, 2)
            act.sem_inc(gate_ready, 1)

            def output(n):
                act.wait_ge(y_turned, 1 + n + 1)
                act.copy(a[:, 0:2 * H, ds(n * P, P)], t_ps[:, 0:2 * H]).then_inc(y_copied, 1)

            def body(n, s, prev, one, two):
                act.wait_ge(vg_in[s], 8 * (n - s) + 16)
                act.wait_ge(y_done, 4 * n + 4)
                act.activation(gate[:, s].rearrange("p h e -> p (h e)"), vg[:, s, H * RET_DV:2 * H * RET_DV],
                               ACT.Silu).then_inc(gate_ready, 1)
                act.wait_ge(turned, 2 + n + 1)
                act.copy(feat[:], t_ps).then_inc(feat_ready, 1)
                if prev:
                    output(n - 1)
                act.wait_ge(o_done, 1 + n + 1)
                act.wait_ge(squared, 4 + 4 * n)
                for h in range(H):
                    act.activation(squares[:, h], o_ps[:, h], ACT.Square, scale=RET_DV ** -0.5,
                                   accum_out=sumsq[:, s, h:h + 1]).then_inc(squared, 1)

            by_chunks(act, body)
            output(TT - 1)


UNITS = 3 * TT
DIL_W = DIL_HEADS * DIL_HD
DIL_OUT = DIL_HD + 2
MASKED = -1e30


def dilated_masks():
    i, j = np.arange(P)[:, None], np.arange(P)[None, :]
    causal = j <= i
    none = np.zeros((P, P), bool)
    pair = causal & (i // (P // 2) == j // (P // 2))
    kinds = [np.concatenate([none, causal], 1), np.concatenate([j >= i, causal], 1), np.concatenate([none, pair], 1)]
    return np.where(np.stack(kinds), 0.0, MASKED).astype(np.float32)


def branch_rows(dram, branch, i, s):
    if branch == 0:
        return [(0, dram[ds((2 * i + s) * P, P), :])]
    if branch == 1:
        rows = dram.rearrange("(b p r) n -> r b p n", b=2, p=P, r=4)[ds(i, 1), s]
        return [(0, rows.rearrange("a p n -> (a p) n"))]
    rows = dram.rearrange("(l r) n -> r l n", r=16)
    return [(h * 64, rows[ds(4 * i + 2 * s + h, 1)].rearrange("a l n -> (a l) n")) for h in range(2)]


def dilated(nc, hp, masks, ident, parts):
    Q0 = RET_IN
    H = DIL_HEADS
    with ExitStack() as ctx:
        sc = Scope(nc, ctx, "dil")
        qk = sc.sbuf("qk", [P, 2, 2 * DIL_W])
        v = sc.sbuf("v", [P, 2, DIL_W])
        mask = sc.sbuf("mask", [P, 3, 2 * P])
        q_t = sc.sbuf("q_t", [P, 2, H // 2, P])
        k_t = sc.sbuf("k_t", [P, 2, H // 2, P])
        probs = sc.sbuf("probs", [P, 2, H, 2 * P])
        probs_t = sc.sbuf("probs_t", [P, 2 * H, P])
        neg_max = sc.sbuf("neg_max", [P, 2, H, 1])
        part = sc.sbuf("part", [P, 2, H, DIL_OUT])
        bank = sc.psum("bank", [P, 8, NB])
        turn_ps = bank[:, 0:2].rearrange("p b (h t) -> p b h t", t=P)
        o_ps = bank[:, 0:2].rearrange("p b (h e) -> p (b h) e", e=2 * DIL_HD)
        s_ps = [bank[:, 2 + h // 2, h % 2 * 2 * P:(h % 2 + 1) * 2 * P] for h in range(H)]
        pt_ps = bank[:, 6:8].rearrange("p b (h t) -> p (b h) t", t=P)
        qk_in = [sc.sem(f"qk_in{s}") for s in range(2)]
        v_in = [sc.sem(f"v_in{s}") for s in range(2)]
        stored = [sc.sem(f"stored{s}") for s in range(2)]
        mask_in = sc.sem("mask_in")
        cleared = sc.sem("cleared")
        turned = sc.sem("turned")
        feat_ready = sc.sem("feat_ready")
        scores_done = sc.sem("scores_done")
        scores_seen = sc.sem("scores_seen")
        maxed = sc.sem("maxed")
        negated = sc.sem("negated")
        exp_done = sc.sem("exp_done")
        pt_low = sc.sem("pt_low")
        pt_high = sc.sem("pt_high")
        low_copied = sc.sem("low_copied")
        high_copied = sc.sem("high_copied")
        o_done = sc.sem("o_done")
        o_copied = sc.sem("o_copied")
        block = ctx.enter_context(nc.Block())

        def has_before(branch, s):
            return (True, s == 1, False)[branch]

        def kind(branch, s):
            return (1, s, 2)[branch]

        def by_units(eng, body):
            for branch in range(3):
                last = branch == 2
                with eng.Fori(TT // 2 * branch, TT // 2 * branch + TT // 2 - 1) as i:
                    for s in range(2):
                        body(2 * i + s, s, has_before(branch, s), has_before(branch, 1 - s), kind(branch, 1 - s),
                             True, True)
                u = TT * branch + TT - 2
                after = min(branch + 1, 2)
                body(u, 0, has_before(branch, 0), has_before(branch, 1), kind(branch, 1), True, not last)
                body(u + 1, 1, has_before(branch, 1), has_before(after, 0), kind(after, 0), not last, not last)

        def own(tiles, before):
            return tiles if before else tiles.rearrange("p (h b) t -> p h b t", b=2)[:, :, 1]

        def keys(before):
            return slice(0 if before else P, 2 * P)

        @block.sync
        def _(sp):
            sp.sem_inc(stored[0], 32)
            sp.sem_inc(stored[1], 32)
            def pieces(dst, dram, cols, branch, i, s, sem, store=False):
                rows = branch_rows(dram, branch, i, s)
                for at, r in rows:
                    a, b = dst[at:at + P // len(rows)], r[:, cols]
                    sp.dma_start(*((b, a) if store else (a, b))).then_inc(sem, 32 // len(rows))

            def load_qk(branch, i, s):
                pieces(qk[:, s], hp, slice(Q0, Q0 + 2 * DIL_W), branch, i, s, qk_in[s])

            def load_v(branch, i, s):
                pieces(v[:, s], hp, slice(Q0 + 2 * DIL_W, Q0 + 3 * DIL_W), branch, i, s, v_in[s])

            def later(branch, i, s, by):
                i, s = i + (s + by) // 2, (s + by) % 2
                if isinstance(i, int) and i >= TT // 2:
                    branch, i = branch + 1, i - TT // 2
                return (branch, i, s) if branch < 3 else None

            def unit(branch, i, s, u):
                if later(branch, i, s, 3):
                    sp.wait_ge(maxed, 8 + 8 * u + 16)
                    load_qk(*later(branch, i, s, 3))
                sp.wait_ge(o_copied, 6 + 2 * u + 2)
                pieces(part[:, s].rearrange("p h e -> p (h e)"), parts[branch], slice(0, H * DIL_OUT), branch, i, s,
                       stored[s], store=True)
                if later(branch, i, s, 1):
                    load_v(*later(branch, i, s, 1))

            sp.dma_start(mask[:], masks.rearrange("m p k -> p m k")).then_inc(mask_in, 16)
            load_qk(0, 0, 0)
            load_qk(0, 0, 1)
            load_v(0, 0, 0)
            sp.wait_ge(cleared, 4)
            sp.wait_ge(maxed, 8 + 8)
            load_qk(0, 1, 0)
            for branch in range(3):
                with sp.Fori(0, TT // 2 - 2) as i:
                    for s in range(2):
                        unit(branch, i, s, TT * branch + 2 * i + s)
                for i in range(TT // 2 - 2, TT // 2):
                    for s in range(2):
                        unit(branch, i, s, TT * branch + 2 * i + s)
            for s in range(2):
                sp.wait_ge(stored[s], 32 + 32 * (UNITS // 2))

        @block.tensor
        def _(pe):
            pe.wait_ge(cleared, 4)

            def turn(u, s):
                pe.wait_ge(qk_in[s], 16 * (u - s) + 32)
                pe.wait_ge(o_copied, 2 * u + 2)
                pe.wait_ge(feat_ready, 3 * u + 3)
                for b in range(2):
                    for c in range(H // 2):
                        col = b * DIL_W + c * P
                        mm = pe.transpose(turn_ps[:, b, c], qk[:, s, col:col + P], ident[:])
                mm.then_inc(turned, 1)

            def score(u, s, before):
                pe.wait_ge(feat_ready, 3 + 3 * u + 3)
                pe.wait_ge(maxed, 8 + 8 * u)
                for h in range(H):
                    q = q_t[:, h % 2, h // 2]
                    if before:
                        pe.matmul(s_ps[h][:, 0:P], q, k_t[:, 1 - s, h // 2], start=True, stop=True)
                    mm = pe.matmul(s_ps[h][:, P:2 * P], q, k_t[:, s, h // 2], start=True, stop=True)
                    if h % 4 == 3:
                        mm.then_inc(scores_done, 1)

            def turn_probs(u, s, high, before):
                for h in range(H // 2):
                    for b in range(0 if before else 1, 2):
                        mm = pe.transpose(pt_ps[:, 2 * h + b], probs[:, s, high * (H // 2) + h, b * P:(b + 1) * P],
                                          ident[:])
                mm.then_inc(pt_high if high else pt_low, 1)

            def body(u, s, before, next_before, next_mask, one, two):
                if one:
                    score(u + 1, 1 - s, next_before)
                pe.wait_ge(exp_done, 8 * u + 4)
                pe.wait_ge(high_copied, 1 + u)
                turn_probs(u, s, 0, before)
                if two:
                    turn(u + 2, s)
                pe.wait_ge(exp_done, 8 * u + 8)
                pe.wait_ge(low_copied, u + 1)
                turn_probs(u, s, 1, before)
                pe.wait_ge(high_copied, 1 + u + 1)
                pe.wait_ge(v_in[s], 16 * (u - s) + 32)
                if two:
                    pe.wait_ge(feat_ready, 3 + 3 * u + 9)
                for h in range(H):
                    e = slice(h // 2 * 2 * DIL_HD, (h // 2 + 1) * 2 * DIL_HD)
                    if before:
                        pe.matmul(o_ps[:, h], probs_t[:, 2 * h], v[:, 1 - s, e], start=True, stop=False)
                    mm = pe.matmul(o_ps[:, h], probs_t[:, 2 * h + 1], v[:, s, e], start=not before, stop=True)
                mm.then_inc(o_done, 1)

            turn(0, 0)
            score(0, 0, True)
            turn(1, 1)
            by_units(pe, body)

        @block.scalar
        def _(act):
            def feats(u, s):
                act.wait_ge(turned, u + 1)
                for parity in range(2):
                    d = slice(parity * DIL_HD, (parity + 1) * DIL_HD)
                    act.mul(q_t[d, parity], turn_ps[d, 0], DIL_HD ** -0.5).then_inc(feat_ready, 1)
                act.copy(k_t[:, s], turn_ps[:, 1]).then_inc(feat_ready, 1)

            def exps(u, s, before):
                act.wait_ge(negated, u + 1)
                for h in range(H):
                    p = probs[:, s, h, keys(before)]
                    act.activation(p, p, ACT.Exp, bias=neg_max[:, s, h],
                                   accum_out=part[:, s, h, DIL_HD + 1:DIL_HD + 2]).then_inc(exp_done, 1)

            def body(u, s, before, next_before, next_mask, one, two):
                act.wait_ge(pt_low, u + 1)
                act.copy(own(probs_t[:, 0:H], before), own(pt_ps, before)).then_inc(low_copied, 1)
                if two:
                    feats(u + 2, s)
                if one:
                    exps(u + 1, 1 - s, next_before)

            act.sem_inc(feat_ready, 3)
            act.wait_ge(cleared, 4)
            feats(0, 0)
            feats(1, 1)
            exps(0, 0, True)
            by_units(act, body)

        @block.vector
        def _(dve):
            dve.memset(k_t[:, 1], 0.0).then_inc(cleared, 1)
            dve.memset(v[:, 1], 0.0).then_inc(cleared, 1)
            for parity in range(2):
                d = slice((1 - parity) * DIL_HD, (2 - parity) * DIL_HD)
                dve.memset(q_t[d, parity], 0.0).then_inc(cleared, 1)
            dve.sem_inc(maxed, 8)
            dve.sem_inc(high_copied, 1)
            dve.sem_inc(o_copied, 6)

            def maxima(u, s, before, kind):
                dve.wait_ge(stored[s], 16 * (u - s) + 32)
                for h in range(H):
                    if h % 4 == 0:
                        dve.wait_ge(scores_done, 2 * u + h // 4 + 1)
                        dve.sem_inc(scores_seen, 1)
                    k = keys(before)
                    dve.tensor_tensor_reduce(probs[:, s, h, k], s_ps[h][:, k], mask[:, kind, k], 1.0, -3e38, ALU.add, ALU.max,
                                             part[:, s, h, DIL_HD:DIL_HD + 1]).then_inc(maxed, 1)
                dve.wait_ge(maxed, 8 + 8 * u + 8)
                dve.tensor_scalar(neg_max[:, s], part[:, s, :, DIL_HD:DIL_HD + 1], -1.0, None,
                                  ALU.mult).then_inc(negated, 1)

            def body(u, s, before, next_before, next_mask, one, two):
                if one:
                    maxima(u + 1, 1 - s, next_before, next_mask)
                dve.wait_ge(pt_high, u + 1)
                dve.tensor_copy(own(probs_t[:, H:2 * H], before), own(pt_ps, before)).then_inc(high_copied, 1)
                dve.wait_ge(o_done, u + 1)
                for parity in range(2):
                    heads = o_ps.rearrange("p (h two) e -> p two h e", two=2)[:, parity]
                    mine = part[:, s].rearrange("p (h two) e -> p two h e", two=2)[:, parity]
                    dve.tensor_copy(mine[:, :, 0:DIL_HD], heads[:, :, parity * DIL_HD:(parity + 1) * DIL_HD]
                                    ).then_inc(o_copied, 1)

            dve.wait_ge(mask_in, 16)
            maxima(0, 0, True, 0)
            by_units(dve, body)


def combine_dilated(nc, parts, ident, a):
    H, K0 = DIL_HEADS, RET_HEADS * RET_DV // P
    KC = DIL_W // P
    with ExitStack() as ctx:
        sc = Scope(nc, ctx, "comb")
        part = sc.sbuf("part", [P, 2, 3, H, DIL_OUT])
        top = sc.sbuf("top", [P, 2, H, 1])
        weight = sc.sbuf("weight", [P, 2, 3, H, 1])
        total = sc.sbuf("total", [P, 2, H, DIL_OUT])
        inverse = sc.sbuf("inverse", [P, 2, H, 1])
        y = sc.sbuf("y", [P, 2, H, DIL_HD])
        turn_ps = sc.psum("turn_ps", [P, 2, KC, P])
        part_in = [sc.sem(f"part_in{s}") for s in range(2)]
        step = sc.sem("step")
        diff = sc.sem("diff")
        weighed = sc.sem("weighed")
        y_done = sc.sem("y_done")
        turned = sc.sem("turned")
        copied = sc.sem("copied")
        block = ctx.enter_context(nc.Block())

        @block.sync
        def _(sp):
            with sp.Fori(0, TT // 2) as i:
                for s in range(2):
                    n = 2 * i + s
                    sp.wait_ge(y_done, n + 1)
                    for b in range(3):
                        sp.dma_start(part[:, s, b].rearrange("p h e -> p (h e)"),
                                     parts[b, ds(n * P, P), :]).then_inc(part_in[s], 16)

        @block.vector
        def _(dve):
            dve.sem_inc(y_done, 2)
            with dve.Fori(0, TT // 2) as i:
                for s in range(2):
                    n = 2 * i + s
                    peak = part[:, s, :, :, DIL_HD:DIL_HD + 1]
                    dve.wait_ge(part_in[s], 48 * i + 48)
                    dve.tensor_tensor(top[:, s], peak[:, 0], peak[:, 1], ALU.max).then_inc(step, 1)
                    dve.wait_ge(step, 11 * n + 1)
                    dve.tensor_tensor(top[:, s], top[:, s], peak[:, 2], ALU.max).then_inc(step, 1)
                    dve.wait_ge(step, 11 * n + 2)
                    for b in range(3):
                        dve.tensor_tensor(weight[:, s, b], peak[:, b], top[:, s], ALU.subtract).then_inc(diff, 1)
                    dve.wait_ge(weighed, n + 1)
                    for b in range(3):
                        dve.tensor_tensor(part[:, s, b], part[:, s, b],
                                          weight[:, s, b].broadcast_to([P, H, DIL_OUT]), ALU.mult).then_inc(step, 1)
                    dve.wait_ge(step, 11 * n + 5)
                    dve.tensor_tensor(total[:, s], part[:, s, 0], part[:, s, 1], ALU.add).then_inc(step, 1)
                    dve.wait_ge(step, 11 * n + 6)
                    dve.tensor_tensor(total[:, s], total[:, s], part[:, s, 2], ALU.add).then_inc(step, 1)
                    dve.wait_ge(step, 11 * n + 7)
                    dve.reciprocal(inverse[:, s], total[:, s, :, DIL_HD + 1:DIL_HD + 2]).then_inc(step, 4)
                    dve.wait_ge(step, 11 * n + 11)
                    dve.wait_ge(turned, n + 1)
                    dve.tensor_tensor(y[:, s], total[:, s, :, 0:DIL_HD],
                                      inverse[:, s].broadcast_to([P, H, DIL_HD]), ALU.mult).then_inc(y_done, 1)

        @block.scalar
        def _(act):
            act.sem_inc(copied, 2)
            with act.Fori(0, TT // 2) as i:
                for s in range(2):
                    n = 2 * i + s
                    act.wait_ge(diff, 3 * n + 3)
                    act.activation(weight[:, s].rearrange("p b h a -> p (b h a)"),
                                   weight[:, s].rearrange("p b h a -> p (b h a)"), ACT.Exp).then_inc(weighed, 1)
                    act.wait_ge(turned, 2 + n + 1)
                    act.copy(a[:, K0:K0 + KC, ds(n * P, P)], turn_ps[:, s]).then_inc(copied, 1)

        @block.tensor
        def _(pe):
            pe.sem_inc(turned, 2)
            with pe.Fori(0, TT // 2) as i:
                for s in range(2):
                    n = 2 * i + s
                    pe.wait_ge(y_done, 2 + n + 1)
                    pe.wait_ge(copied, n + 1)
                    flat = y[:, s].rearrange("p h e -> p (h e)")
                    for c in range(KC):
                        mm = pe.transpose(turn_ps[:, s, c], flat[:, c * P:(c + 1) * P], ident[:])
                    mm.then_inc(turned, 1)


def conv_tokens(nc, name, xhi, xlo, w, taps_dram, ident, n_tiles, out):
    with ExitStack() as ctx:
        sc = Scope(nc, ctx, name)
        w_raw = sc.sbuf("w_raw", [P, 2, KD, P])
        w_hi = sc.sbuf("w_hi", [P, 2, KD, P], F32R)
        w_lo = sc.sbuf("w_lo", [P, 2, KD, P], F32R)
        conv = sc.sbuf("conv", [P, 2, SEQ])
        rows = sc.sbuf("rows", [P, 2, TT, P])
        taps = sc.sbuf("taps", [P, n_tiles, GDN_CONV])
        acc = sc.psum("acc", [P, 2, SEQ])
        turn = sc.psum("turn", [P, 2, TT, P])
        taps_in = sc.sem("taps_in")
        w_in = [sc.sem(f"w_in{s}") for s in range(2)]
        hi_ready = sc.sem("hi_ready")
        lo_ready = sc.sem("lo_ready")
        prod_done = sc.sem("prod_done")
        tap_done = sc.sem("tap_done")
        tap_added = sc.sem("tap_added")
        acc_free = sc.sem("acc_free")
        silu_done = sc.sem("silu_done")
        turned = sc.sem("turned")
        copied = sc.sem("copied")
        stored = [sc.sem(f"stored{s}") for s in range(2)]
        block = ctx.enter_context(nc.Block())

        def tap(j, c):
            return taps[:, ds(j, 1), c:c + 1].rearrange("p a c -> p (a c)")

        def by_tile_pairs(eng, body):
            with eng.Fori(0, n_tiles // 2 - 1) as i:
                for s in range(2):
                    body(2 * i + s, s, True, True)
            body(n_tiles - 2, 0, True, False)
            body(n_tiles - 1, 1, False, False)

        @block.sync
        def _(sp):
            sp.dma_start(taps[:], taps_dram).then_inc(taps_in, 16)
            with sp.Fori(0, n_tiles // 2) as i:
                for s in range(2):
                    j = 2 * i + s
                    sp.wait_ge(lo_ready, j + 1)
                    sp.dma_start(w_raw[:, s], w[ds(j, 1)].rearrange("a p k n -> p (a k) n")).then_inc(w_in[s], 16)

        @block.tensor
        def _(pe):
            pe.sem_inc(prod_done, 2)
            pe.sem_inc(turned, 2)

            def products(j, s):
                pe.wait_ge(lo_ready, 2 + j + 1)
                pe.wait_ge(acc_free, j + 1)
                for k in range(KD):
                    for ww, xx in ((w_hi, xhi), (w_hi, xlo), (w_lo, xhi)):
                        for hf in range(2):
                            tok = slice(hf * HALF, (hf + 1) * HALF)
                            mm = pe.matmul(acc[:, s, tok], ww[:, s, k], xx[:, k, tok],
                                           start=(k == 0 and ww is w_hi and xx is xhi),
                                           stop=(k == KD - 1 and ww is w_lo))
                mm.then_inc(prod_done, 1)

            def body(j, s, one, two):
                if one:
                    products(j + 1, 1 - s)
                pe.wait_ge(silu_done, j + 1)
                pe.wait_ge(copied, j + 1)
                for t in range(TT):
                    mm = pe.transpose(turn[:, s, t], conv[:, s, t * P:(t + 1) * P], ident[:])
                mm.then_inc(turned, 1)

            products(0, 0)
            by_tile_pairs(pe, body)

        @block.scalar
        def _(act):
            act.sem_inc(copied, 2)
            act.sem_inc(stored[0], 16)
            act.sem_inc(stored[1], 16)

            def split_hi(j, s):
                act.wait_ge(w_in[s], 8 * (j - s) + 16)
                act.wait_ge(prod_done, j + 1)
                act.copy(w_hi[:, s], w_raw[:, s]).then_inc(hi_ready, 1)

            def last_tap(j, s):
                act.wait_ge(prod_done, 2 + j + 1)
                act.wait_ge(turned, j + 1)
                act.activation(conv[:, s], acc[:, s], ACT.Copy, scale=tap(j, GDN_CONV - 1)).then_inc(tap_done, 1)

            def finish(j, s):
                act.wait_ge(acc_free, 2 + j + 1)
                act.activation(conv[:, s], conv[:, s], ACT.Silu).then_inc(silu_done, 1)

            def copy_out(j, s):
                act.wait_ge(turned, 2 + j + 1)
                act.wait_ge(stored[s], 8 * (j - s) + 16)
                act.copy(rows[:, s], turn[:, s]).then_inc(copied, 1)
                act.wait_ge(copied, 2 + j + 1)
                act.dma_start(out[:, :, ds(j * P, P)].rearrange("t p n -> p t n"), rows[:, s]).then_inc(stored[s], 16)

            def body(j, s, one, two):
                last_tap(j, s)
                if two:
                    split_hi(j + 2, s)
                finish(j, s)
                copy_out(j, s)

            act.wait_ge(taps_in, 16)
            split_hi(0, 0)
            split_hi(1, 1)
            by_tile_pairs(act, body)
            for s in range(2):
                act.wait_ge(stored[s], 16 + 16 * (n_tiles // 2))

        @block.vector
        def _(dve):
            dve.sem_inc(lo_ready, 2)
            dve.sem_inc(acc_free, 2)

            def split_lo(j, s):
                dve.wait_ge(hi_ready, j + 1)
                dve.tensor_tensor(w_lo[:, s], w_raw[:, s], f32(w_hi[:, s]), ALU.subtract).then_inc(lo_ready, 1)

            def body(j, s, one, two):
                dve.wait_ge(tap_done, j + 1)
                for back in range(1, GDN_CONV):
                    if back > 1:
                        dve.wait_ge(tap_added, 2 * j + back - 1)
                    dve.scalar_tensor_tensor(out=conv[:, s, back:SEQ], in0=acc[:, s, 0:SEQ - back],
                                             scalar=tap(j, GDN_CONV - 1 - back), in1=conv[:, s, back:SEQ],
                                             op0=ALU.mult, op1=ALU.add
                                             ).then_inc(tap_added if back < GDN_CONV - 1 else acc_free, 1)
                if two:
                    split_lo(j + 2, s)

            dve.wait_ge(taps_in, 16)
            split_lo(0, 0)
            split_lo(1, 1)
            by_tile_pairs(dve, body)


def project_decay(nc, xhi, xlo, w_dram, a_log, dt_bias, upper, beta, gates):
    H = GDN_HEADS
    g, gc, exp_gc, exp_rest, exp_all = gates
    with ExitStack() as ctx:
        sc = Scope(nc, ctx, "decay")
        w_raw = sc.sbuf("w_raw", [P, KD, 2 * H])
        w_hi = sc.sbuf("w_hi", [P, KD, 2 * H], F32R)
        w_lo = sc.sbuf("w_lo", [P, KD, 2 * H], F32R)
        rate = sc.sbuf("rate", [P, H])
        dt = sc.sbuf("dt", [P, H])
        ones = sc.sbuf("ones", [P, P])
        t = [sc.sbuf(f"t{i}", [P, TT, H]) for i in range(8)]
        acc = sc.psum("acc", [P, TT, 2 * H])
        sums = sc.psum("sums", [P, TT, H])
        whole = sc.psum("whole", [P, TT, H])
        loaded = sc.sem("loaded")
        split = sc.sem("split")
        projected = sc.sem("projected")
        a_step = sc.sem("a_step")
        d_step = sc.sem("d_step")
        summed = sc.sem("summed")
        block = ctx.enter_context(nc.Block())

        @block.sync
        def _(sp):
            sp.dma_start(w_raw[:], w_dram).then_inc(loaded, 16)
            sp.dma_start(rate[:], a_log.broadcast_to([P, H])).then_inc(loaded, 16)
            sp.dma_start(dt[:], dt_bias.broadcast_to([P, H])).then_inc(loaded, 16)

        @block.tensor
        def _(pe):
            pe.wait_ge(split, 2)
            for tt in range(TT):
                tok = slice(tt * P, (tt + 1) * P)
                for k in range(KD):
                    for xx, ww in ((xhi, w_hi), (xhi, w_lo), (xlo, w_hi)):
                        mm = pe.matmul(acc[:, tt], xx[:, k, tok], ww[:, k],
                                       start=(k == 0 and xx is xhi and ww is w_hi), stop=(k == KD - 1 and xx is xlo))
            mm.then_inc(projected, 1)
            pe.wait_ge(d_step, 17)
            pe.matmul(sums[:].rearrange("p t h -> p (t h)"), upper[:], g[:].rearrange("p t h -> p (t h)"),
                      start=True, stop=True)
            pe.matmul(whole[:].rearrange("p t h -> p (t h)"), ones[:], g[:].rearrange("p t h -> p (t h)"),
                      start=True, stop=True).then_inc(summed, 1)

        @block.scalar
        def _(act):
            act.wait_ge(loaded, 48)
            act.copy(w_hi[:], w_raw[:]).then_inc(split, 1)
            act.activation(rate[:], rate[:], ACT.Exp).then_inc(a_step, 1)
            act.wait_ge(d_step, 4)
            act.activation(t[1][:], t[1][:], ACT.Exp).then_inc(a_step, 1)
            act.wait_ge(d_step, 5)
            act.activation(t[0][:], t[0][:], ACT.Exp, scale=-1.0).then_inc(a_step, 1)
            act.wait_ge(d_step, 6)
            act.activation(t[3][:], t[2][:], ACT.Ln).then_inc(a_step, 1)
            act.wait_ge(d_step, 20)
            act.activation(exp_gc[:], gc[:], ACT.Exp).then_inc(a_step, 1)
            act.activation(exp_rest[:], exp_rest[:], ACT.Exp).then_inc(a_step, 1)
            act.activation(exp_all[:], exp_all[:], ACT.Exp).then_inc(a_step, 1)

        @block.vector
        def _(dve):
            count = [0]

            def step(op):
                count[0] += 1
                op.then_inc(d_step, 1)
                dve.wait_ge(d_step, count[0])

            step(dve.memset(ones[:], 1.0))
            dve.wait_ge(split, 1)
            dve.tensor_tensor(w_lo[:], w_raw[:], f32(w_hi[:]), ALU.subtract).then_inc(split, 1)
            dve.wait_ge(projected, 1)
            step(dve.tensor_tensor(t[4][:], acc[:, :, H:2 * H], dt[:].unsqueeze(1).broadcast_to([P, TT, H]), ALU.add))
            step(dve.tensor_scalar(t[1][:], t[4][:], -1.0, None, ALU.mult))
            step(dve.tensor_tensor(t[1][:], t[1][:], t[4][:], ALU.min))
            step(dve.tensor_copy(t[0][:], acc[:, :, 0:H]))
            dve.wait_ge(a_step, 2)
            step(dve.tensor_scalar(t[2][:], t[1][:], 1.0, None, ALU.add))
            step(dve.tensor_scalar(t[5][:], t[2][:], -1.0, None, ALU.add))
            step(dve.tensor_scalar(t[6][:], t[5][:], 0.0, None, ALU.is_equal))
            step(dve.tensor_tensor(t[5][:], t[5][:], t[6][:], ALU.add))
            step(dve.reciprocal(t[5][:], t[5][:]))
            dve.wait_ge(a_step, 4)
            step(dve.tensor_tensor(t[3][:], t[3][:], t[5][:], ALU.mult))
            step(dve.tensor_tensor(t[3][:], t[3][:], t[6][:], ALU.add))
            step(dve.tensor_tensor(t[3][:], t[3][:], t[1][:], ALU.mult))
            step(dve.tensor_scalar(t[4][:], t[4][:], 0.0, None, ALU.max))
            step(dve.tensor_tensor(t[4][:], t[4][:], t[3][:], ALU.add))
            step(dve.tensor_tensor(t[4][:], t[4][:], rate[:].unsqueeze(1).broadcast_to([P, TT, H]), ALU.mult))
            step(dve.tensor_scalar(g[:], t[4][:], -1.0, None, ALU.mult))
            step(dve.tensor_scalar(t[7][:], t[0][:], 1.0, None, ALU.add))
            dve.reciprocal(beta[:], t[7][:]).then_inc(split, 1)
            dve.wait_ge(summed, 1)
            step(dve.tensor_copy(gc[:], sums[:]))
            dve.tensor_copy(exp_all[:], whole[:]).then_inc(split, 1)
            step(dve.tensor_tensor(exp_rest[:], whole[:], gc[:], ALU.subtract))


LEVELS = 6


def delta_constants():
    i = np.arange(P)
    upper = (i[None, :] >= i[:, None]).astype(np.float32)
    first = -((i[:, None] // 2 == i[None, :] // 2) & (i[:, None] < i[None, :])).astype(np.float32)
    joins = []
    for level in range(1, LEVELS + 1):
        b = 2 ** level
        joins.append((i[:, None] // (2 * b) == i[None, :] // (2 * b)) & (i[:, None] % (2 * b) >= b) & (i[None, :] % (2 * b) < b))
    return upper, first, np.stack(joins).astype(np.float32)


def delta_rule(nc, qkv, gate_dram, norm_w, first_dram, joins_dram, upper, ident, beta, gates, a):
    H = GDN_HEADS
    HG = H // 2
    g, gc, exp_gc, exp_rest, exp_all = gates
    with ExitStack() as ctx:
        sc = Scope(nc, ctx, "gdn")
        x = sc.sbuf("x", [P, 2, 3 * H, P])
        gate = sc.sbuf("gate", [P, 2, H, P])
        squares = sc.sbuf("squares", [P, 2 * H, P])
        sumsq = sc.sbuf("sumsq", [P, 2 * H])
        norm = sc.sbuf("norm", [P, 2 * H])
        norm_scale = sc.sbuf("norm_scale", [P, 2 * H])
        norm_eps = sc.sbuf("norm_eps", [P, 2 * H])
        power = sc.sbuf("power", [P, 2 * H])
        rms_eps = sc.sbuf("rms_eps", [P, H])
        factor = sc.sbuf("factor", [P, 4, H])
        k_n = sc.sbuf("k_n", [P, H, P])
        k_b = sc.sbuf("k_b", [P, H, P])
        q_n = sc.sbuf("q_n", [P, H, P])
        q_d = sc.sbuf("q_d", [P, H, P])
        k_be = sc.sbuf("k_be", [P, 2, H, P])
        k_d = sc.sbuf("k_d", [P, 2, H, P])
        v_b = sc.sbuf("v_b", [P, 2, H, P])
        k_nt = sc.sbuf("k_nt", [P, H, P])
        k_bt = sc.sbuf("k_bt", [P, H, P])
        q_nt = sc.sbuf("q_nt", [P, H, P])
        q_dt = sc.sbuf("q_dt", [P, 2, H, P])
        g_rep = sc.sbuf("g_rep", [P, H, P])
        decay = sc.sbuf("decay", [P, H, P])
        b_mat = sc.sbuf("b_mat", [P, H, P])
        attn = sc.sbuf("attn", [P, 2, H, P])
        xt = sc.sbuf("xt", [P, 2, H, P])
        xm = sc.sbuf("xm", [P, H, P])
        t_m = sc.sbuf("t_m", [P, H, P])
        w_t = sc.sbuf("w_t", [P, H, P])
        v_new = sc.sbuf("v_new", [P, H, P])
        state = sc.sbuf("state", [P, 2, H, P])
        y = sc.sbuf("y", [P, H, P])
        o_sumsq = sc.sbuf("o_sumsq", [P, H])
        o_norm = sc.sbuf("o_norm", [P, H])
        weight = sc.sbuf("weight", [P, P])
        first = sc.sbuf("first", [P, P])
        joins = sc.sbuf("joins", [P, LEVELS, P])
        bank = sc.psum("bank", [P, 8, NB])
        pairs = [bank[:, 2 * i:2 * i + 2].rearrange("p b (h t) -> p (b h) t", t=P) for i in range(4)]
        consts_in = sc.sem("consts_in")
        consts_set = sc.sem("consts_set")
        x_in = [sc.sem(f"x_in{s}") for s in range(2)]
        slot_seen = sc.sem("slot_seen")
        gate_in = [sc.sem(f"gate_in{s}") for s in range(2)]
        squared = sc.sem("squared")
        sq_summed = sc.sem("sq_summed")
        norm_step = sc.sem("norm_step")
        norm_seen = sc.sem("norm_seen")
        kn_done = sc.sem("kn_done")
        kb_done = sc.sem("kb_done")
        qn_done = sc.sem("qn_done")
        pool_ops = sc.sem("pool_ops")
        g_done = sc.sem("g_done")
        g_rows = sc.sem("g_rows")
        diff_done = sc.sem("diff_done")
        decay_exp = sc.sem("decay_exp")
        decay_done = sc.sem("decay_done")
        kn_turned, kn_copied = sc.sem("kn_turned"), sc.sem("kn_copied")
        kb_turned, kb_copied = sc.sem("kb_turned"), sc.sem("kb_copied")
        qn_turned, qn_copied = sc.sem("qn_turned"), sc.sem("qn_copied")
        qd_turned, qd_copied = sc.sem("qd_turned"), sc.sem("qd_copied")
        kk_done, b_done = sc.sem("kk_done"), sc.sem("b_done")
        qk_done, attn_done = sc.sem("qk_done"), sc.sem("attn_done")
        first_done = sc.sem("first_done")
        t_done, tm_done = sc.sem("t_done"), sc.sem("tm_done")
        d_done, xt_done = sc.sem("d_done"), sc.sem("xt_done")
        x_done, x_copied = sc.sem("x_done"), sc.sem("x_copied")
        wt_done, wt_copied = sc.sem("wt_done"), sc.sem("wt_copied")
        v_done, v_copied = sc.sem("v_done"), sc.sem("v_copied")
        o_done, o_copied = sc.sem("o_done"), sc.sem("o_copied")
        o_squared, o_summed = sc.sem("o_squared"), sc.sem("o_summed")
        o_norm_step = sc.sem("o_norm_step")
        kv_done = sc.sem("kv_done")
        state_done = sc.sem("state_done")
        silu_done, gated = sc.sem("silu_done"), sc.sem("gated")
        y_done = sc.sem("y_done")
        y_turned = sc.sem("y_turned")
        y_copied = sc.sem("y_copied")
        XD = 1 + 2 * LEVELS

        block = ctx.enter_context(nc.Block())

        def per_head(ap):
            return ap.unsqueeze(2).broadcast_to([P, H, P])

        def heads(ap):
            return ap.unsqueeze(1).broadcast_to([P, H, P])

        def group(ap, q):
            return ap[:, q * HG:(q + 1) * HG]

        @block.sync
        def _(sp):
            sp.dma_start(weight[:], norm_w.broadcast_to([P, P])).then_inc(consts_in, 16)
            sp.dma_start(first[:], first_dram).then_inc(consts_in, 16)
            sp.dma_start(joins[:], joins_dram.rearrange("l p n -> p l n")).then_inc(consts_in, 16)
            with sp.Fori(0, TT // 2) as i:
                for s in range(2):
                    n = 2 * i + s
                    sp.wait_ge(pool_ops, 4 * n + 4)
                    sp.sem_inc(slot_seen, 1)
                    sp.wait_ge(kb_done, n + 1)
                    sp.wait_ge(qn_done, n + 1)
                    sp.dma_start(x[:, s].rearrange("p h d -> p (h d)"),
                                 qkv[ds(n, 1)].rearrange("a p n -> (a p) n")).then_inc(x_in[s], 16)
                    sp.wait_ge(y_done, 8 * n + 8)
                    sp.dma_start(gate[:, s].rearrange("p h d -> p (h d)"), gate_dram[ds(n * P, P), :]
                                 ).then_inc(gate_in[s], 16)

        @block.tensor
        def _(pe):
            pe.sem_inc(y_turned, 1)

            def turn(dst, src, done):
                for h in range(H):
                    mm = pe.transpose(dst[:, h], src[:, h], ident[:])
                mm.then_inc(done, 1)

            def front(m, step, s):
                if step == 1:
                    pe.wait_ge(g_done, m + 1)
                    for h in range(H):
                        mm = pe.matmul(pairs[2][:, h], g_rep[:, h], upper[:], start=True, stop=True)
                    mm.then_inc(g_rows, 1)
                if step == 3:
                    pe.wait_ge(kn_done, m + 1)
                    pe.wait_ge(state_done, 16 + 8 * m - 8)
                    turn(pairs[3], k_n, kn_turned)
                if step == 4:
                    pe.wait_ge(kb_done, 2 + m + 1)
                    pe.wait_ge(diff_done, 8 * m + 8)
                    turn(pairs[2], k_b, kb_turned)
                if step == 5:
                    pe.wait_ge(qn_done, 2 + m + 1)
                    pe.wait_ge(kn_copied, m + 1)
                    turn(pairs[3], q_n, qn_turned)
                if step == 6:
                    pe.wait_ge(kb_copied, m + 1)
                    pe.wait_ge(y_copied, m + 1)
                    for h in range(H):
                        mm = pe.matmul(pairs[2][:, h], k_nt[:, h], k_bt[:, h], start=True, stop=True)
                    mm.then_inc(kk_done, 1)
                    pe.wait_ge(pool_ops, 8 + 4 * m + 1)
                    pe.wait_ge(qn_copied, m + 1)
                    turn(pairs[3], q_d, qd_turned)
                if step == 7:
                    pe.wait_ge(b_done, m + 1)
                    for h in range(H):
                        mm = pe.matmul(pairs[2][:, h], k_nt[:, h], q_nt[:, h], start=True, stop=True)
                    mm.then_inc(qk_done, 1)

            def first_x(m, s):
                pe.wait_ge(xt_done, XD * m + 1)
                pe.wait_ge(attn_done, 1 + m + 1)
                for q in range(2):
                    for h in range(HG):
                        mm = pe.transpose(group(pairs[2], q)[:, h], group(xt[:, s], q)[:, h], ident[:])
                    mm.then_inc(x_done, 1)

            def level(n, s, l):
                for q in range(2):
                    pe.wait_ge(x_copied, 2 * LEVELS * n + 2 * l - 1 + q)
                    for h in range(HG):
                        mm = pe.matmul(group(pairs[0], q)[:, h], group(b_mat, q)[:, h], group(xm, q)[:, h],
                                       start=True, stop=True)
                    mm.then_inc(t_done, 1)
                if l == 1:
                    pe.wait_ge(o_copied, 1 + n)
                for q in range(2):
                    pe.wait_ge(tm_done, 2 * LEVELS * n + 2 * l - 1 + q)
                    for h in range(HG):
                        mm = pe.matmul(group(pairs[1], q)[:, h], group(t_m, q)[:, h], group(xt[:, s], q)[:, h],
                                       start=True, stop=True)
                    mm.then_inc(d_done, 1)
                if l < LEVELS:
                    for q in range(2):
                        pe.wait_ge(xt_done, XD * n + 2 * l + q)
                        for h in range(HG):
                            mm = pe.transpose(group(pairs[0], q)[:, h], group(xt[:, s], q)[:, h], ident[:])
                        mm.then_inc(x_done, 1)

            def back(n, s, one):
                pe.wait_ge(xt_done, XD * n + XD)
                if one:
                    pe.wait_ge(qd_copied, n + 2)
                for h in range(H):
                    mm = pe.matmul(pairs[3][:, h], k_be[:, s, h], xt[:, s, h], start=True, stop=True)
                mm.then_inc(wt_done, 1)
                if one:
                    front(n + 1, 7, 1 - s)
                pe.wait_ge(wt_copied, n + 1)
                pe.wait_ge(state_done, 16 + 8 * n)
                for h in range(H):
                    pe.matmul(pairs[0][:, h], xt[:, s, h], v_b[:, s, h], start=True, stop=False)
                    mm = pe.matmul(pairs[0][:, h], w_t[:, h], state[:, s, h], start=False, stop=True)
                mm.then_inc(v_done, 1)
                if one:
                    first_x(n + 1, 1 - s)
                pe.wait_ge(v_copied, n + 1)
                for h in range(H):
                    mm = pe.matmul(pairs[3][:, h], k_d[:, s, h], v_new[:, h], start=True, stop=True)
                mm.then_inc(kv_done, 1)
                for h in range(H):
                    pe.matmul(pairs[1][:, h], q_dt[:, s, h], state[:, s, h], start=True, stop=False)
                    mm = pe.matmul(pairs[1][:, h], attn[:, s, h], v_new[:, h], start=False, stop=True)
                mm.then_inc(o_done, 1)

            def output(n):
                pe.wait_ge(y_done, 16 + 8 * n + 8)
                turn(pairs[2], y, y_turned)

            def body(n, s, prev, one, two):
                for l in range(1, LEVELS + 1):
                    level(n, s, l)
                    if l == 5 and prev:
                        if one:
                            pe.wait_ge(kb_copied, n + 2)
                        output(n - 1)
                    if one:
                        front(n + 1, l, 1 - s)
                back(n, s, one)

            for step in range(1, 8):
                front(0, step, 0)
            first_x(0, 0)
            by_chunks(pe, body)
            output(TT - 1)

        @block.scalar
        def _(act):
            act.sem_inc(y_copied, 2)
            act.sem_inc(o_copied, 1)

            def copy(dst, src, ready, count, done, scale=1.0):
                act.wait_ge(ready, count)
                (act.copy(dst, src) if scale == 1.0 else act.mul(dst, src, scale)).then_inc(done, 1)

            def front(m, step, s):
                if step == 0:
                    act.wait_ge(x_in[s], 8 * (m - s) + 16)
                    act.wait_ge(o_summed, m)
                    act.activation(squares[:], x[:, s, 0:2 * H], ACT.Square).then_inc(squared, 1)
                    act.wait_ge(g_rows, 1 + m)
                    act.copy(g_rep[:], g[:, ds(m, 1), :].rearrange("p a h -> p (a h)").unsqueeze(2)
                             .broadcast_to([P, H, P])).then_inc(g_done, 1)
                if step == 1:
                    act.wait_ge(diff_done, 8 * m + 8)
                    act.activation(decay[:], decay[:], ACT.Exp).then_inc(decay_exp, 1)
                if step == 3:
                    copy(k_nt[:], pairs[3], kn_turned, m + 1, kn_copied)
                if step == 4:
                    copy(k_bt[:], pairs[2], kb_turned, m + 1, kb_copied)
                if step == 5:
                    copy(q_nt[:], pairs[3], qn_turned, m + 1, qn_copied)
                if step == 6:
                    copy(q_dt[:, s], pairs[3], qd_turned, m + 1, qd_copied)

            def copy_x(n, l, src):
                for q in range(2):
                    copy(group(xm, q), group(src, q), x_done, 2 * LEVELS * n + 2 * l + q + 1, x_copied)

            def output(n):
                act.wait_ge(y_turned, 1 + n + 1)
                act.copy(a[:, 0:H, ds(n * P, P)], pairs[2]).then_inc(y_copied, 1)

            def square_outputs(n, fronts):
                act.wait_ge(o_copied, 1 + n + 1)
                act.wait_ge(sq_summed, fronts)
                act.activation(squares[:, 0:H], y[:], ACT.Square, scale=GDN_DV ** -0.5).then_inc(o_squared, 1)

            def body(n, s, prev, one, two):
                for l in range(1, LEVELS + 1):
                    if l < LEVELS:
                        copy_x(n, l, pairs[0])
                    if l == 1 and prev:
                        square_outputs(n - 1, n + 2 if one else TT)
                    if one:
                        front(n + 1, l, 1 - s)
                    if l == 5 and prev:
                        output(n - 1)
                copy(w_t[:], pairs[3], wt_done, n + 1, wt_copied, scale=-1.0)
                if two:
                    front(n + 2, 0, s)
                copy(v_new[:], pairs[0], v_done, n + 1, v_copied)
                if one:
                    copy_x(n + 1, 0, pairs[2])
                act.wait_ge(gate_in[s], 8 * (n - s) + 16)
                act.activation(gate[:, s], gate[:, s], ACT.Silu).then_inc(silu_done, 1)
                act.wait_ge(y_turned, 1 + n)
                copy(y[:], pairs[1], o_done, n + 1, o_copied)

            for step in range(8):
                front(0, step, 0)
            front(1, 0, 1)
            copy_x(0, 0, pairs[2])
            by_chunks(act, body)
            square_outputs(TT - 1, TT)
            output(TT - 1)

        @block.vector
        def _(dve):
            dve.sem_inc(g_rows, 1)
            dve.sem_inc(o_summed, 2)
            dve.sem_inc(kb_done, 2)
            dve.sem_inc(qn_done, 2)
            dve.sem_inc(attn_done, 1)
            dve.sem_inc(y_done, 16)
            dve.memset(state[:, 0], 0.0).then_inc(state_done, 16)
            dve.memset(norm_scale[:, 0:H], float(GDN_DK)).then_inc(consts_set, 1)
            dve.memset(norm_scale[:, H:2 * H], 1.0).then_inc(consts_set, 1)
            dve.memset(norm_eps[:, 0:H], 1e-6 * GDN_DK).then_inc(consts_set, 1)
            dve.memset(norm_eps[:, H:2 * H], 1e-6).then_inc(consts_set, 1)
            dve.memset(power[:], -0.5).then_inc(consts_set, 1)
            dve.memset(rms_eps[:], EPS).then_inc(consts_set, 1)
            dve.wait_ge(consts_in, 48)

            def front(m, step, s):
                if step == 0:
                    dve.wait_ge(squared, m + 1)
                    dve.tensor_reduce(sumsq[:], squares[:], AX.X, ALU.add).then_inc(sq_summed, 1)
                if step == 1:
                    dve.wait_ge(g_rows, 1 + m + 1)
                    dve.wait_ge(attn_done, 1 + m)
                    for h in range(H):
                        dve.tensor_scalar(decay[:, h], pairs[2][:, h],
                                          gc[:, ds(m, 1), h:h + 1].rearrange("p a h -> p (a h)"), 0.0,
                                          ALU.subtract, ALU.min).then_inc(diff_done, 1)
                if step == 2:
                    dve.wait_ge(norm_step, 7 * m + 3)
                    dve.tensor_tensor(k_n[:], x[:, s, H:2 * H], per_head(norm[:, H:2 * H]), ALU.mult).then_inc(kn_done, 1)
                if step == 3:
                    dve.wait_ge(norm_step, 7 * m + 7)
                    dve.tensor_tensor(k_b[:], x[:, s, H:2 * H], per_head(factor[:, 0]), ALU.mult).then_inc(kb_done, 1)
                if step == 4:
                    dve.tensor_tensor(q_n[:], x[:, s, 0:H], per_head(norm[:, 0:H]), ALU.mult).then_inc(qn_done, 1)
                if step == 6:
                    dve.wait_ge(kk_done, m + 1)
                    dve.wait_ge(decay_done, m + 1)
                    dve.tensor_tensor(b_mat[:], pairs[2], decay[:], ALU.mult).then_inc(b_done, 1)
                    dve.wait_ge(b_done, m + 1)
                    dve.tensor_tensor(xt[:, s], b_mat[:], heads(first[:]), ALU.mult).then_inc(first_done, 1)
                    dve.wait_ge(first_done, m + 1)
                    dve.tensor_tensor(xt[:, s], xt[:, s], heads(ident[:]), ALU.add).then_inc(xt_done, 1)
                if step == 7:
                    dve.wait_ge(qk_done, m + 1)
                    dve.tensor_tensor(attn[:, s], pairs[2], decay[:], ALU.mult).then_inc(attn_done, 1)

            def level(n, s, l):
                for q in range(2):
                    dve.wait_ge(t_done, 2 * LEVELS * n + 2 * l - 1 + q)
                    dve.tensor_tensor(group(t_m, q), group(pairs[0], q),
                                      joins[:, l - 1].unsqueeze(1).broadcast_to([P, HG, P]), ALU.mult
                                      ).then_inc(tm_done, 1)
                for q in range(2):
                    dve.wait_ge(d_done, 2 * LEVELS * n + 2 * l - 1 + q)
                    dve.tensor_tensor(group(xt[:, s], q), group(xt[:, s], q), group(pairs[1], q),
                                      ALU.subtract).then_inc(xt_done, 1)

            def sum_outputs(n):
                dve.wait_ge(o_squared, n + 1)
                dve.tensor_reduce(o_sumsq[:], squares[:, 0:H], AX.X, ALU.add).then_inc(o_summed, 1)

            def output(n, s):
                dve.wait_ge(o_norm_step, 2 * n + 2)
                dve.wait_ge(gated, n + 1)
                for h in range(H):
                    dve.scalar_tensor_tensor(out=y[:, h], in0=y[:, h], scalar=o_norm[:, h:h + 1],
                                             in1=gate[:, s, h], op0=ALU.mult, op1=ALU.mult).then_inc(y_done, 1)

            def body(n, s, prev, one, two):
                for l in range(1, LEVELS + 1):
                    level(n, s, l)
                    if l == 1 and prev:
                        sum_outputs(n - 1)
                    if one:
                        front(n + 1, l, 1 - s)
                    if l == 3 and prev:
                        output(n - 1, 1 - s)
                if one:
                    front(n + 1, 7, 1 - s)
                if two:
                    front(n + 2, 0, s)
                dve.wait_ge(kv_done, n + 1)
                dve.wait_ge(state_done, 16 + 8 * n)
                for h in range(H):
                    dve.scalar_tensor_tensor(out=state[:, 1 - s, h], in0=state[:, s, h],
                                             scalar=exp_all[:, ds(n, 1), h:h + 1].rearrange("p a h -> p (a h)"),
                                             in1=pairs[3][:, h], op0=ALU.mult, op1=ALU.add).then_inc(state_done, 1)

            for step in range(8):
                front(0, step, 0)
            front(1, 0, 1)
            by_chunks(dve, body)
            sum_outputs(TT - 1)
            output(TT - 1, 1)

        @block.gpsimd
        def _(pool):
            pool.sem_inc(pool_ops, 8)
            pool.wait_ge(consts_set, 6)
            pool.wait_ge(consts_in, 48)

            def at(table, m):
                return table[:, ds(m, 1), :].rearrange("p a h -> p (a h)")

            def norms(m):
                pool.wait_ge(sq_summed, m + 1)
                pool.tensor_tensor(norm[:], sumsq[:], norm_scale[:], ALU.mult).then_inc(norm_step, 1)
                pool.wait_ge(norm_step, 7 * m + 1)
                pool.tensor_tensor(norm[:], norm[:], norm_eps[:], ALU.add).then_inc(norm_step, 1)
                pool.wait_ge(norm_step, 7 * m + 2)
                pool.tensor_tensor(norm[:], norm[:], power[:], ALU.pow).then_inc(norm_step, 1)
                pool.wait_ge(norm_step, 7 * m + 3)
                pool.sem_inc(norm_seen, 1)
                pool.tensor_tensor(factor[:, 0], norm[:, H:2 * H], at(beta, m), ALU.mult).then_inc(norm_step, 1)
                pool.tensor_tensor(factor[:, 2], norm[:, H:2 * H], at(exp_rest, m), ALU.mult).then_inc(norm_step, 1)
                pool.tensor_tensor(factor[:, 3], norm[:, 0:H], at(exp_gc, m), ALU.mult).then_inc(norm_step, 1)
                pool.wait_ge(norm_step, 7 * m + 4)
                pool.sem_inc(norm_seen, 1)
                pool.tensor_tensor(factor[:, 1], factor[:, 0], at(exp_gc, m), ALU.mult).then_inc(norm_step, 1)

            def front(m, s):
                pool.wait_ge(norm_step, 7 * m + 7)
                pool.tensor_tensor(q_d[:], x[:, s, 0:H], per_head(factor[:, 3]), ALU.mult).then_inc(pool_ops, 1)
                pool.wait_ge(decay_exp, m + 1)
                pool.tensor_tensor(decay[:], decay[:], heads(upper[:]), ALU.mult).then_inc(decay_done, 1)
                pool.tensor_tensor(k_be[:, s], x[:, s, H:2 * H], per_head(factor[:, 1]), ALU.mult).then_inc(pool_ops, 1)
                pool.tensor_tensor(k_d[:, s], x[:, s, H:2 * H], per_head(factor[:, 2]), ALU.mult).then_inc(pool_ops, 1)
                pool.tensor_tensor(v_b[:, s], x[:, s, 2 * H:3 * H], per_head(at(beta, m)), ALU.mult
                                   ).then_inc(pool_ops, 1)

            def output_norm(n):
                pool.wait_ge(o_summed, 2 + n + 1)
                pool.tensor_tensor(o_norm[:], o_sumsq[:], rms_eps[:], ALU.add).then_inc(o_norm_step, 1)
                pool.wait_ge(o_norm_step, 2 * n + 1)
                pool.tensor_tensor(o_norm[:], o_norm[:], power[:, 0:H], ALU.pow).then_inc(o_norm_step, 1)

            def body(n, s, prev, one, two):
                if prev:
                    output_norm(n - 1)
                if one:
                    front(n + 1, 1 - s)
                if two:
                    pool.wait_ge(kb_done, 2 + n + 2)
                    pool.wait_ge(qn_done, 2 + n + 2)
                    norms(n + 2)
                pool.wait_ge(silu_done, n + 1)
                pool.tensor_tensor(gate[:, s], gate[:, s], heads(weight[:]), ALU.mult).then_inc(gated, 1)

            norms(0)
            front(0, 0)
            pool.wait_ge(kb_done, 2 + 1)
            pool.wait_ge(qn_done, 2 + 1)
            norms(1)
            by_chunks(pool, body)
            output_norm(TT - 1)


def build(nc, t, out):
    def dram(name, shape):
        return nc.dram_tensor(name, shape, F32).ap()

    hp = dram("hp", [SEQ, EV_IN])
    parts = dram("parts", [3, SEQ, DIL_HEADS * DIL_OUT])
    qkv = dram("qkv", [TT, P, 3 * GDN_W])
    gate = dram("gate", [SEQ, GDN_W])
    x1, x2, x3 = (dram(f"x{i}", [SEQ, D]) for i in (1, 2, 3))

    def k_rows(w):
        return w.rearrange("(k p) n -> k p n", p=P)

    def split_operand(ctx, name):
        sc = Scope(nc, ctx, name)
        return [sc.sbuf(part, [P, KD, SEQ], F32R, side="right") for part in ("hi", "lo")]

    def even_mixer(ident, next_ctx):
        with ExitStack() as ctx:
            x_hi, x_lo = split_operand(ctx, "even_x")
            transpose_phase(nc, "even_turn", t["x"], KD, ident, x_hi, x_lo)
            project_tokens(nc, "even_in", x_hi, x_lo, t["ev_w_in"], EV_IN // NB, hp, 0)
        with ExitStack() as ctx:
            mixed = Scope(nc, ctx, "even").sbuf("mixed", [P, EV_MIX // P, SEQ])
            with ExitStack() as inner:
                tables = Scope(nc, inner, "even_rot")
                cos = tables.sbuf("cos", [P, TT, ROT])
                sin = tables.sbuf("sin", [P, TT, ROT])
                _, _, chunk_decay = retention_constants()
                rotary_tables(nc, t["positions"], t["inv_freq"], cos, sin)
                retention(nc, hp, t["ret_mask"], t["ret_factor"], chunk_decay, ident, cos, sin, mixed)
            dilated(nc, hp, t["dil_masks"], ident, parts)
            combine_dilated(nc, parts, ident, mixed)
            hi, lo = split_operand(next_ctx, "ffn0_x")
            project_out(nc, "even_out", mixed, EV_MIX // P, k_rows(t["ev_w_out"]), t["x"],
                        t["ln1_g"][0:1], t["ln1_b"][0:1], ident, x1, hi, lo)
        return hi, lo

    def odd_mixer(ident, upper, next_ctx):
        with ExitStack() as ctx:
            odd = Scope(nc, ctx, "odd")
            beta = odd.sbuf("beta", [P, TT, GDN_HEADS])
            gates = [odd.sbuf(name, [P, TT, GDN_HEADS]) for name in ("g", "gc", "exp_gc", "exp_rest", "exp_all")]
            with ExitStack() as inner:
                x_hi, x_lo = split_operand(inner, "odd_x")
                transpose_phase(nc, "odd_turn", x2, KD, ident, x_hi, x_lo)
                project_decay(nc, x_hi, x_lo, t["od_w_ba"], t["od_a_log"], t["od_dt_bias"], upper, beta, gates)
                conv_tokens(nc, "odd_qkv", x_hi, x_lo, t["od_w_qkv"], t["od_taps"], ident, 3 * GDN_W // P, qkv)
                project_tokens(nc, "odd_gate", x_hi, x_lo, t["od_w_gate"], GDN_W // NB, gate, 0)
            mixed = odd.sbuf("mixed", [P, KD, SEQ])
            delta_rule(nc, qkv, gate, t["od_norm_w"], t["delta_first"], t["delta_joins"], upper, ident, beta,
                       gates, mixed)
            hi, lo = split_operand(next_ctx, "ffn1_x")
            project_out(nc, "odd_out", mixed, KD, k_rows(t["od_w_out"]), x2, t["ln1_g"][1:2], t["ln1_b"][1:2],
                        ident, x3, hi, lo)
        return hi, lo

    with ExitStack() as top_ctx:
        top = Scope(nc, top_ctx, "top")
        ident = top.sbuf("ident", [P, P])
        upper = top.sbuf("upper", [P, P])
        load_constants(nc, [(ident, t["ident"]), (upper, t["upper"])])
        for layer, (x, y) in enumerate(((x1, x2), (x3, out))):
            with ExitStack() as h_ctx:
                with ExitStack() as x_ctx:
                    if layer == 0:
                        hi, lo = even_mixer(ident, x_ctx)
                    else:
                        hi, lo = odd_mixer(ident, upper, x_ctx)
                    h = Scope(nc, h_ctx, f"ffn{layer}").sbuf("h", [P, KF, SEQ])
                    ffn_up(nc, f"ffn{layer}_up", hi, lo, t[f"ffn_up{layer}"], t[f"ffn_taps{layer}"], h)
                project_out(nc, f"ffn{layer}_down", h, KF, k_rows(t[f"ffn_down{layer}"]), x,
                            t["ln2_g"][layer:layer + 1], t["ln2_b"][layer:layer + 1], ident, y)


def load_constants(nc, pairs):
    with ExitStack() as ctx:
        loaded = Scope(nc, ctx, "const").sem("loaded")
        block = ctx.enter_context(nc.Block())

        @block.sync
        def _(sp):
            for dst, src in pairs:
                sp.dma_start(dst[:], src).then_inc(loaded, 16)
            sp.wait_ge(loaded, 16 * len(pairs))


def lay_out(inputs):
    given = {name: np.asarray(a) for name, a in inputs.items()}
    arrays = {
        "x": given["x"][0],
        "positions": given["positions"][0].reshape(TT, P).T,
        "ev_w_in": given["ev_w_in"][0].reshape(KD, P, EV_IN // NB, NB).transpose(2, 1, 0, 3),
        "ev_w_out": given["ev_w_out"][0],
        "od_w_out": given["od_w_out"][0],
        "od_a_log": given["od_a_log"],
        "od_dt_bias": given["od_dt_bias"],
        "od_norm_w": given["od_norm_w"],
        "od_taps": given["od_conv_w"][0].reshape(GDN_CONV, 3 * GDN_W // P, P).transpose(2, 1, 0),
    }
    w = given["od_w_in"][0]
    arrays["od_w_qkv"] = w[:, :3 * GDN_W].reshape(KD, P, 3 * GDN_W // P, P).transpose(2, 1, 0, 3)
    arrays["od_w_gate"] = w[:, 3 * GDN_W:4 * GDN_W].reshape(KD, P, GDN_W // NB, NB).transpose(2, 1, 0, 3)
    arrays["od_w_ba"] = w[:, 4 * GDN_W:].reshape(KD, P, 2 * GDN_HEADS).transpose(1, 0, 2)
    for layer in range(2):
        taps = np.concatenate([given["ffn_conv_w"][layer], given["ffn_conv_b"][layer][None]], 0)
        arrays[f"ffn_taps{layer}"] = taps.reshape(FFN_CONV + 1, 2, KF, P).transpose(3, 2, 1, 0)
        arrays[f"ffn_up{layer}"] = given["ffn_w_up"][layer].reshape(KD, P, 2, KF, P).transpose(3, 1, 2, 0, 4)
        arrays[f"ffn_down{layer}"] = given["ffn_w_down"][layer]
    for name in ("ln1_g", "ln1_b", "ln2_g", "ln2_b"):
        arrays[name] = given[name]

    arrays["ident"] = np.eye(P, dtype=np.float32)
    arrays["upper"], arrays["delta_first"], arrays["delta_joins"] = delta_constants()
    arrays["ret_mask"], arrays["ret_factor"], _ = retention_constants()
    arrays["dil_masks"] = dilated_masks()
    arrays["inv_freq"] = inverse_frequencies()
    return {name: np.ascontiguousarray(array) for name, array in arrays.items()}


def kernel(**inputs):
    import concourse.bacc as bacc
    from concourse.bass_utils import run_bass_kernel_spmd

    nc = bacc.Bacc("TRN2", target_bir_lowering=False, num_devices=1)
    tensors, feeds = {}, {}
    for name, a in lay_out(inputs).items():
        feeds[f"in_{name}"] = a
        tensors[name] = nc.dram_tensor(f"in_{name}", a.shape, mybir.dt.from_np(a.dtype), kind="ExternalInput").ap()
    out = nc.dram_tensor("out_y", [SEQ, D], F32, kind="ExternalOutput").ap()
    build(nc, tensors, out)
    result = run_bass_kernel_spmd(nc, [feeds], core_ids=[0])
    return result.results[0]["out_y"].reshape(1, SEQ, D)
```

```python
from contextlib import ExitStack

import numpy as np

import concourse.bass as bass
import concourse.mybir as mybir
from concourse.alu_op_type import AluOpType as ALU

P = 128
SEQ = 1024
D = 1024
TT = SEQ // P
KD = D // P
NB = 512
HALF_T = TT // 2
HALF = SEQ // 2

RET_HEADS, RET_DK, RET_DV = 4, 128, 256
DIL_HEADS, DIL_HD = 8, 64
DIL_PAIRS = ((128, 1), (512, 4), (2048, 16))
ROPE_DIMS = DIL_HD // 4
EV_IN = 2 * RET_HEADS * RET_DK + 2 * RET_HEADS * RET_DV + 3 * DIL_HEADS * DIL_HD
EV_MIX = RET_HEADS * RET_DV + DIL_HEADS * DIL_HD
RET_IN = 2 * RET_HEADS * RET_DK + 2 * RET_HEADS * RET_DV
GDN_HEADS, GDN_DK, GDN_DV, GDN_CONV = 8, 128, 128, 4
GDN_W = GDN_HEADS * GDN_DK
D_FF = 2816
KF = D_FF // P
FFN_CONV = 3
DN_ALPHA = (2.0 * 2) ** 0.25
EPS = 1e-5

ACT = mybir.ActivationFunctionType
AX = mybir.AxisListType
F32 = mybir.dt.float32
F32R = mybir.dt.float32r
I32 = mybir.dt.int32
ds = bass.ds


class Scope:

    def __init__(self, nc, ctx, prefix):
        self.nc, self.ctx, self.prefix, self.sems = nc, ctx, prefix, []
        ctx.callback(self.clear)

    def sbuf(self, name, shape, dt=F32, side=None):
        return self.ctx.enter_context(self.nc.sbuf_tensor(f"{self.prefix}_{name}", shape, dt, side=side))

    def psum(self, name, shape, dt=F32):
        return self.ctx.enter_context(self.nc.psum_tensor(f"{self.prefix}_{name}", shape, dt))

    def sem(self, name):
        self.sems.append(self.nc.alloc_semaphore(name=f"{self.prefix}_{name}"))
        return self.sems[-1]

    def clear(self):
        if self.sems:
            self.nc.clear_and_free_semaphores(self.sems)
            self.nc.all_engine_barrier()


def f32(ap):
    return ap.bitcast(F32)


class Beside:

    def __init__(self, **steps):
        self.steps = steps

    def run(self, name, eng):
        if name in self.steps:
            self.steps[name](eng)


def project_tokens(nc, name, xhi, xlo, w, n_tiles, out, x_dram=None, beside=None):
    with ExitStack() as ctx:
        sc = Scope(nc, ctx, name)
        w_raw = sc.sbuf("w_raw", [P, KD, NB])
        w_hi = sc.sbuf("w_hi", [P, KD, NB], F32R)
        w_lo = sc.sbuf("w_lo", [P, KD, NB], F32R)
        stage = sc.sbuf("stage", [P, 2, HALF_T, NB])
        acc = sc.psum("acc", [P, 2, HALF_T, NB])
        w_in = [sc.sem(f"w_in{s}") for s in range(2)]
        hi_ready = sc.sem("hi_ready")
        lo_ready = sc.sem("lo_ready")
        w_used = sc.sem("w_used")
        half_done = sc.sem("half_done")
        acc_free = sc.sem("acc_free")
        stored = [sc.sem(f"stored{s}") for s in range(2)]
        KH = KD // 2
        if x_dram is not None:
            x_raw = sc.sbuf("x_raw", [P, KD, SEQ])
            x_in = [[sc.sem(f"x_in{h}_{k}") for k in range(KD)] for h in range(2)]
            x_hi_ready = sc.sem("x_hi_ready")
            x_lo_ready = sc.sem("x_lo_ready")
        other = beside(Scope(nc, ctx, f"{name}_beside"), [acc[:, 1, 0], acc[:, 1, 1]]) if beside else None

        def half(h):
            return slice(h * HALF, (h + 1) * HALF)

        block = ctx.enter_context(nc.Block())

        @block.sync
        def _(sp):
            def load_w(n, s):
                sp.wait_ge(lo_ready, KD * n + KH * (s + 1))
                sp.dma_start(w_raw[:, s * KH:(s + 1) * KH, :],
                             w[ds(n, 1), :, s * KH:(s + 1) * KH, :].rearrange("a p k n -> p (a k) n")
                             ).then_inc(w_in[s], 16)

            def load_x(h, k):
                sp.dma_start(x_raw[:, k, half(h)], x_dram[:, k, half(h)]).then_inc(x_in[h][k], 16)

            if other:
                other.run("loads", sp)
            for s in range(2):
                load_w(0, s)
                if x_dram is not None:
                    for k in range(s * KH, (s + 1) * KH):
                        load_x(0, k)
            if x_dram is not None:
                for k in range(KD):
                    load_x(1, k)
            with sp.Fori(1, n_tiles) as n:
                for s in range(2):
                    load_w(n, s)

        @block.scalar
        def _(act):
            act.sem_inc(acc_free, 2)
            act.sem_inc(stored[0], 16)
            act.sem_inc(stored[1], 16)

            def split_x(h, k):
                act.wait_ge(x_in[h][k], 16)
                act.copy(xhi[:, k, half(h)], x_raw[:, k, half(h)]).then_inc(x_hi_ready, 1)

            def split_hi(n, with_x=False):
                for k in range(KD):
                    if k % KH == 0:
                        act.wait_ge(w_in[k // KH], 16 * n + 16)
                    act.wait_ge(w_used, KD * n + k + 1)
                    act.copy(w_hi[:, k], w_raw[:, k]).then_inc(hi_ready, 1)
                    if with_x:
                        split_x(0, k)

            def store_half(n, h):
                if h == 0:
                    act.wait_ge(half_done, n + 1)
                else:
                    act.wait_ge(w_used, KD * (n + 2))
                act.wait_ge(stored[h], 16 * n + 16)
                act.copy(stage[:, h], acc[:, h]).then_inc(acc_free, 1)
                act.wait_ge(acc_free, 2 * n + h + 3)
                rows = out[h * HALF:(h + 1) * HALF, ds(n * NB, NB)]
                act.dma_start(rows.rearrange("(t p) n -> p t n", p=P), stage[:, h]).then_inc(stored[h], 16)

            if other:
                other.run("act_early", act)
            split_hi(0, x_dram is not None)
            if x_dram is not None:
                for k in range(KD):
                    split_x(1, k)
            if other:
                other.run("act_late", act)
            with act.Fori(0, n_tiles - 1) as n:
                store_half(n, 0)
                split_hi(n + 1)
                store_half(n, 1)
            store_half(n_tiles - 1, 0)
            store_half(n_tiles - 1, 1)
            for h in range(2):
                act.wait_ge(stored[h], 16 * n_tiles + 16)

        @block.vector
        def _(dve):
            def split_x(h, k):
                dve.wait_ge(x_hi_ready, h * KD + k + 1)
                dve.tensor_tensor(xlo[:, k, half(h)], x_raw[:, k, half(h)], f32(xhi[:, k, half(h)]),
                                  ALU.subtract).then_inc(x_lo_ready, 1)

            def split_lo(n, with_x=False):
                for k in range(KD):
                    dve.wait_ge(hi_ready, KD * n + k + 1)
                    dve.tensor_tensor(w_lo[:, k], w_raw[:, k], f32(w_hi[:, k]), ALU.subtract).then_inc(lo_ready, 1)
                    if with_x:
                        split_x(0, k)

            dve.sem_inc(lo_ready, KD)
            if other:
                other.run("dve_early", dve)
            split_lo(0, x_dram is not None)
            if x_dram is not None:
                for k in range(KD):
                    split_x(1, k)
            if other:
                other.run("dve_late", dve)
            with dve.Fori(1, n_tiles) as n:
                split_lo(n)

        @block.tensor
        def _(pe):
            def products(n, first):
                for h in range(2):
                    if first and h == 1 and other:
                        other.run("pe_halfway", pe)
                    pe.wait_ge(acc_free, 2 * n + h + 1)
                    for k in range(KD):
                        if h == 0:
                            pe.wait_ge(lo_ready, KD * (n + 1) + k + 1)
                        if first and x_dram is not None:
                            pe.wait_ge(x_lo_ready, h * KD + k + 1)
                        for t in range(HALF_T):
                            tok = slice(h * HALF + t * P, h * HALF + (t + 1) * P)
                            pe.matmul(acc[:, h, t], xhi[:, k, tok], w_hi[:, k], start=(k == 0), stop=False)
                            pe.matmul(acc[:, h, t], xhi[:, k, tok], w_lo[:, k], start=False, stop=False)
                            mm = pe.matmul(acc[:, h, t], xlo[:, k, tok], w_hi[:, k],
                                           start=False, stop=(k == KD - 1))
                        if h == 1:
                            mm.then_inc(w_used, 1)
                        if h == 0 and k == KD - 1:
                            mm.then_inc(half_done, 1)
                        if first and h == 0 and k == 1 and other:
                            other.run("pe_between", pe)

            pe.sem_inc(w_used, KD)
            if other:
                other.run("pe_early", pe)
            products(0, True)
            with pe.Fori(1, n_tiles) as n:
                products(n, False)


def ffn_up(nc, name, xhi, xlo, w, taps_dram, h):
    with ExitStack() as ctx:
        sc = Scope(nc, ctx, name)
        w_raw = sc.sbuf("w_raw", [P, 2, KD, P])
        w_hi = sc.sbuf("w_hi", [P, 2, 2, KD, P], F32R)
        w_lo = sc.sbuf("w_lo", [P, 2, 2, KD, P], F32R)
        conv = sc.sbuf("conv", [P, 2, SEQ])
        taps = sc.sbuf("taps", [P, KF, 2, FFN_CONV + 1])
        acc = sc.psum("acc", [P, 2, 2, SEQ])
        taps_in = sc.sem("taps_in")
        w_in = sc.sem("w_in")
        hi_ready = sc.sem("hi_ready")
        lo_ready = sc.sem("lo_ready")
        prod_done = sc.sem("prod_done")
        tap_done = sc.sem("tap_done")
        tap_added = sc.sem("tap_added")
        gate_done = sc.sem("gate_done")
        acc_free = sc.sem("acc_free")
        h_done = sc.sem("h_done")

        def tap(j, part, c):
            return taps[:, ds(j, 1), part, c:c + 1].rearrange("p a c -> p (a c)")

        block = ctx.enter_context(nc.Block())

        @block.sync
        def _(sp):
            sp.dma_start(taps[:], taps_dram).then_inc(taps_in, 16)
            with sp.Fori(0, KF) as j:
                sp.wait_ge(lo_ready, j + 1)
                sp.dma_start(w_raw[:], w[ds(j, 1)].rearrange("a p g k n -> p (a g) k n")).then_inc(w_in, 16)

        @block.tensor
        def _(pe):
            pe.sem_inc(prod_done, 4)
            with pe.Fori(0, KF // 2) as i:
                for s in range(2):
                    j = 2 * i + s
                    pe.wait_ge(lo_ready, j + 2)
                    pe.wait_ge(acc_free, j + 1)
                    for g in range(2):
                        for k in range(KD):
                            for ww, xx in ((w_hi, xhi), (w_hi, xlo), (w_lo, xhi)):
                                for hf in range(2):
                                    tok = slice(hf * HALF, (hf + 1) * HALF)
                                    mm = pe.matmul(acc[:, s, g, tok], ww[:, s, g, k], xx[:, k, tok],
                                                   start=(k == 0 and ww is w_hi and xx is xhi),
                                                   stop=(k == KD - 1 and ww is w_lo))
                        mm.then_inc(prod_done, 1)

        @block.scalar
        def _(act):
            def split_hi(j, s):
                act.wait_ge(w_in, 16 * j + 16)
                act.wait_ge(prod_done, 2 * j + 2)
                act.copy(w_hi[:, s], w_raw[:]).then_inc(hi_ready, 1)

            def last_tap(j, s):
                act.wait_ge(h_done, j + 1)
                for g in range(2):
                    act.wait_ge(prod_done, 2 * j + g + 5)
                    act.activation(conv[:, g], acc[:, s, g], ACT.Identity, bias=tap(j, g, FFN_CONV),
                                   scale=tap(j, g, FFN_CONV - 1)).then_inc(tap_done, 1)
                act.wait_ge(gate_done, 2 * j + 1)
                act.activation(conv[:, 0], conv[:, 0], ACT.Silu).then_inc(gate_done, 1)

            act.wait_ge(taps_in, 16)
            split_hi(0, 0)
            with act.Fori(0, KF // 2 - 1) as i:
                for s in range(2):
                    split_hi(2 * i + s + 1, 1 - s)
                    last_tap(2 * i + s, s)
            split_hi(KF - 1, 1)
            last_tap(KF - 2, 0)
            last_tap(KF - 1, 1)

        @block.vector
        def _(dve):
            dve.sem_inc(lo_ready, 1)
            dve.sem_inc(acc_free, 2)
            dve.sem_inc(h_done, 1)
            def split_lo(j, s):
                dve.wait_ge(hi_ready, j + 1)
                dve.tensor_tensor(w_lo[:, s], w_raw[:], f32(w_hi[:, s]), ALU.subtract).then_inc(lo_ready, 1)

            def other_taps(j, s):
                for g in range(2):
                    dve.wait_ge(tap_done, 2 * j + g + 1)
                    c = conv[:, g]
                    dve.scalar_tensor_tensor(out=c[:, 1:SEQ], in0=acc[:, s, g, 0:SEQ - 1], scalar=tap(j, g, 1),
                                             in1=c[:, 1:SEQ], op0=ALU.mult, op1=ALU.add).then_inc(tap_added, 1)
                    dve.wait_ge(tap_added, 2 * j + g + 1)
                    last = dve.scalar_tensor_tensor(out=c[:, 2:SEQ], in0=acc[:, s, g, 0:SEQ - 2],
                                                    scalar=tap(j, g, 0), in1=c[:, 2:SEQ],
                                                    op0=ALU.mult, op1=ALU.add)
                    last.then_inc(gate_done if g == 0 else acc_free, 1)
                dve.wait_ge(gate_done, 2 * j + 2)
                dve.wait_ge(acc_free, j + 3)
                dve.tensor_tensor(h[:, ds(j, 1), :].rearrange("p a t -> p (a t)"), conv[:, 0], conv[:, 1],
                                  ALU.mult).then_inc(h_done, 1)

            dve.wait_ge(taps_in, 16)
            split_lo(0, 0)
            with dve.Fori(0, KF // 2 - 1) as i:
                for s in range(2):
                    split_lo(2 * i + s + 1, 1 - s)
                    other_taps(2 * i + s, s)
            split_lo(KF - 1, 1)
            other_taps(KF - 2, 0)
            other_taps(KF - 1, 1)


def project_out(nc, name, a, k_tiles, w, resid, gain, bias, ident, out, hi=None, lo=None):
    with ExitStack() as ctx:
        sc = Scope(nc, ctx, name)
        w_raw = sc.sbuf("w_raw", [P, 2, D])
        w_hi = sc.sbuf("w_hi", [P, 2, D], F32R)
        w_lo = sc.sbuf("w_lo", [P, 2, D], F32R)
        a_hi = sc.sbuf("a_hi", [P, 2, HALF], F32R)
        a_lo = sc.sbuf("a_lo", [P, 2, HALF], F32R)
        y = sc.sbuf("y", [P, TT, D])
        gain_b = sc.sbuf("gain_b", [P, D])
        bias_b = sc.sbuf("bias_b", [P, D])
        stats = sc.sbuf("stats", [P, TT, 2, 6])
        mean_var = sc.sbuf("mean_var", [P, TT, 2])
        rstd = sc.sbuf("rstd", [P, TT, 1])
        power = sc.sbuf("power", [P, 1])
        acc = sc.psum("acc", [P, HALF_T, 2, NB])
        w_in = [sc.sem(f"w_in{s}") for s in range(2)]
        resid_in = sc.sem("resid_in")
        affine_in = sc.sem("affine_in")
        power_set = sc.sem("power_set")
        hi_ready = sc.sem("hi_ready")
        lo_ready = sc.sem("lo_ready")
        step_done = sc.sem("step_done")
        summed = sc.sem("summed")
        stats_done = sc.sem("stats_done")
        moments = sc.sem("moments")
        rstd_ready = sc.sem("rstd_ready")
        centred = sc.sem("centred")
        finished = sc.sem("finished")
        turned = sc.sem("turned")
        hi_copied = sc.sem("hi_copied")
        lo_copied = sc.sem("lo_copied")
        stored = sc.sem("stored")
        KP = k_tiles // 2
        PEELED = 8

        def sums(t):
            return acc[:, t % HALF_T].rearrange("p b n -> p (b n)")

        def turned_ps(t):
            return sums(t).rearrange("p (k t) -> p k t", t=P)

        block = ctx.enter_context(nc.Block())

        @block.sync
        def _(sp):
            def load(step, k, s):
                sp.wait_ge(lo_ready, 2 * step + 2)
                sp.dma_start(w_raw[:, s], w[ds(k, 1)].rearrange("a p n -> (a p) n")).then_inc(w_in[s], 16)

            load(0, 0, 0)
            load(1, 1, 1)
            for k in range(2, 6):
                load(k, k, k % 2)
                for t in (2 * k - 4, 2 * k - 3):
                    sp.dma_start(y[:, t], resid[t * P:(t + 1) * P, :]).then_inc(resid_in, 16)
            sp.dma_start(gain_b[:], gain.broadcast_to([P, D])).then_inc(affine_in, 16)
            sp.dma_start(bias_b[:], bias.broadcast_to([P, D])).then_inc(affine_in, 16)
            for hf in range(2):
                with sp.Fori(3 - 3 * hf, KP) as i:
                    for s in range(2):
                        load(hf * k_tiles + 2 * i + s, 2 * i + s, s)
            for t in range(TT):
                sp.wait_ge(finished, t + 1)
                sp.dma_start(out[t * P:(t + 1) * P, :], y[:, t]).then_inc(stored, 16)
            sp.wait_ge(stored, 16 * TT)

        @block.scalar
        def _(act):
            for hf in range(2):
                with act.Fori(0, KP) as i:
                    for s in range(2):
                        step = hf * k_tiles + 2 * i + s
                        act.wait_ge(step_done, step + 1)
                        act.copy(a_hi[:, s], a[:, ds(2 * i + s, 1), hf * HALF:(hf + 1) * HALF]
                                 .rearrange("p a t -> p (a t)")).then_inc(hi_ready, 1)
                        act.wait_ge(w_in[s], 16 * (hf * KP + i) + 16)
                        act.copy(w_hi[:, s], w_raw[:, s]).then_inc(hi_ready, 1)
            if hi is not None:
                for t in range(TT):
                    act.wait_ge(turned, t + 1)
                    act.copy(hi[:, :, t * P:(t + 1) * P], turned_ps(t)).then_inc(hi_copied, 1)

        @block.tensor
        def _(pe):
            pe.sem_inc(step_done, 2)

            def products(step, s, hf, first, last):
                pe.wait_ge(lo_ready, 2 * step + 6)
                for t in range(HALF_T):
                    if first and hf == 1:
                        pe.wait_ge(summed, t + 1)
                    tok = slice(t * P, (t + 1) * P)
                    for aa, ww in ((a_hi, w_hi), (a_hi, w_lo), (a_lo, w_hi)):
                        for n in range(2):
                            mm = pe.matmul(acc[:, t, n], aa[:, s, tok], ww[:, s, n * NB:(n + 1) * NB],
                                           start=(first and aa is a_hi and ww is w_hi),
                                           stop=(last and aa is a_lo))
                mm.then_inc(step_done, 1)

            for hf in range(2):
                base = hf * k_tiles
                products(base, 0, hf, True, False)
                products(base + 1, 1, hf, False, False)
                with pe.Fori(1, KP - 1) as i:
                    for s in range(2):
                        products(base + 2 * i + s, s, hf, False, False)
                products(base + k_tiles - 2, 0, hf, False, False)
                products(base + k_tiles - 1, 1, hf, False, True)
            if hi is not None:
                for t in range(TT):
                    pe.wait_ge(finished, t + 1)
                    if t < HALF_T:
                        pe.wait_ge(summed, HALF_T + t + 1)
                    else:
                        pe.wait_ge(lo_copied, t - HALF_T + 1)
                    for k in range(KD):
                        mm = pe.transpose(turned_ps(t)[:, k], y[:, t, k * P:(k + 1) * P], ident[:])
                    mm.then_inc(turned, 1)

        @block.vector
        def _(dve):
            dve.sem_inc(lo_ready, 4)
            dve.memset(power[:], -0.5).then_inc(power_set, 1)

            def split_lo(hf, k, s):
                step = hf * k_tiles + k
                dve.wait_ge(hi_ready, 2 * step + 1)
                dve.tensor_tensor(a_lo[:, s], a[:, ds(k, 1), hf * HALF:(hf + 1) * HALF].rearrange("p a t -> p (a t)"),
                                  f32(a_hi[:, s]), ALU.subtract).then_inc(lo_ready, 1)
                dve.wait_ge(hi_ready, 2 * step + 2)
                dve.tensor_tensor(w_lo[:, s], w_raw[:, s], f32(w_hi[:, s]), ALU.subtract).then_inc(lo_ready, 1)

            def add_resid(t):
                dve.scalar_tensor_tensor(out=y[:, t], in0=y[:, t], scalar=DN_ALPHA, in1=sums(t),
                                         op0=ALU.mult, op1=ALU.add).then_inc(summed, 1)

            def tile_moments(t):
                dve.wait_ge(summed, t + 1)
                for b in range(2):
                    dve.bn_stats(stats[:, t, b], y[:, t, b * NB:(b + 1) * NB]).then_inc(stats_done, 1)
                dve.wait_ge(stats_done, 2 * t + 2)
                dve.bn_aggr(mean_var[:, t], stats[:, t].rearrange("p b c -> p (b c)")).then_inc(moments, 1)

            def centre(t):
                dve.wait_ge(moments, t + 1)
                dve.scalar_tensor_tensor(out=y[:, t], in0=y[:, t], scalar=mean_var[:, t, 0:1], in1=gain_b[:],
                                         op0=ALU.subtract, op1=ALU.mult).then_inc(centred, 1)

            def finish(t):
                dve.wait_ge(centred, t + 1)
                dve.wait_ge(rstd_ready, 2 * t + 2)
                dve.scalar_tensor_tensor(out=y[:, t], in0=y[:, t], scalar=rstd[:, t], in1=bias_b[:],
                                         op0=ALU.mult, op1=ALU.add).then_inc(finished, 1)

            def turned_lo(t):
                if hi is not None:
                    tok = slice(t * P, (t + 1) * P)
                    dve.wait_ge(hi_copied, t + 1)
                    dve.tensor_tensor(lo[:, :, tok], turned_ps(t), f32(hi[:, :, tok]), ALU.subtract).then_inc(lo_copied, 1)

            with dve.Fori(0, KP) as i:
                for s in range(2):
                    split_lo(0, 2 * i + s, s)
            split_lo(1, 0, 0)
            dve.wait_ge(step_done, 2 + k_tiles)
            dve.wait_ge(resid_in, 16 * TT)
            dve.wait_ge(affine_in, 32)
            for t in range(HALF_T):
                add_resid(t)
            for k in range(1, PEELED):
                split_lo(1, k, k % 2)
                if k <= 2:
                    tile_moments(2 * k - 2)
                    tile_moments(2 * k - 1)
                elif k <= 2 + HALF_T:
                    centre(k - 3)
                    finish(k - 3)
            if KP > PEELED // 2:
                with dve.Fori(PEELED // 2, KP) as i:
                    for s in range(2):
                        split_lo(1, 2 * i + s, s)
            dve.wait_ge(step_done, 2 + 2 * k_tiles)
            add_resid(HALF_T)
            for t in range(HALF_T, TT):
                if t + 1 < TT:
                    add_resid(t + 1)
                tile_moments(t)
            for t in range(HALF_T, TT):
                centre(t)
                turned_lo(t - HALF_T)
                finish(t)
            for t in range(HALF_T, TT):
                turned_lo(t)

        @block.gpsimd
        def _(pool):
            pool.wait_ge(power_set, 1)
            for t in range(TT):
                pool.wait_ge(moments, t + 1)
                pool.tensor_scalar(rstd[:, t], mean_var[:, t, 1:2], EPS, None, ALU.add).then_inc(rstd_ready, 1)
                pool.wait_ge(rstd_ready, 2 * t + 1)
                pool.tensor_tensor(rstd[:, t], rstd[:, t], power[:], ALU.pow).then_inc(rstd_ready, 1)


ROT_A = RET_DK // 2
ROT_B = ROPE_DIMS // 2
ROT = ROT_A + ROT_B
TWO_PI_1 = 6.28125
TWO_PI_2 = float(np.array([np.float32(2 * np.pi - 6.28125)]).view(np.int32).__and__(-4096).view(np.float32)[0])
TWO_PI_3 = float(2 * np.pi - TWO_PI_1 - TWO_PI_2)
ROUND = 1.5 * 2.0 ** 23


def inverse_frequencies():
    def steps(theta, n_rot):
        half = np.arange(n_rot // 2, dtype=np.float32)
        return np.power(np.float32(theta), -half * np.float32(2) / np.float32(n_rot))

    return np.concatenate([steps(10000.0, RET_DK), steps(500000.0, ROPE_DIMS)])[None]


def rotary_tables(sc, positions, inv_freq, cos, sin):
    pos_i = sc.sbuf("pos_i", [P, TT], I32)
    pos = sc.sbuf("pos", [P, TT])
    inv = sc.sbuf("inv", [P, ROT])
    ang = sc.sbuf("ang", [P, TT, ROT])
    turns = sc.sbuf("turns", [P, TT, ROT])
    loaded = sc.sem("loaded")
    step = sc.sem("step")
    reduced = sc.sem("reduced")
    tables_done = sc.sem("tables_done")

    def loads(sp):
        sp.dma_start(pos_i[:], positions).then_inc(loaded, 16)
        sp.dma_start(inv[:], inv_freq.broadcast_to([P, ROT])).then_inc(loaded, 16)

    def reduce_angles(dve):
        count = [0]

        def then_wait(op):
            count[0] += 1
            op.then_inc(step, 1)
            dve.wait_ge(step, count[0])

        dve.wait_ge(loaded, 32)
        then_wait(dve.tensor_copy(pos[:], pos_i[:]))
        then_wait(dve.tensor_tensor(ang[:], pos[:].unsqueeze(2).broadcast_to([P, TT, ROT]),
                                    inv[:].unsqueeze(1).broadcast_to([P, TT, ROT]), ALU.mult))
        for table, quarter in ((sin, 0.0), (cos, 0.25)):
            then_wait(dve.tensor_scalar(turns[:], ang[:], 1.0 / (2 * np.pi), quarter, ALU.mult, ALU.add))
            then_wait(dve.tensor_scalar(turns[:], turns[:], ROUND, None, ALU.add))
            then_wait(dve.tensor_scalar(turns[:], turns[:], -ROUND, None, ALU.add))
            then_wait(dve.scalar_tensor_tensor(out=table[:], in0=turns[:], scalar=-TWO_PI_1, in1=ang[:],
                                               op0=ALU.mult, op1=ALU.add))
            then_wait(dve.scalar_tensor_tensor(out=table[:], in0=turns[:], scalar=-TWO_PI_2, in1=table[:],
                                               op0=ALU.mult, op1=ALU.add))
            then_wait(dve.scalar_tensor_tensor(out=table[:], in0=turns[:], scalar=-TWO_PI_3, in1=table[:],
                                               op0=ALU.mult, op1=ALU.add))
            then_wait(dve.tensor_scalar(table[:], table[:], quarter * 2 * np.pi, None, ALU.add))
            then_wait(dve.tensor_scalar(turns[:], table[:], 1.0 / (2 * np.pi), ROUND, ALU.mult, ALU.add))
            then_wait(dve.tensor_scalar(turns[:], turns[:], -ROUND, None, ALU.add))
            then_wait(dve.scalar_tensor_tensor(out=table[:], in0=turns[:], scalar=-2 * np.pi, in1=table[:],
                                               op0=ALU.mult, op1=ALU.add))
            then_wait(dve.tensor_scalar(table[:], table[:], 3.1415925, None, ALU.min))
            dve.tensor_scalar(table[:], table[:], -3.1415925, None, ALU.max).then_inc(reduced, 1)

    def sines(act):
        for n, table in enumerate((sin, cos)):
            act.wait_ge(reduced, n + 1)
            act.activation(table[:], table[:], ACT.Sin).then_inc(tables_done, 1)

    return Beside(loads=loads, dve_late=reduce_angles, act_late=sines)


def retention_constants():
    h = np.arange(RET_HEADS, dtype=np.float64)
    lg = np.log1p(-(2.0 ** (-5.0 - h)))
    idx = np.arange(P, dtype=np.float64)
    rel = idx[None, :] - idx[:, None]
    scale = RET_DK ** -0.5
    mask = np.where(rel[:, None, :] >= 0, np.exp(np.maximum(rel, 0)[:, None, :] * lg[None, :, None]), 0.0) * scale
    xi = np.exp((idx[:, None] + 1) * lg[None, :])
    zeta = np.exp((P - 1 - idx[:, None]) * lg[None, :]) * scale
    return mask.astype(np.float32), np.concatenate([xi, zeta], 1).astype(np.float32), [float(x) for x in np.exp(P * lg)]


def by_pairs(eng, body):
    with eng.Fori(0, TT // 2 - 1) as i:
        for s in range(2):
            body(2 * i + s, s, True)
    body(TT - 2, 0, True)
    body(TT - 1, 1, False)


def by_chunks(eng, body):
    body(0, 0, False, True, True)
    body(1, 1, True, True, True)
    with eng.Fori(1, TT // 2 - 1) as i:
        for s in range(2):
            body(2 * i + s, s, True, True, True)
    body(TT - 2, 0, True, True, False)
    body(TT - 1, 1, True, False, False)


def retention(nc, hp, mask_dram, factor_dram, chunk_decay, ident, cos, sin, a):
    H, W = RET_HEADS, RET_HEADS * RET_DK
    V0, G0, B0 = 2 * W, 2 * W + H * RET_DV, RET_IN
    NBH = 2 * DIL_HEADS
    with ExitStack() as ctx:
        sc = Scope(nc, ctx, "ret")
        qk = sc.sbuf("qk", [P, 2, 2 * W])
        small = sc.sbuf("small", [P, 2, NBH * DIL_HD])
        vg = sc.sbuf("vg", [P, 2, 2 * H * RET_DV])
        rot = sc.sbuf("rot", [P, 2, 2 * H, RET_DK])
        scaled = sc.sbuf("scaled", [P, 2 * H, RET_DK])
        prod = sc.sbuf("prod", [P, 4, 2 * H, ROT_A])
        prod_b = sc.sbuf("prod_b", [P, 4, NBH, ROT_B])
        feat = sc.sbuf("feat", [P, 3 * H, P])
        scores = sc.sbuf("scores", [P, H, P])
        state = sc.sbuf("state", [P, 2, H, RET_DV])
        gate = sc.sbuf("gate", [P, 2, H, RET_DV])
        y = sc.sbuf("y", [P, H, RET_DV])
        squares = sc.sbuf("squares", [P, H, RET_DV])
        sumsq = sc.sbuf("sumsq", [P, 2, H])
        rstd = sc.sbuf("rstd", [P, 2, H])
        power = sc.sbuf("power", [P, H])
        eps = sc.sbuf("eps", [P, H])
        mask = sc.sbuf("mask", [P, H, P])
        factor = sc.sbuf("factor", [P, 2 * H])
        bank = sc.psum("bank", [P, 8, NB])
        t_ps = bank[:, 0:3].rearrange("p b n -> p (b n)").rearrange("p (h t) -> p h t", t=P)
        s_ps = bank[:, 3].rearrange("p (h t) -> p h t", t=P)
        o_ps = bank[:, 4:6].rearrange("p b n -> p (b n)").rearrange("p (h e) -> p h e", e=RET_DV)
        kv_ps = bank[:, 6:8].rearrange("p b n -> p (b n)").rearrange("p (h e) -> p h e", e=RET_DV)
        consts_in = sc.sem("consts_in")
        power_set = sc.sem("power_set")
        qk_in = [sc.sem(f"qk_in{s}") for s in range(2)]
        vg_in = [sc.sem(f"vg_in{s}") for s in range(2)]
        qk_stored = [sc.sem(f"qk_stored{s}") for s in range(2)]
        cos_done = sc.sem("cos_done")
        sin_done = sc.sem("sin_done")
        rot_done = sc.sem("rot_done")
        scaled_done = sc.sem("scaled_done")
        slot_seen = sc.sem("slot_seen")
        qk_prod = sc.sem("qk_prod")
        qk_rot = sc.sem("qk_rot")
        turned = sc.sem("turned")
        feat_ready = sc.sem("feat_ready")
        scores_done = sc.sem("scores_done")
        masked = sc.sem("masked")
        kv_done = sc.sem("kv_done")
        state_ready = sc.sem("state_ready")
        o_done = sc.sem("o_done")
        squared = sc.sem("squared")
        gate_ready = sc.sem("gate_ready")
        rstd_step = sc.sem("rstd_step")
        y_done = sc.sem("y_done")
        y_turned = sc.sem("y_turned")
        y_copied = sc.sem("y_copied")
        block = ctx.enter_context(nc.Block())

        @block.sync
        def _(sp):
            sp.dma_start(mask[:], mask_dram).then_inc(consts_in, 16)
            sp.dma_start(factor[:], factor_dram).then_inc(consts_in, 16)

            def load_qk(n, s):
                sp.dma_start(qk[:, s], hp[ds(n * P, P), 0:2 * W]).then_inc(qk_in[s], 16)
                sp.dma_start(small[:, s], hp[ds(n * P, P), B0:B0 + NBH * DIL_HD]).then_inc(qk_in[s], 16)

            def load_vg(n, s):
                sp.dma_start(vg[:, s], hp[ds(n * P, P), V0:V0 + 2 * H * RET_DV]).then_inc(vg_in[s], 16)

            def store_small(n, s, two):
                sp.wait_ge(qk_rot, 2 + 2 * n + 2)
                sp.dma_start(hp[ds(n * P, P), B0:B0 + NBH * DIL_HD], small[:, s]).then_inc(qk_stored[s], 16)
                if two:
                    sp.wait_ge(cos_done, 2 * n + 2)
                    sp.sem_inc(slot_seen, 1)
                    sp.wait_ge(sin_done, 2 * n + 2)
                    sp.wait_ge(qk_stored[s], 8 * (n - s) + 16)
                    load_qk(n + 2, s)

            def body(n, s, three):
                sp.wait_ge(o_done, n + 1)
                sp.wait_ge(gate_ready, n + 1)
                load_vg(n + 1, 1 - s)
                store_small(n + 1, 1 - s, three)

            load_qk(0, 0)
            load_qk(1, 1)
            load_vg(0, 0)
            store_small(0, 0, True)
            with sp.Fori(0, TT // 2 - 2) as i:
                for s in range(2):
                    body(2 * i + s, s, True)
            for n in range(TT - 4, TT - 1):
                body(n, n % 2, n + 3 < TT)
            for s in range(2):
                sp.wait_ge(qk_stored[s], 16 * (TT // 2))

        @block.vector
        def _(dve):
            dve.sem_inc(rot_done, 2)
            dve.sem_inc(masked, 1)
            dve.sem_inc(y_done, 8)
            dve.memset(state[:, 0].rearrange("p h e -> p (h e)"), 0.0).then_inc(state_ready, 4)
            dve.memset(power[:], -0.5).then_inc(power_set, 1)
            dve.memset(eps[:], EPS).then_inc(power_set, 1)
            dve.wait_ge(consts_in, 32)

            def rotate(n, s):
                heads = qk[:, s].rearrange("p (h d) -> p h d", d=RET_DK)
                c = cos[:, ds(n, 1), 0:ROT_A].broadcast_to([P, 2 * H, ROT_A])
                dve.wait_ge(qk_in[s], 16 * (n - s) + 32)
                dve.wait_ge(rot_done, 2 + 2 * n)
                dve.tensor_tensor(prod[:, 0], heads[:, :, 0:ROT_A], c, ALU.mult).then_inc(cos_done, 1)
                dve.tensor_tensor(prod[:, 1], heads[:, :, ROT_A:RET_DK], c, ALU.mult).then_inc(cos_done, 1)
                dve.wait_ge(cos_done, 2 * n + 2)
                dve.wait_ge(sin_done, 2 * n + 2)
                dve.wait_ge(scaled_done, 2 + n - 1)
                dve.wait_ge(turned, 2 + n - 1)
                dve.tensor_tensor(rot[:, s, :, 0:ROT_A], prod[:, 0], prod[:, 2], ALU.subtract).then_inc(rot_done, 1)
                dve.tensor_tensor(rot[:, s, :, ROT_A:RET_DK], prod[:, 1], prod[:, 3], ALU.add).then_inc(rot_done, 1)

            def output(n, s):
                dve.wait_ge(rstd_step, 2 * n + 2)
                dve.wait_ge(gate_ready, 1 + n + 1)
                dve.wait_ge(y_turned, 1 + n)
                for h in range(H):
                    dve.scalar_tensor_tensor(out=y[:, h], in0=o_ps[:, h], scalar=rstd[:, s, h:h + 1],
                                             in1=gate[:, s, h], op0=ALU.mult, op1=ALU.mult).then_inc(y_done, 1)

            def body(n, s, prev, one, two):
                if prev:
                    output(n - 1, 1 - s)
                dve.wait_ge(scores_done, n + 1)
                dve.tensor_tensor(scores[:], s_ps, mask[:], ALU.mult).then_inc(masked, 1)
                dve.wait_ge(kv_done, 1 + n + 1)
                dve.wait_ge(state_ready, 4 + 4 * n)
                for h in range(H):
                    dve.scalar_tensor_tensor(out=state[:, 1 - s, h], in0=state[:, s, h], scalar=chunk_decay[h],
                                             in1=kv_ps[:, h], op0=ALU.mult, op1=ALU.add).then_inc(state_ready, 1)
                if one:
                    rotate(n + 1, 1 - s)

            rotate(0, 0)
            by_chunks(dve, body)
            output(TT - 1, 1)

        @block.gpsimd
        def _(pool):
            pool.sem_inc(scaled_done, 2)
            pool.sem_inc(qk_rot, 2)
            pool.wait_ge(consts_in, 32)
            pool.wait_ge(power_set, 2)

            def rotate(n, s):
                heads = qk[:, s].rearrange("p (h d) -> p h d", d=RET_DK)
                sn = sin[:, ds(n, 1), 0:ROT_A].broadcast_to([P, 2 * H, ROT_A])
                pool.wait_ge(qk_in[s], 16 * (n - s) + 32)
                pool.wait_ge(rot_done, 2 + 2 * n)
                pool.tensor_tensor(prod[:, 2], heads[:, :, ROT_A:RET_DK], sn, ALU.mult).then_inc(sin_done, 1)
                pool.tensor_tensor(prod[:, 3], heads[:, :, 0:ROT_A], sn, ALU.mult).then_inc(sin_done, 1)
                pairs = small[:, s].rearrange("p (h d) -> p h d", d=DIL_HD)
                d1, d2 = pairs[:, :, 0:ROT_B], pairs[:, :, ROT_B:ROPE_DIMS]
                cb = cos[:, ds(n, 1), ROT_A:ROT].broadcast_to([P, NBH, ROT_B])
                sb = sin[:, ds(n, 1), ROT_A:ROT].broadcast_to([P, NBH, ROT_B])
                pool.wait_ge(qk_rot, 2 + 2 * n)
                for m, (xx, tt) in enumerate(((d1, cb), (d2, cb), (d2, sb), (d1, sb))):
                    pool.tensor_tensor(prod_b[:, m], xx, tt, ALU.mult).then_inc(qk_prod, 1)
                pool.wait_ge(qk_prod, 4 * n + 4)
                pool.tensor_tensor(d1, prod_b[:, 0], prod_b[:, 2], ALU.subtract).then_inc(qk_rot, 1)
                pool.tensor_tensor(d2, prod_b[:, 1], prod_b[:, 3], ALU.add).then_inc(qk_rot, 1)
                pool.wait_ge(rot_done, 2 + 2 * n + 2)
                pool.wait_ge(kv_done, 1 + n)
                pool.tensor_tensor(scaled[:], rot[:, s], factor[:].unsqueeze(2).broadcast_to([P, 2 * H, RET_DK]),
                                   ALU.mult).then_inc(scaled_done, 1)

            def output_norm(n, s):
                pool.wait_ge(squared, 4 + 4 * n + 4)
                pool.tensor_tensor(rstd[:, s], sumsq[:, s], eps[:], ALU.add).then_inc(rstd_step, 1)
                pool.wait_ge(rstd_step, 2 * n + 1)
                pool.tensor_tensor(rstd[:, s], rstd[:, s], power[:], ALU.pow).then_inc(rstd_step, 1)

            def body(n, s, prev, one, two):
                if prev:
                    output_norm(n - 1, 1 - s)
                if one:
                    rotate(n + 1, 1 - s)

            rotate(0, 0)
            by_chunks(pool, body)
            output_norm(TT - 1, 1)

        @block.tensor
        def _(pe):
            pe.sem_inc(turned, 2)
            pe.sem_inc(kv_done, 1)
            pe.sem_inc(y_turned, 1)
            pe.sem_inc(o_done, 1)

            def output(n):
                pe.wait_ge(y_done, 8 + 4 * n + 4)
                for c in range(2 * H):
                    mm = pe.transpose(t_ps[:, c], y[:, c // 2, (c % 2) * P:(c % 2 + 1) * P], ident[:])
                mm.then_inc(y_turned, 1)

            def body(n, s, prev, one, two):
                pe.wait_ge(rot_done, 2 + 2 * n + 2)
                pe.wait_ge(y_copied, n + 1)
                for h in range(2 * H):
                    pe.transpose(t_ps[:, h], rot[:, s, h], ident[:])
                pe.wait_ge(scaled_done, 2 + n + 1)
                for h in range(H):
                    mm = pe.transpose(t_ps[:, 2 * H + h], scaled[:, h], ident[:])
                mm.then_inc(turned, 1)
                pe.wait_ge(state_ready, 4 + 4 * n)
                pe.wait_ge(vg_in[s], 8 * (n - s) + 16)
                for h in range(H):
                    v = vg[:, s, h * RET_DV:(h + 1) * RET_DV]
                    mm = pe.matmul(kv_ps[:, h], scaled[:, H + h], v, start=True, stop=True)
                mm.then_inc(kv_done, 1)
                pe.wait_ge(feat_ready, n + 1)
                pe.wait_ge(masked, 1 + n)
                for h in range(H):
                    mm = pe.matmul(s_ps[:, h], feat[:, H + h], feat[:, h], start=True, stop=True)
                mm.then_inc(scores_done, 1)
                if prev:
                    output(n - 1)
                pe.wait_ge(masked, 1 + n + 1)
                pe.wait_ge(y_done, 8 + 4 * n)
                for h in range(H):
                    v = vg[:, s, h * RET_DV:(h + 1) * RET_DV]
                    pe.matmul(o_ps[:, h], feat[:, 2 * H + h], state[:, s, h], start=True, stop=False)
                    mm = pe.matmul(o_ps[:, h], scores[:, h], v, start=False, stop=True)
                mm.then_inc(o_done, 1)

            by_chunks(pe, body)
            output(TT - 1)

        @block.scalar
        def _(act):
            act.sem_inc(squared, 4)
            act.sem_inc(y_copied, 2)
            act.sem_inc(gate_ready, 1)

            def output(n):
                act.wait_ge(y_turned, 1 + n + 1)
                act.copy(a[:, 0:2 * H, ds(n * P, P)], t_ps[:, 0:2 * H]).then_inc(y_copied, 1)

            def body(n, s, prev, one, two):
                act.wait_ge(vg_in[s], 8 * (n - s) + 16)
                act.wait_ge(y_done, 4 * n + 4)
                act.activation(gate[:, s].rearrange("p h e -> p (h e)"), vg[:, s, H * RET_DV:2 * H * RET_DV],
                               ACT.Silu).then_inc(gate_ready, 1)
                act.wait_ge(turned, 2 + n + 1)
                act.copy(feat[:], t_ps).then_inc(feat_ready, 1)
                if prev:
                    output(n - 1)
                act.wait_ge(o_done, 1 + n + 1)
                act.wait_ge(squared, 4 + 4 * n)
                for h in range(H):
                    act.activation(squares[:, h], o_ps[:, h], ACT.Square, scale=RET_DV ** -0.5,
                                   accum_out=sumsq[:, s, h:h + 1]).then_inc(squared, 1)

            by_chunks(act, body)
            output(TT - 1)


UNITS = 3 * TT
DIL_W = DIL_HEADS * DIL_HD
DIL_OUT = DIL_HD + 2
MASKED = -1e30


def dilated_masks():
    i, j = np.arange(P)[:, None], np.arange(P)[None, :]
    causal = j <= i
    none = np.zeros((P, P), bool)
    pair = causal & (i // (P // 2) == j // (P // 2))
    kinds = [np.concatenate([none, causal], 1), np.concatenate([j >= i, causal], 1), np.concatenate([none, pair], 1)]
    return np.where(np.stack(kinds), 0.0, MASKED).astype(np.float32)


def branch_rows(dram, branch, i, s):
    if branch == 0:
        return [(0, dram[ds((2 * i + s) * P, P), :])]
    if branch == 1:
        rows = dram.rearrange("(b p r) n -> r b p n", b=2, p=P, r=4)[ds(i, 1), s]
        return [(0, rows.rearrange("a p n -> (a p) n"))]
    rows = dram.rearrange("(l r) n -> r l n", r=16)
    return [(h * 64, rows[ds(4 * i + 2 * s + h, 1)].rearrange("a l n -> (a l) n")) for h in range(2)]


def dilated(nc, hp, masks, ident, parts, gathered):
    Q0 = RET_IN
    H = DIL_HEADS
    with ExitStack() as ctx:
        sc = Scope(nc, ctx, "dil")
        qk = sc.sbuf("qk", [P, 2, 2 * DIL_W])
        v = sc.sbuf("v", [P, 2, DIL_W])
        mask = sc.sbuf("mask", [P, 3, 2 * P])
        q_t = sc.sbuf("q_t", [P, 2, 2, H // 2, P])
        k_t = sc.sbuf("k_t", [P, 2, H // 2, P])
        probs = sc.sbuf("probs", [P, 2, H, 2 * P])
        probs_t = sc.sbuf("probs_t", [P, 2 * H, P])
        neg_max = sc.sbuf("neg_max", [P, 2, H, 1])
        part = sc.sbuf("part", [P, 2, H, DIL_OUT])
        bank = sc.psum("bank", [P, 8, NB])
        turn_ps = bank[:, 0:2].rearrange("p b (h t) -> p b h t", t=P)
        o_ps = bank[:, 0:2].rearrange("p b (h e) -> p (b h) e", e=2 * DIL_HD)
        s_ps = [bank[:, 2 + h // 2, h % 2 * 2 * P:(h % 2 + 1) * 2 * P] for h in range(H)]
        pt_ps = bank[:, 6:8].rearrange("p b (h t) -> p (b h) t", t=P)
        qk_in = [sc.sem(f"qk_in{s}") for s in range(2)]
        v_in = [sc.sem(f"v_in{s}") for s in range(2)]
        stored = [sc.sem(f"stored{s}") for s in range(2)]
        mask_in = sc.sem("mask_in")
        gather_done = sc.sem("gather_done")
        cleared = sc.sem("cleared")
        turned = sc.sem("turned")
        q_ready = sc.sem("q_ready")
        k_ready = sc.sem("k_ready")
        scores_done = sc.sem("scores_done")
        scores_seen = sc.sem("scores_seen")
        maxed = sc.sem("maxed")
        negated = sc.sem("negated")
        exp_done = sc.sem("exp_done")
        pt_low = sc.sem("pt_low")
        pt_high = sc.sem("pt_high")
        low_copied = sc.sem("low_copied")
        high_copied = sc.sem("high_copied")
        o_done = sc.sem("o_done")
        o_copied = sc.sem("o_copied")
        block = ctx.enter_context(nc.Block())

        def has_before(branch, s):
            return (True, s == 1, False)[branch]

        def kind(branch, s):
            return (1, s, 2)[branch]

        def by_units(eng, body):
            for branch in range(3):
                last = branch == 2
                with eng.Fori(TT // 2 * branch, TT // 2 * branch + TT // 2 - 1) as i:
                    for s in range(2):
                        body(2 * i + s, s, has_before(branch, s), has_before(branch, 1 - s), kind(branch, 1 - s),
                             True, True)
                u = TT * branch + TT - 2
                after = min(branch + 1, 2)
                body(u, 0, has_before(branch, 0), has_before(branch, 1), kind(branch, 1), True, not last)
                body(u + 1, 1, has_before(branch, 1), has_before(after, 0), kind(after, 0), not last, not last)

        def own(tiles, before):
            return tiles if before else tiles.rearrange("p (h b) t -> p h b t", b=2)[:, :, 1]

        def keys(before):
            return slice(0 if before else P, 2 * P)

        @block.sync
        def _(sp):
            sp.sem_inc(stored[0], 32)
            sp.sem_inc(stored[1], 32)
            def pieces(dst, dram, cols, branch, i, s, sem, store=False):
                rows = branch_rows(dram, branch, i, s)
                for at, r in rows:
                    a, b = dst[at:at + P // len(rows)], r[:, cols]
                    sp.dma_start(*((b, a) if store else (a, b))).then_inc(sem, 32 // len(rows))

            def load_qk(branch, i, s):
                pieces(qk[:, s], hp, slice(Q0, Q0 + 2 * DIL_W), branch, i, s, qk_in[s])

            def load_v(branch, i, s):
                pieces(v[:, s], hp, slice(Q0 + 2 * DIL_W, Q0 + 3 * DIL_W), branch, i, s, v_in[s])

            def later(branch, i, s, by):
                i, s = i + (s + by) // 2, (s + by) % 2
                if isinstance(i, int) and i >= TT // 2:
                    branch, i = branch + 1, i - TT // 2
                return (branch, i, s) if branch < 3 else None

            def unit(branch, i, s, u):
                if later(branch, i, s, 3):
                    sp.wait_ge(maxed, 8 + 8 * u + 16)
                    load_qk(*later(branch, i, s, 3))
                sp.wait_ge(o_copied, 6 + 2 * u + 2)
                pieces(part[:, s].rearrange("p h e -> p (h e)"), parts[branch], slice(0, H * DIL_OUT), branch, i, s,
                       stored[s], store=True)
                if later(branch, i, s, 1):
                    load_v(*later(branch, i, s, 1))

            sp.dma_start(mask[:], masks.rearrange("m p k -> p m k")).then_inc(mask_in, 16)
            load_qk(0, 0, 0)
            load_qk(0, 0, 1)
            load_v(0, 0, 0)
            sp.wait_ge(cleared, 6)
            sp.wait_ge(maxed, 8 + 8)
            load_qk(0, 1, 0)
            for branch in range(3):
                with sp.Fori(0, TT // 2 - 2) as i:
                    for s in range(2):
                        unit(branch, i, s, TT * branch + 2 * i + s)
                if branch > 0:
                    for s in range(2):
                        sp.wait_ge(stored[s], 32 + 32 * branch * (TT // 2))
                    sp.dma_start(gathered[:, branch - 1], parts[branch - 1].rearrange("(t p) n -> p t n", p=P)
                                 ).then_inc(gather_done, 16)
                for i in range(TT // 2 - 2, TT // 2):
                    for s in range(2):
                        unit(branch, i, s, TT * branch + 2 * i + s)
            for s in range(2):
                sp.wait_ge(stored[s], 32 + 32 * (UNITS // 2))
            sp.wait_ge(gather_done, 32)

        @block.tensor
        def _(pe):
            pe.wait_ge(cleared, 6)

            def turn(u, s):
                pe.wait_ge(qk_in[s], 16 * (u - s) + 32)
                pe.wait_ge(o_copied, 2 * u + 2)
                pe.wait_ge(k_ready, u + 1)
                for b in range(2):
                    for c in range(H // 2):
                        col = b * DIL_W + c * P
                        mm = pe.transpose(turn_ps[:, b, c], qk[:, s, col:col + P], ident[:])
                mm.then_inc(turned, 1)

            def score(u, s, before):
                pe.wait_ge(q_ready, 2 * u + 2)
                pe.wait_ge(k_ready, 1 + u + 1)
                pe.wait_ge(maxed, 8 + 8 * u)
                for h in range(H):
                    q = q_t[:, s, h % 2, h // 2]
                    if before:
                        pe.matmul(s_ps[h][:, 0:P], q, k_t[:, 1 - s, h // 2], start=True, stop=True)
                    mm = pe.matmul(s_ps[h][:, P:2 * P], q, k_t[:, s, h // 2], start=True, stop=True)
                    if h % 4 == 3:
                        mm.then_inc(scores_done, 1)

            def turn_probs(u, s, high, before):
                for h in range(H // 2):
                    for b in range(0 if before else 1, 2):
                        mm = pe.transpose(pt_ps[:, 2 * h + b], probs[:, s, high * (H // 2) + h, b * P:(b + 1) * P],
                                          ident[:])
                mm.then_inc(pt_high if high else pt_low, 1)

            def body(u, s, before, next_before, next_mask, one, two):
                pe.wait_ge(exp_done, 8 * u + 4)
                pe.wait_ge(high_copied, 1 + u)
                turn_probs(u, s, 0, before)
                if two:
                    turn(u + 2, s)
                pe.wait_ge(exp_done, 8 * u + 8)
                pe.wait_ge(low_copied, u + 1)
                turn_probs(u, s, 1, before)
                if one:
                    score(u + 1, 1 - s, next_before)
                pe.wait_ge(v_in[s], 16 * (u - s) + 32)
                if two:
                    pe.wait_ge(q_ready, 2 * u + 6)
                for h in range(H):
                    if h == H // 2:
                        pe.wait_ge(high_copied, 1 + u + 1)
                        if two:
                            pe.wait_ge(k_ready, 1 + u + 3)
                    e = slice(h // 2 * 2 * DIL_HD, (h // 2 + 1) * 2 * DIL_HD)
                    if before:
                        pe.matmul(o_ps[:, h], probs_t[:, 2 * h], v[:, 1 - s, e], start=True, stop=False)
                    mm = pe.matmul(o_ps[:, h], probs_t[:, 2 * h + 1], v[:, s, e], start=not before, stop=True)
                mm.then_inc(o_done, 1)

            turn(0, 0)
            score(0, 0, True)
            turn(1, 1)
            by_units(pe, body)

        @block.scalar
        def _(act):
            def q_feats(u, s):
                act.wait_ge(turned, u + 1)
                for parity in range(2):
                    d = slice(parity * DIL_HD, (parity + 1) * DIL_HD)
                    act.mul(q_t[d, s, parity], turn_ps[d, 0], DIL_HD ** -0.5).then_inc(q_ready, 1)

            def k_feats(u, s):
                act.copy(k_t[:, s], turn_ps[:, 1]).then_inc(k_ready, 1)

            def exps(u, s, before):
                act.wait_ge(negated, u + 1)
                for h in range(H):
                    if h == 6:
                        act.wait_ge(pt_low, u + 1)
                        act.copy(own(probs_t[:, 0:H], before), own(pt_ps, before)).then_inc(low_copied, 1)
                    p = probs[:, s, h, keys(before)]
                    act.activation(p, p, ACT.Exp, bias=neg_max[:, s, h],
                                   accum_out=part[:, s, h, DIL_HD + 1:DIL_HD + 2]).then_inc(exp_done, 1)

            def body(u, s, before, next_before, next_mask, one, two):
                if two:
                    q_feats(u + 2, s)
                    act.wait_ge(scores_done, 2 * u + 4)
                    k_feats(u + 2, s)
                if one:
                    exps(u + 1, 1 - s, next_before)

            act.sem_inc(k_ready, 1)
            act.wait_ge(cleared, 6)
            for u in range(2):
                q_feats(u, u)
                if u == 1:
                    act.wait_ge(scores_done, 2)
                k_feats(u, u)
            exps(0, 0, True)
            by_units(act, body)

        @block.vector
        def _(dve):
            dve.memset(k_t[:, 1], 0.0).then_inc(cleared, 1)
            dve.memset(v[:, 1], 0.0).then_inc(cleared, 1)
            for parity in range(2):
                d = slice((1 - parity) * DIL_HD, (2 - parity) * DIL_HD)
                for s in range(2):
                    dve.memset(q_t[d, s, parity], 0.0).then_inc(cleared, 1)
            dve.sem_inc(maxed, 8)
            dve.sem_inc(high_copied, 1)
            dve.sem_inc(o_copied, 6)

            def maxima(u, s, before, kind):
                dve.wait_ge(stored[s], 16 * (u - s) + 32)
                for h in range(H):
                    if h % 4 == 0:
                        dve.wait_ge(scores_done, 2 * u + h // 4 + 1)
                        dve.sem_inc(scores_seen, 1)
                    k = keys(before)
                    dve.tensor_tensor_reduce(probs[:, s, h, k], s_ps[h][:, k], mask[:, kind, k], 1.0, -3e38, ALU.add, ALU.max,
                                             part[:, s, h, DIL_HD:DIL_HD + 1]).then_inc(maxed, 1)
                dve.wait_ge(maxed, 8 + 8 * u + 8)
                dve.tensor_scalar(neg_max[:, s], part[:, s, :, DIL_HD:DIL_HD + 1], -1.0, None,
                                  ALU.mult).then_inc(negated, 1)

            def body(u, s, before, next_before, next_mask, one, two):
                dve.wait_ge(pt_high, u + 1)
                dve.tensor_copy(own(probs_t[:, H:2 * H], before), own(pt_ps, before)).then_inc(high_copied, 1)
                if one:
                    maxima(u + 1, 1 - s, next_before, next_mask)
                dve.wait_ge(o_done, u + 1)
                for parity in range(2):
                    heads = o_ps.rearrange("p (h two) e -> p two h e", two=2)[:, parity]
                    mine = part[:, s].rearrange("p (h two) e -> p two h e", two=2)[:, parity]
                    dve.tensor_copy(mine[:, :, 0:DIL_HD], heads[:, :, parity * DIL_HD:(parity + 1) * DIL_HD]
                                    ).then_inc(o_copied, 1)

            dve.wait_ge(mask_in, 16)
            maxima(0, 0, True, 0)
            by_units(dve, body)


def combine_dilated(nc, parts, gathered, ident, a):
    H, K0 = DIL_HEADS, RET_HEADS * RET_DV // P
    KC = DIL_W // P
    with ExitStack() as ctx:
        sc = Scope(nc, ctx, "comb")
        part = gathered[:].rearrange("p b t (h e) -> p b t h e", h=H)
        top = sc.sbuf("top", [P, 2, H])
        weight = sc.sbuf("weight", [P, 2, 3, H])
        total = sc.sbuf("total", [P, 2, H, DIL_OUT])
        inverse = sc.sbuf("inverse", [P, 2, H, 1])
        y = sc.sbuf("y", [P, 2, H, DIL_HD])
        turn_ps = sc.psum("turn_ps", [P, 2, KC, P])
        part_in = [sc.sem(f"part_in{t}") for t in range(TT)]
        topped = sc.sem("topped")
        diff = sc.sem("diff")
        weighed = sc.sem("weighed")
        first_two = sc.sem("first_two")
        third = sc.sem("third")
        totals = sc.sem("totals")
        inverted = sc.sem("inverted")
        y_done = sc.sem("y_done")
        turned = sc.sem("turned")
        copied = sc.sem("copied")
        block = ctx.enter_context(nc.Block())

        @block.sync
        def _(sp):
            for t in range(TT):
                sp.dma_start(gathered[:, 2, t], parts[2, t * P:(t + 1) * P, :]).then_inc(part_in[t], 16)

        @block.vector
        def _(dve):
            dve.sem_inc(totals, 2)
            dve.sem_inc(inverted, 2)

            def differences(n, s):
                peak = part[:, :, n, :, DIL_HD]
                dve.wait_ge(part_in[n], 16)
                dve.tensor_tensor(top[:, s], peak[:, 0], peak[:, 1], ALU.max).then_inc(topped, 1)
                dve.wait_ge(topped, 2 * n + 1)
                dve.tensor_tensor(top[:, s], top[:, s], peak[:, 2], ALU.max).then_inc(topped, 1)
                dve.wait_ge(topped, 2 * n + 2)
                dve.tensor_tensor(weight[:, s], peak, top[:, s].unsqueeze(1).broadcast_to([P, 3, H]), ALU.subtract
                                  ).then_inc(diff, 1)

            def body(n, s, more):
                if more:
                    differences(n + 1, 1 - s)
                dve.wait_ge(weighed, n + 1)
                two = part[:, 0:2, n]
                dve.tensor_tensor(two, two, weight[:, s, 0:2].unsqueeze(3).broadcast_to([P, 2, H, DIL_OUT]),
                                  ALU.mult).then_inc(first_two, 1)
                dve.wait_ge(first_two, 2 * n + 1)
                dve.wait_ge(y_done, n + 1)
                dve.tensor_tensor(total[:, s], two[:, 0], two[:, 1], ALU.add).then_inc(first_two, 1)
                dve.wait_ge(first_two, 2 * n + 2)
                dve.wait_ge(third, n + 1)
                dve.tensor_tensor(total[:, s], total[:, s], part[:, 2, n], ALU.add).then_inc(totals, 1)
                dve.wait_ge(totals, 2 + n + 1)
                dve.reciprocal(inverse[:, s], total[:, s, :, DIL_HD + 1:DIL_HD + 2]).then_inc(inverted, 1)

            differences(0, 0)
            for n in range(TT):
                body(n, n % 2, n + 1 < TT)

        @block.gpsimd
        def _(pool):
            pool.sem_inc(y_done, 2)

            def divide(n, s):
                pool.wait_ge(inverted, 2 + n + 1)
                pool.wait_ge(turned, n + 1)
                pool.tensor_tensor(y[:, s], total[:, s, :, 0:DIL_HD], inverse[:, s].broadcast_to([P, H, DIL_HD]),
                                   ALU.mult).then_inc(y_done, 1)

            def body(n, s, more):
                pool.wait_ge(weighed, n + 1)
                pool.tensor_tensor(part[:, 2, n], part[:, 2, n],
                                   weight[:, s, 2].unsqueeze(2).broadcast_to([P, H, DIL_OUT]), ALU.mult
                                   ).then_inc(third, 1)
                divide(n, s)

            for n in range(TT):
                body(n, n % 2, n + 1 < TT)

        @block.scalar
        def _(act):
            act.sem_inc(copied, 2)

            def weigh(n, s):
                act.wait_ge(diff, n + 1)
                flat = weight[:, s].rearrange("p b h -> p (b h)")
                act.activation(flat, flat, ACT.Exp).then_inc(weighed, 1)

            def body(n, s, more):
                if more:
                    weigh(n + 1, 1 - s)
                act.wait_ge(turned, 2 + n + 1)
                act.copy(a[:, K0:K0 + KC, ds(n * P, P)], turn_ps[:, s]).then_inc(copied, 1)

            weigh(0, 0)
            by_pairs(act, body)

        @block.tensor
        def _(pe):
            pe.sem_inc(turned, 2)

            def body(n, s, more):
                pe.wait_ge(y_done, 2 + n + 1)
                pe.wait_ge(copied, n + 1)
                flat = y[:, s].rearrange("p h e -> p (h e)")
                for c in range(KC):
                    mm = pe.transpose(turn_ps[:, s, c], flat[:, c * P:(c + 1) * P], ident[:])
                mm.then_inc(turned, 1)

            by_pairs(pe, body)


def conv_tokens(nc, name, xhi, xlo, w, taps_dram, ident, n_tiles, out):
    with ExitStack() as ctx:
        sc = Scope(nc, ctx, name)
        w_raw = sc.sbuf("w_raw", [P, 2, KD, P])
        w_hi = sc.sbuf("w_hi", [P, 2, KD, P], F32R)
        w_lo = sc.sbuf("w_lo", [P, 2, KD, P], F32R)
        conv = sc.sbuf("conv", [P, 2, SEQ])
        rows = sc.sbuf("rows", [P, 2, TT, P])
        taps = sc.sbuf("taps", [P, n_tiles, GDN_CONV])
        acc = sc.psum("acc", [P, 2, SEQ])
        turn = sc.psum("turn", [P, 2, TT, P])
        taps_in = sc.sem("taps_in")
        w_in = [sc.sem(f"w_in{s}") for s in range(2)]
        hi_ready = sc.sem("hi_ready")
        lo_ready = sc.sem("lo_ready")
        prod_done = sc.sem("prod_done")
        tap_done = sc.sem("tap_done")
        tap_added = sc.sem("tap_added")
        acc_free = sc.sem("acc_free")
        silu_done = sc.sem("silu_done")
        turned = sc.sem("turned")
        copied = sc.sem("copied")
        stored = [sc.sem(f"stored{s}") for s in range(2)]
        block = ctx.enter_context(nc.Block())

        def tap(j, c):
            return taps[:, ds(j, 1), c:c + 1].rearrange("p a c -> p (a c)")

        def by_tile_pairs(eng, body):
            with eng.Fori(0, n_tiles // 2 - 1) as i:
                for s in range(2):
                    body(2 * i + s, s, True, True)
            body(n_tiles - 2, 0, True, False)
            body(n_tiles - 1, 1, False, False)

        @block.sync
        def _(sp):
            sp.dma_start(taps[:], taps_dram).then_inc(taps_in, 16)
            with sp.Fori(0, n_tiles // 2) as i:
                for s in range(2):
                    j = 2 * i + s
                    sp.wait_ge(lo_ready, j + 1)
                    sp.dma_start(w_raw[:, s], w[ds(j, 1)].rearrange("a p k n -> p (a k) n")).then_inc(w_in[s], 16)

        @block.tensor
        def _(pe):
            pe.sem_inc(prod_done, 2)
            pe.sem_inc(turned, 2)

            def products(j, s):
                pe.wait_ge(lo_ready, 2 + j + 1)
                pe.wait_ge(acc_free, j + 1)
                for k in range(KD):
                    for ww, xx in ((w_hi, xhi), (w_hi, xlo), (w_lo, xhi)):
                        for hf in range(2):
                            tok = slice(hf * HALF, (hf + 1) * HALF)
                            mm = pe.matmul(acc[:, s, tok], ww[:, s, k], xx[:, k, tok],
                                           start=(k == 0 and ww is w_hi and xx is xhi),
                                           stop=(k == KD - 1 and ww is w_lo))
                mm.then_inc(prod_done, 1)

            def body(j, s, one, two):
                if one:
                    products(j + 1, 1 - s)
                pe.wait_ge(silu_done, j + 1)
                pe.wait_ge(copied, j + 1)
                for t in range(TT):
                    mm = pe.transpose(turn[:, s, t], conv[:, s, t * P:(t + 1) * P], ident[:])
                mm.then_inc(turned, 1)

            products(0, 0)
            by_tile_pairs(pe, body)

        @block.scalar
        def _(act):
            act.sem_inc(copied, 2)
            act.sem_inc(stored[0], 16)
            act.sem_inc(stored[1], 16)

            def split_hi(j, s):
                act.wait_ge(w_in[s], 8 * (j - s) + 16)
                act.wait_ge(prod_done, j + 1)
                act.copy(w_hi[:, s], w_raw[:, s]).then_inc(hi_ready, 1)

            def last_tap(j, s):
                act.wait_ge(prod_done, 2 + j + 1)
                act.wait_ge(turned, j + 1)
                act.activation(conv[:, s], acc[:, s], ACT.Copy, scale=tap(j, GDN_CONV - 1)).then_inc(tap_done, 1)

            def finish(j, s):
                act.wait_ge(acc_free, 2 + j + 1)
                act.activation(conv[:, s], conv[:, s], ACT.Silu).then_inc(silu_done, 1)

            def copy_out(j, s):
                act.wait_ge(turned, 2 + j + 1)
                act.wait_ge(stored[s], 8 * (j - s) + 16)
                act.copy(rows[:, s], turn[:, s]).then_inc(copied, 1)
                act.wait_ge(copied, 2 + j + 1)
                act.dma_start(out[:, :, ds(j * P, P)].rearrange("t p n -> p t n"), rows[:, s]).then_inc(stored[s], 16)

            def body(j, s, one, two):
                last_tap(j, s)
                if two:
                    split_hi(j + 2, s)
                finish(j, s)
                copy_out(j, s)

            act.wait_ge(taps_in, 16)
            split_hi(0, 0)
            split_hi(1, 1)
            by_tile_pairs(act, body)
            for s in range(2):
                act.wait_ge(stored[s], 16 + 16 * (n_tiles // 2))

        @block.vector
        def _(dve):
            dve.sem_inc(lo_ready, 2)
            dve.sem_inc(acc_free, 2)

            def split_lo(j, s):
                dve.wait_ge(hi_ready, j + 1)
                dve.tensor_tensor(w_lo[:, s], w_raw[:, s], f32(w_hi[:, s]), ALU.subtract).then_inc(lo_ready, 1)

            def body(j, s, one, two):
                dve.wait_ge(tap_done, j + 1)
                for back in range(1, GDN_CONV):
                    if back > 1:
                        dve.wait_ge(tap_added, 2 * j + back - 1)
                    dve.scalar_tensor_tensor(out=conv[:, s, back:SEQ], in0=acc[:, s, 0:SEQ - back],
                                             scalar=tap(j, GDN_CONV - 1 - back), in1=conv[:, s, back:SEQ],
                                             op0=ALU.mult, op1=ALU.add
                                             ).then_inc(tap_added if back < GDN_CONV - 1 else acc_free, 1)
                if two:
                    split_lo(j + 2, s)

            dve.wait_ge(taps_in, 16)
            split_lo(0, 0)
            split_lo(1, 1)
            by_tile_pairs(dve, body)


def project_decay(sc, lent, xhi, xlo, w_dram, a_log, dt_bias, upper, ident, beta, gates):
    H = GDN_HEADS
    g, gc, exp_gc, exp_rest, exp_all = gates
    w_raw = sc.sbuf("w_raw", [P, KD, 2 * H])
    w_hi = sc.sbuf("w_hi", [P, KD, 2 * H], F32R)
    w_lo = sc.sbuf("w_lo", [P, KD, 2 * H], F32R)
    rate = sc.sbuf("rate", [P, H])
    dt = sc.sbuf("dt", [P, H])
    ones = sc.sbuf("ones", [P, P])
    t = [sc.sbuf(f"t{i}", [P, TT, H]) for i in range(8)]
    rows = sc.sbuf("rows", [2 * H, SEQ])
    acc = lent[0][:, 0:TT * 2 * H].rearrange("p (t h) -> p t h", t=TT)
    sums, whole = (lent[1][:, c * TT * H:(c + 1) * TT * H] for c in range(2))
    loaded = sc.sem("loaded")
    split = sc.sem("split")
    rows_done = sc.sem("rows_done")
    rows_copied = sc.sem("rows_copied")
    projected = sc.sem("projected")
    a_step = sc.sem("a_step")
    d_step = sc.sem("d_step")
    summed = sc.sem("summed")

    def loads(sp):
        sp.dma_start(w_raw[:], w_dram).then_inc(loaded, 16)
        sp.dma_start(rate[:], a_log.broadcast_to([P, H])).then_inc(loaded, 16)
        sp.dma_start(dt[:], dt_bias.broadcast_to([P, H])).then_inc(loaded, 16)

    def project(pe):
        pe.wait_ge(split, 2)
        for k in range(KD):
            for ww, xx in ((w_hi, xhi), (w_hi, xlo), (w_lo, xhi)):
                for hf in range(2):
                    mm = pe.matmul(lent[hf][0:2 * H], ww[:, k], xx[:, k, hf * HALF:(hf + 1) * HALF],
                                   start=(k == 0 and ww is w_hi and xx is xhi), stop=(k == KD - 1 and ww is w_lo))
        mm.then_inc(rows_done, 1)

    def turn(pe):
        pe.wait_ge(rows_copied, 2)
        for tt in range(TT):
            mm = pe.transpose(acc[:, tt], rows[:, tt * P:(tt + 1) * P], ident[0:2 * H, 0:2 * H])
        mm.then_inc(projected, 1)

    def sum_chunks(pe):
        pe.wait_ge(d_step, 17)
        pe.matmul(sums, upper[:], g[:].rearrange("p t h -> p (t h)"), start=True, stop=True)
        pe.matmul(whole, ones[:], g[:].rearrange("p t h -> p (t h)"), start=True, stop=True).then_inc(summed, 1)
        pe.wait_ge(d_step, 20)

    def split_hi(act):
        act.wait_ge(loaded, 48)
        act.copy(w_hi[:], w_raw[:]).then_inc(split, 1)

    def exponentials(act):
        act.activation(rate[:], rate[:], ACT.Exp).then_inc(a_step, 1)
        act.wait_ge(d_step, 4)
        act.activation(t[1][:], t[1][:], ACT.Exp).then_inc(a_step, 1)
        act.wait_ge(d_step, 5)
        act.activation(t[0][:], t[0][:], ACT.Exp, scale=-1.0).then_inc(a_step, 1)
        act.wait_ge(d_step, 6)
        act.activation(t[3][:], t[2][:], ACT.Ln).then_inc(a_step, 1)
        act.wait_ge(d_step, 20)
        act.activation(exp_gc[:], gc[:], ACT.Exp).then_inc(a_step, 1)
        act.activation(exp_rest[:], exp_rest[:], ACT.Exp).then_inc(a_step, 1)
        act.activation(exp_all[:], exp_all[:], ACT.Exp).then_inc(a_step, 1)

    def split_lo(dve):
        dve.wait_ge(split, 1)
        dve.tensor_tensor(w_lo[:], w_raw[:], f32(w_hi[:]), ALU.subtract).then_inc(split, 1)

    def gate_steps(dve):
        count = [0]

        def step(op):
            count[0] += 1
            op.then_inc(d_step, 1)
            dve.wait_ge(d_step, count[0])

        step(dve.memset(ones[:], 1.0))
        dve.wait_ge(rows_done, 1)
        for hf in range(2):
            dve.tensor_copy(rows[:, hf * HALF:(hf + 1) * HALF], lent[hf][0:2 * H]).then_inc(rows_copied, 1)
        dve.wait_ge(projected, 1)
        step(dve.tensor_tensor(t[4][:], acc[:, :, H:2 * H], dt[:].unsqueeze(1).broadcast_to([P, TT, H]), ALU.add))
        step(dve.tensor_scalar(t[1][:], t[4][:], -1.0, None, ALU.mult))
        step(dve.tensor_tensor(t[1][:], t[1][:], t[4][:], ALU.min))
        step(dve.tensor_copy(t[0][:], acc[:, :, 0:H]))
        dve.wait_ge(a_step, 2)
        step(dve.tensor_scalar(t[2][:], t[1][:], 1.0, None, ALU.add))
        step(dve.tensor_scalar(t[5][:], t[2][:], -1.0, None, ALU.add))
        step(dve.tensor_scalar(t[6][:], t[5][:], 0.0, None, ALU.is_equal))
        step(dve.tensor_tensor(t[5][:], t[5][:], t[6][:], ALU.add))
        step(dve.reciprocal(t[5][:], t[5][:]))
        dve.wait_ge(a_step, 4)
        step(dve.tensor_tensor(t[3][:], t[3][:], t[5][:], ALU.mult))
        step(dve.tensor_tensor(t[3][:], t[3][:], t[6][:], ALU.add))
        step(dve.tensor_tensor(t[3][:], t[3][:], t[1][:], ALU.mult))
        step(dve.tensor_scalar(t[4][:], t[4][:], 0.0, None, ALU.max))
        step(dve.tensor_tensor(t[4][:], t[4][:], t[3][:], ALU.add))
        step(dve.tensor_tensor(t[4][:], t[4][:], rate[:].unsqueeze(1).broadcast_to([P, TT, H]), ALU.mult))
        step(dve.tensor_scalar(g[:], t[4][:], -1.0, None, ALU.mult))
        step(dve.tensor_scalar(t[7][:], t[0][:], 1.0, None, ALU.add))
        dve.reciprocal(beta[:], t[7][:]).then_inc(split, 1)
        dve.wait_ge(summed, 1)
        step(dve.tensor_copy(gc[:].rearrange("p t h -> p (t h)"), sums))
        dve.tensor_copy(exp_all[:].rearrange("p t h -> p (t h)"), whole).then_inc(split, 1)
        step(dve.tensor_tensor(exp_rest[:].rearrange("p t h -> p (t h)"), whole,
                               gc[:].rearrange("p t h -> p (t h)"), ALU.subtract))

    return Beside(loads=loads, act_early=split_hi, dve_early=split_lo, pe_early=project, pe_between=turn,
                  dve_late=gate_steps, act_late=exponentials, pe_halfway=sum_chunks)


LEVELS = 6


def delta_constants():
    i = np.arange(P)
    upper = (i[None, :] >= i[:, None]).astype(np.float32)
    first = -((i[:, None] // 2 == i[None, :] // 2) & (i[:, None] < i[None, :])).astype(np.float32)
    joins = []
    for level in range(1, LEVELS + 1):
        b = 2 ** level
        joins.append((i[:, None] // (2 * b) == i[None, :] // (2 * b)) & (i[:, None] % (2 * b) >= b) & (i[None, :] % (2 * b) < b))
    return upper, first, np.stack(joins).astype(np.float32)


def delta_rule(nc, qkv, gate_dram, norm_w, first_dram, joins_dram, upper, ident, beta, gates, a):
    H = GDN_HEADS
    HG = H // 2
    g, gc, exp_gc, exp_rest, exp_all = gates
    with ExitStack() as ctx:
        sc = Scope(nc, ctx, "gdn")
        x = sc.sbuf("x", [P, 2, 3 * H, P])
        gate = sc.sbuf("gate", [P, 2, H, P])
        squares = sc.sbuf("squares", [P, 2 * H, P])
        sumsq = sc.sbuf("sumsq", [P, 2 * H])
        norm = sc.sbuf("norm", [P, 2 * H])
        norm_scale = sc.sbuf("norm_scale", [P, 2 * H])
        norm_eps = sc.sbuf("norm_eps", [P, 2 * H])
        power = sc.sbuf("power", [P, 2 * H])
        rms_eps = sc.sbuf("rms_eps", [P, H])
        factor = sc.sbuf("factor", [P, 4, H])
        k_n = sc.sbuf("k_n", [P, H, P])
        k_b = sc.sbuf("k_b", [P, H, P])
        q_n = sc.sbuf("q_n", [P, H, P])
        q_d = sc.sbuf("q_d", [P, H, P])
        k_be = sc.sbuf("k_be", [P, 2, H, P])
        k_d = sc.sbuf("k_d", [P, 2, H, P])
        v_b = sc.sbuf("v_b", [P, 2, H, P])
        k_nt = sc.sbuf("k_nt", [P, H, P])
        k_bt = sc.sbuf("k_bt", [P, H, P])
        q_nt = sc.sbuf("q_nt", [P, H, P])
        q_dt = sc.sbuf("q_dt", [P, 2, H, P])
        g_rep = sc.sbuf("g_rep", [P, H, P])
        neg_gc = sc.sbuf("neg_gc", [P, TT, H])
        decay = sc.sbuf("decay", [P, H, P])
        b_mat = sc.sbuf("b_mat", [P, H, P])
        attn = sc.sbuf("attn", [P, 2, H, P])
        xt = sc.sbuf("xt", [P, 2, H, P])
        xm = sc.sbuf("xm", [P, H, P])
        t_m = sc.sbuf("t_m", [P, H, P])
        w_t = sc.sbuf("w_t", [P, H, P])
        v_new = sc.sbuf("v_new", [P, H, P])
        state = sc.sbuf("state", [P, 2, H, P])
        y = sc.sbuf("y", [P, H, P])
        o_sumsq = sc.sbuf("o_sumsq", [P, H])
        o_norm = sc.sbuf("o_norm", [P, H])
        weight = sc.sbuf("weight", [P, P])
        first = sc.sbuf("first", [P, P])
        joins = sc.sbuf("joins", [P, LEVELS, P])
        bank = sc.psum("bank", [P, 8, NB])
        pairs = [bank[:, 2 * i:2 * i + 2].rearrange("p b (h t) -> p (b h) t", t=P) for i in range(4)]
        consts_in = sc.sem("consts_in")
        consts_set = sc.sem("consts_set")
        x_in = [sc.sem(f"x_in{s}") for s in range(2)]
        slot_seen = sc.sem("slot_seen")
        gate_in = [sc.sem(f"gate_in{s}") for s in range(2)]
        squared = sc.sem("squared")
        sq_summed = sc.sem("sq_summed")
        norm_step = sc.sem("norm_step")
        norm_seen = sc.sem("norm_seen")
        kn_done = sc.sem("kn_done")
        kb_done = sc.sem("kb_done")
        qn_done = sc.sem("qn_done")
        pool_ops = sc.sem("pool_ops")
        g_done = sc.sem("g_done")
        g_rows = sc.sem("g_rows")
        decay_exp = sc.sem("decay_exp")
        decay_done = sc.sem("decay_done")
        kn_turned, kn_copied = sc.sem("kn_turned"), sc.sem("kn_copied")
        kb_turned, kb_copied = sc.sem("kb_turned"), sc.sem("kb_copied")
        qn_turned, qn_copied = sc.sem("qn_turned"), sc.sem("qn_copied")
        qd_turned, qd_copied = sc.sem("qd_turned"), sc.sem("qd_copied")
        kk_done, b_done = sc.sem("kk_done"), sc.sem("b_done")
        qk_done, attn_done = sc.sem("qk_done"), sc.sem("attn_done")
        first_done = sc.sem("first_done")
        t_done, tm_done = sc.sem("t_done"), sc.sem("tm_done")
        d_done, xt_done = sc.sem("d_done"), sc.sem("xt_done")
        x_done, x_copied = sc.sem("x_done"), sc.sem("x_copied")
        wt_done, wt_copied = sc.sem("wt_done"), sc.sem("wt_copied")
        v_done, v_copied = sc.sem("v_done"), sc.sem("v_copied")
        o_done, o_copied = sc.sem("o_done"), sc.sem("o_copied")
        o_squared, o_summed = sc.sem("o_squared"), sc.sem("o_summed")
        o_norm_step = sc.sem("o_norm_step")
        kv_done = sc.sem("kv_done")
        state_done = sc.sem("state_done")
        silu_done, gated = sc.sem("silu_done"), sc.sem("gated")
        y_done = sc.sem("y_done")
        y_turned = sc.sem("y_turned")
        y_copied = sc.sem("y_copied")
        XD = 1 + 2 * LEVELS

        block = ctx.enter_context(nc.Block())

        def per_head(ap):
            return ap.unsqueeze(2).broadcast_to([P, H, P])

        def heads(ap):
            return ap.unsqueeze(1).broadcast_to([P, H, P])

        def group(ap, q):
            return ap[:, q * HG:(q + 1) * HG]

        @block.sync
        def _(sp):
            sp.dma_start(weight[:], norm_w.broadcast_to([P, P])).then_inc(consts_in, 16)
            sp.dma_start(first[:], first_dram).then_inc(consts_in, 16)
            sp.dma_start(joins[:], joins_dram.rearrange("l p n -> p l n")).then_inc(consts_in, 16)
            with sp.Fori(0, TT // 2) as i:
                for s in range(2):
                    n = 2 * i + s
                    sp.wait_ge(pool_ops, 4 * n + 4)
                    sp.sem_inc(slot_seen, 1)
                    sp.wait_ge(kb_done, n + 1)
                    sp.wait_ge(qn_done, n + 1)
                    sp.dma_start(x[:, s].rearrange("p h d -> p (h d)"),
                                 qkv[ds(n, 1)].rearrange("a p n -> (a p) n")).then_inc(x_in[s], 16)
                    sp.wait_ge(y_done, 8 * n + 8)
                    sp.dma_start(gate[:, s].rearrange("p h d -> p (h d)"), gate_dram[ds(n * P, P), :]
                                 ).then_inc(gate_in[s], 16)

        @block.tensor
        def _(pe):
            pe.sem_inc(y_turned, 1)

            def turn(dst, src, done):
                for h in range(H):
                    mm = pe.transpose(dst[:, h], src[:, h], ident[:])
                mm.then_inc(done, 1)

            def front(m, step, s):
                if step == 1:
                    pe.wait_ge(g_done, m + 1)
                    for h in range(H):
                        mm = pe.matmul(pairs[2][:, h], g_rep[:, h], upper[:], start=True, stop=True)
                    mm.then_inc(g_rows, 1)
                if step == 3:
                    pe.wait_ge(kn_done, m + 1)
                    pe.wait_ge(state_done, 16 + 8 * m - 8)
                    turn(pairs[3], k_n, kn_turned)
                if step == 4:
                    pe.wait_ge(kb_done, 2 + m + 1)
                    pe.wait_ge(decay_exp, 8 * m + 8)
                    turn(pairs[2], k_b, kb_turned)
                if step == 5:
                    pe.wait_ge(qn_done, 2 + m + 1)
                    pe.wait_ge(kn_copied, m + 1)
                    turn(pairs[3], q_n, qn_turned)
                if step == 6:
                    pe.wait_ge(kb_copied, m + 1)
                    pe.wait_ge(y_copied, m + 1)
                    for h in range(H):
                        mm = pe.matmul(pairs[2][:, h], k_nt[:, h], k_bt[:, h], start=True, stop=True)
                    mm.then_inc(kk_done, 1)
                    pe.wait_ge(pool_ops, 8 + 4 * m + 1)
                    pe.wait_ge(qn_copied, m + 1)
                    turn(pairs[3], q_d, qd_turned)
                if step == 7:
                    pe.wait_ge(b_done, m + 1)
                    for h in range(H):
                        mm = pe.matmul(pairs[2][:, h], k_nt[:, h], q_nt[:, h], start=True, stop=True)
                    mm.then_inc(qk_done, 1)

            def first_x(m, s):
                pe.wait_ge(xt_done, XD * m + 1)
                pe.wait_ge(attn_done, 1 + m + 1)
                for q in range(2):
                    for h in range(HG):
                        mm = pe.transpose(group(pairs[2], q)[:, h], group(xt[:, s], q)[:, h], ident[:])
                    mm.then_inc(x_done, 1)

            def level(n, s, l):
                for q in range(2):
                    pe.wait_ge(x_copied, 2 * LEVELS * n + 2 * l - 1 + q)
                    for h in range(HG):
                        mm = pe.matmul(group(pairs[0], q)[:, h], group(b_mat, q)[:, h], group(xm, q)[:, h],
                                       start=True, stop=True)
                    mm.then_inc(t_done, 1)
                if l == 1:
                    pe.wait_ge(o_copied, 1 + n)
                for q in range(2):
                    pe.wait_ge(tm_done, 2 * LEVELS * n + 2 * l - 1 + q)
                    for h in range(HG):
                        mm = pe.matmul(group(pairs[1], q)[:, h], group(t_m, q)[:, h], group(xt[:, s], q)[:, h],
                                       start=True, stop=True)
                    mm.then_inc(d_done, 1)
                if l < LEVELS:
                    for q in range(2):
                        pe.wait_ge(xt_done, XD * n + 2 * l + q)
                        for h in range(HG):
                            mm = pe.transpose(group(pairs[0], q)[:, h], group(xt[:, s], q)[:, h], ident[:])
                        mm.then_inc(x_done, 1)

            def back(n, s, one):
                if one:
                    pe.wait_ge(qd_copied, n + 2)
                for h in range(H):
                    if h % HG == 0:
                        pe.wait_ge(xt_done, XD * n + XD - 1 + h // HG)
                    mm = pe.matmul(pairs[3][:, h], k_be[:, s, h], xt[:, s, h], start=True, stop=True)
                mm.then_inc(wt_done, 1)
                if one:
                    front(n + 1, 7, 1 - s)
                pe.wait_ge(wt_copied, n + 1)
                pe.wait_ge(state_done, 16 + 8 * n)
                for h in range(H):
                    pe.matmul(pairs[0][:, h], xt[:, s, h], v_b[:, s, h], start=True, stop=False)
                    mm = pe.matmul(pairs[0][:, h], w_t[:, h], state[:, s, h], start=False, stop=True)
                mm.then_inc(v_done, 1)
                if one:
                    first_x(n + 1, 1 - s)
                pe.wait_ge(v_copied, n + 1)
                for h in range(H):
                    mm = pe.matmul(pairs[3][:, h], k_d[:, s, h], v_new[:, h], start=True, stop=True)
                mm.then_inc(kv_done, 1)
                for h in range(H):
                    pe.matmul(pairs[1][:, h], q_dt[:, s, h], state[:, s, h], start=True, stop=False)
                    mm = pe.matmul(pairs[1][:, h], attn[:, s, h], v_new[:, h], start=False, stop=True)
                mm.then_inc(o_done, 1)

            def output(n):
                pe.wait_ge(y_done, 16 + 8 * n + 8)
                turn(pairs[2], y, y_turned)

            def body(n, s, prev, one, two):
                for l in range(1, LEVELS + 1):
                    level(n, s, l)
                    if l == 5 and prev:
                        if one:
                            pe.wait_ge(kb_copied, n + 2)
                        output(n - 1)
                    if one:
                        front(n + 1, l, 1 - s)
                back(n, s, one)

            for step in range(1, 8):
                front(0, step, 0)
            first_x(0, 0)
            by_chunks(pe, body)
            output(TT - 1)

        @block.scalar
        def _(act):
            act.sem_inc(y_copied, 2)
            act.sem_inc(o_copied, 1)
            act.wait_ge(consts_set, 7)

            def copy(dst, src, ready, count, done, scale=1.0):
                act.wait_ge(ready, count)
                (act.copy(dst, src) if scale == 1.0 else act.mul(dst, src, scale)).then_inc(done, 1)

            def front(m, step, s):
                if step == 0:
                    act.wait_ge(x_in[s], 8 * (m - s) + 16)
                    act.wait_ge(o_summed, m)
                    act.activation(squares[:], x[:, s, 0:2 * H], ACT.Square).then_inc(squared, 1)
                    act.wait_ge(g_rows, 1 + m)
                    act.copy(g_rep[:], g[:, ds(m, 1), :].rearrange("p a h -> p (a h)").unsqueeze(2)
                             .broadcast_to([P, H, P])).then_inc(g_done, 1)
                if step == 1:
                    act.wait_ge(g_rows, 1 + m + 1)
                    act.wait_ge(attn_done, 1 + m)
                    for h in range(H):
                        act.activation(decay[:, h], pairs[2][:, h], ACT.Exp,
                                       bias=neg_gc[:, ds(m, 1), h:h + 1].rearrange("p a h -> p (a h)")
                                       ).then_inc(decay_exp, 1)
                if step == 3:
                    copy(k_nt[:], pairs[3], kn_turned, m + 1, kn_copied)
                if step == 4:
                    copy(k_bt[:], pairs[2], kb_turned, m + 1, kb_copied)
                if step == 5:
                    copy(q_nt[:], pairs[3], qn_turned, m + 1, qn_copied)
                if step == 6:
                    copy(q_dt[:, s], pairs[3], qd_turned, m + 1, qd_copied)

            def copy_x(n, l, src):
                for q in range(2):
                    copy(group(xm, q), group(src, q), x_done, 2 * LEVELS * n + 2 * l + q + 1, x_copied)

            def output(n):
                act.wait_ge(y_turned, 1 + n + 1)
                act.copy(a[:, 0:H, ds(n * P, P)], pairs[2]).then_inc(y_copied, 1)

            def square_outputs(n, fronts):
                act.wait_ge(o_copied, 1 + n + 1)
                act.wait_ge(sq_summed, fronts)
                act.activation(squares[:, 0:H], y[:], ACT.Square, scale=GDN_DV ** -0.5).then_inc(o_squared, 1)

            def body(n, s, prev, one, two):
                for l in range(1, LEVELS + 1):
                    if l < LEVELS:
                        copy_x(n, l, pairs[0])
                    if l == 1 and prev:
                        square_outputs(n - 1, n + 2 if one else TT)
                    if one:
                        front(n + 1, l, 1 - s)
                    if l == 5 and prev:
                        output(n - 1)
                copy(w_t[:], pairs[3], wt_done, n + 1, wt_copied, scale=-1.0)
                if two:
                    front(n + 2, 0, s)
                copy(v_new[:], pairs[0], v_done, n + 1, v_copied)
                if one:
                    copy_x(n + 1, 0, pairs[2])
                act.wait_ge(gate_in[s], 8 * (n - s) + 16)
                act.activation(gate[:, s], gate[:, s], ACT.Silu).then_inc(silu_done, 1)
                act.wait_ge(y_turned, 1 + n)
                copy(y[:], pairs[1], o_done, n + 1, o_copied)

            for step in range(8):
                front(0, step, 0)
            front(1, 0, 1)
            copy_x(0, 0, pairs[2])
            by_chunks(act, body)
            square_outputs(TT - 1, TT)
            output(TT - 1)

        @block.vector
        def _(dve):
            dve.sem_inc(g_rows, 1)
            dve.sem_inc(o_summed, 2)
            dve.sem_inc(kb_done, 2)
            dve.sem_inc(qn_done, 2)
            dve.sem_inc(attn_done, 1)
            dve.sem_inc(y_done, 16)
            dve.memset(state[:, 0], 0.0).then_inc(state_done, 16)
            dve.memset(norm_scale[:, 0:H], float(GDN_DK)).then_inc(consts_set, 1)
            dve.memset(norm_scale[:, H:2 * H], 1.0).then_inc(consts_set, 1)
            dve.memset(norm_eps[:, 0:H], 1e-6 * GDN_DK).then_inc(consts_set, 1)
            dve.memset(norm_eps[:, H:2 * H], 1e-6).then_inc(consts_set, 1)
            dve.memset(power[:], -0.5).then_inc(consts_set, 1)
            dve.memset(rms_eps[:], EPS).then_inc(consts_set, 1)
            dve.tensor_scalar(neg_gc[:], gc[:], -1.0, None, ALU.mult).then_inc(consts_set, 1)
            dve.wait_ge(consts_in, 48)

            def front(m, step, s):
                if step == 0:
                    dve.wait_ge(squared, m + 1)
                    dve.tensor_reduce(sumsq[:], squares[:], AX.X, ALU.add).then_inc(sq_summed, 1)
                if step == 5:
                    dve.wait_ge(decay_exp, 8 * m + 8)
                    dve.tensor_tensor(decay[:], decay[:], heads(upper[:]), ALU.min).then_inc(decay_done, 1)
                if step == 2:
                    dve.wait_ge(norm_step, 7 * m + 3)
                    dve.tensor_tensor(k_n[:], x[:, s, H:2 * H], per_head(norm[:, H:2 * H]), ALU.mult).then_inc(kn_done, 1)
                if step == 3:
                    dve.wait_ge(norm_step, 7 * m + 7)
                    dve.tensor_tensor(k_b[:], x[:, s, H:2 * H], per_head(factor[:, 0]), ALU.mult).then_inc(kb_done, 1)
                if step == 4:
                    dve.tensor_tensor(q_n[:], x[:, s, 0:H], per_head(norm[:, 0:H]), ALU.mult).then_inc(qn_done, 1)
                if step == 6:
                    dve.wait_ge(kk_done, m + 1)
                    dve.wait_ge(decay_done, m + 1)
                    dve.tensor_tensor(b_mat[:], pairs[2], decay[:], ALU.mult).then_inc(b_done, 1)
                    dve.wait_ge(b_done, m + 1)
                    dve.tensor_tensor(xt[:, s], b_mat[:], heads(first[:]), ALU.mult).then_inc(first_done, 1)
                    dve.wait_ge(first_done, m + 1)
                    dve.tensor_tensor(xt[:, s], xt[:, s], heads(ident[:]), ALU.add).then_inc(xt_done, 1)
                if step == 7:
                    dve.wait_ge(qk_done, m + 1)
                    dve.tensor_tensor(attn[:, s], pairs[2], decay[:], ALU.mult).then_inc(attn_done, 1)

            def level(n, s, l):
                for q in range(2):
                    dve.wait_ge(t_done, 2 * LEVELS * n + 2 * l - 1 + q)
                    dve.tensor_tensor(group(t_m, q), group(pairs[0], q),
                                      joins[:, l - 1].unsqueeze(1).broadcast_to([P, HG, P]), ALU.mult
                                      ).then_inc(tm_done, 1)
                for q in range(2):
                    dve.wait_ge(d_done, 2 * LEVELS * n + 2 * l - 1 + q)
                    dve.tensor_tensor(group(xt[:, s], q), group(xt[:, s], q), group(pairs[1], q),
                                      ALU.subtract).then_inc(xt_done, 1)

            def sum_outputs(n):
                dve.wait_ge(o_squared, n + 1)
                dve.tensor_reduce(o_sumsq[:], squares[:, 0:H], AX.X, ALU.add).then_inc(o_summed, 1)

            def output(n, s):
                dve.wait_ge(o_norm_step, 2 * n + 2)
                dve.wait_ge(gated, n + 1)
                for h in range(H):
                    dve.scalar_tensor_tensor(out=y[:, h], in0=y[:, h], scalar=o_norm[:, h:h + 1],
                                             in1=gate[:, s, h], op0=ALU.mult, op1=ALU.mult).then_inc(y_done, 1)

            def body(n, s, prev, one, two):
                for l in range(1, LEVELS + 1):
                    level(n, s, l)
                    if l == 1 and prev:
                        sum_outputs(n - 1)
                    if one:
                        front(n + 1, l, 1 - s)
                    if l == 3 and prev:
                        output(n - 1, 1 - s)
                if one:
                    front(n + 1, 7, 1 - s)
                if two:
                    front(n + 2, 0, s)
                dve.wait_ge(kv_done, n + 1)
                dve.wait_ge(state_done, 16 + 8 * n)
                for h in range(H):
                    dve.scalar_tensor_tensor(out=state[:, 1 - s, h], in0=state[:, s, h],
                                             scalar=exp_all[:, ds(n, 1), h:h + 1].rearrange("p a h -> p (a h)"),
                                             in1=pairs[3][:, h], op0=ALU.mult, op1=ALU.add).then_inc(state_done, 1)

            for step in range(8):
                front(0, step, 0)
            front(1, 0, 1)
            by_chunks(dve, body)
            sum_outputs(TT - 1)
            output(TT - 1, 1)

        @block.gpsimd
        def _(pool):
            pool.sem_inc(pool_ops, 8)
            pool.wait_ge(consts_set, 7)
            pool.wait_ge(consts_in, 48)

            def at(table, m):
                return table[:, ds(m, 1), :].rearrange("p a h -> p (a h)")

            def norms(m):
                pool.wait_ge(sq_summed, m + 1)
                pool.tensor_tensor(norm[:], sumsq[:], norm_scale[:], ALU.mult).then_inc(norm_step, 1)
                pool.wait_ge(norm_step, 7 * m + 1)
                pool.tensor_tensor(norm[:], norm[:], norm_eps[:], ALU.add).then_inc(norm_step, 1)
                pool.wait_ge(norm_step, 7 * m + 2)
                pool.tensor_tensor(norm[:], norm[:], power[:], ALU.pow).then_inc(norm_step, 1)
                pool.wait_ge(norm_step, 7 * m + 3)
                pool.sem_inc(norm_seen, 1)
                pool.tensor_tensor(factor[:, 0], norm[:, H:2 * H], at(beta, m), ALU.mult).then_inc(norm_step, 1)
                pool.tensor_tensor(factor[:, 2], norm[:, H:2 * H], at(exp_rest, m), ALU.mult).then_inc(norm_step, 1)
                pool.tensor_tensor(factor[:, 3], norm[:, 0:H], at(exp_gc, m), ALU.mult).then_inc(norm_step, 1)
                pool.wait_ge(norm_step, 7 * m + 4)
                pool.sem_inc(norm_seen, 1)
                pool.tensor_tensor(factor[:, 1], factor[:, 0], at(exp_gc, m), ALU.mult).then_inc(norm_step, 1)

            def front(m, s):
                pool.wait_ge(norm_step, 7 * m + 7)
                pool.tensor_tensor(q_d[:], x[:, s, 0:H], per_head(factor[:, 3]), ALU.mult).then_inc(pool_ops, 1)
                pool.tensor_tensor(k_be[:, s], x[:, s, H:2 * H], per_head(factor[:, 1]), ALU.mult).then_inc(pool_ops, 1)
                pool.tensor_tensor(k_d[:, s], x[:, s, H:2 * H], per_head(factor[:, 2]), ALU.mult).then_inc(pool_ops, 1)
                pool.tensor_tensor(v_b[:, s], x[:, s, 2 * H:3 * H], per_head(at(beta, m)), ALU.mult
                                   ).then_inc(pool_ops, 1)

            def output_norm(n):
                pool.wait_ge(o_summed, 2 + n + 1)
                pool.tensor_tensor(o_norm[:], o_sumsq[:], rms_eps[:], ALU.add).then_inc(o_norm_step, 1)
                pool.wait_ge(o_norm_step, 2 * n + 1)
                pool.tensor_tensor(o_norm[:], o_norm[:], power[:, 0:H], ALU.pow).then_inc(o_norm_step, 1)

            def body(n, s, prev, one, two):
                if prev:
                    output_norm(n - 1)
                if one:
                    front(n + 1, 1 - s)
                if two:
                    pool.wait_ge(kb_done, 2 + n + 2)
                    pool.wait_ge(qn_done, 2 + n + 2)
                    norms(n + 2)
                pool.wait_ge(silu_done, n + 1)
                pool.tensor_tensor(gate[:, s], gate[:, s], heads(weight[:]), ALU.mult).then_inc(gated, 1)

            norms(0)
            front(0, 0)
            pool.wait_ge(kb_done, 2 + 1)
            pool.wait_ge(qn_done, 2 + 1)
            norms(1)
            by_chunks(pool, body)
            output_norm(TT - 1)


def build(nc, t, out):
    def dram(name, shape):
        return nc.dram_tensor(name, shape, F32).ap()

    hp = dram("hp", [SEQ, EV_IN])
    parts = dram("parts", [3, SEQ, DIL_HEADS * DIL_OUT])
    qkv = dram("qkv", [TT, P, 3 * GDN_W])
    gate = dram("gate", [SEQ, GDN_W])
    x1, x2, x3 = (dram(f"x{i}", [SEQ, D]) for i in (1, 2, 3))

    def k_rows(w):
        return w.rearrange("(k p) n -> k p n", p=P)

    def split_operand(ctx, name):
        sc = Scope(nc, ctx, name)
        return [sc.sbuf(part, [P, KD, SEQ], F32R, side="right") for part in ("hi", "lo")]

    def even_mixer(ident, next_ctx):
        with ExitStack() as ctx:
            with ExitStack() as inner:
                tables = Scope(nc, inner, "even_rot")
                cos = tables.sbuf("cos", [P, TT, ROT], side="right")
                sin = tables.sbuf("sin", [P, TT, ROT], side="right")
                with ExitStack() as x_ctx:
                    x_hi, x_lo = split_operand(x_ctx, "even_x")
                    project_tokens(nc, "even_in", x_hi, x_lo, t["ev_w_in"], EV_IN // NB, hp, t["x_turned"],
                                   lambda sc, lent: rotary_tables(sc, t["positions"], t["inv_freq"], cos, sin))
                mixed = Scope(nc, ctx, "even").sbuf("mixed", [P, EV_MIX // P, SEQ])
                _, _, chunk_decay = retention_constants()
                retention(nc, hp, t["ret_mask"], t["ret_factor"], chunk_decay, ident, cos, sin, mixed)
            with ExitStack() as inner:
                gathered = Scope(nc, inner, "even_parts").sbuf("gathered", [P, 3, TT, DIL_HEADS * DIL_OUT])
                dilated(nc, hp, t["dil_masks"], ident, parts, gathered)
                combine_dilated(nc, parts, gathered, ident, mixed)
            hi, lo = split_operand(next_ctx, "ffn0_x")
            project_out(nc, "even_out", mixed, EV_MIX // P, k_rows(t["ev_w_out"]), t["x"],
                        t["ln1_g"][0:1], t["ln1_b"][0:1], ident, x1, hi, lo)
        return hi, lo

    def odd_mixer(ident, upper, x_hi, x_lo, x_ctx, next_ctx):
        with ExitStack() as ctx:
            small = Scope(nc, next_ctx, "odd_small")
            beta, *gates = [small.sbuf(name, [P, TT, GDN_HEADS], side="right")
                            for name in ("beta", "g", "gc", "exp_gc", "exp_rest", "exp_all")]
            conv_tokens(nc, "odd_qkv", x_hi, x_lo, t["od_w_qkv"], t["od_taps"], ident, 3 * GDN_W // P, qkv)
            project_tokens(nc, "odd_gate", x_hi, x_lo, t["od_w_gate"], GDN_W // NB, gate, None,
                           lambda sc, lent: project_decay(sc, lent, x_hi, x_lo, t["od_w_ba"], t["od_a_log"],
                                                          t["od_dt_bias"], upper, ident, beta, gates))
            x_ctx.close()
            mixed = Scope(nc, ctx, "odd").sbuf("mixed", [P, KD, SEQ])
            delta_rule(nc, qkv, gate, t["od_norm_w"], t["delta_first"], t["delta_joins"], upper, ident, beta,
                       gates, mixed)
            hi, lo = split_operand(next_ctx, "ffn1_x")
            project_out(nc, "odd_out", mixed, KD, k_rows(t["od_w_out"]), x2, t["ln1_g"][1:2], t["ln1_b"][1:2],
                        ident, x3, hi, lo)
        return hi, lo

    with ExitStack() as top_ctx:
        top = Scope(nc, top_ctx, "top")
        ident = top.sbuf("ident", [P, P])
        upper = top.sbuf("upper", [P, P])
        load_constants(nc, [(ident, t["ident"]), (upper, t["upper"])])

        h_ctx = top_ctx.enter_context(ExitStack())
        with ExitStack() as x_ctx:
            hi, lo = even_mixer(ident, x_ctx)
            h = Scope(nc, h_ctx, "ffn0").sbuf("h", [P, KF, SEQ])
            ffn_up(nc, "ffn0_up", hi, lo, t["ffn_up0"], t["ffn_taps0"], h)
        h_ctx.close()
        x2_ctx = top_ctx.enter_context(ExitStack())
        place = Scope(nc, x2_ctx, "odd_x")
        x2_hi, x2_lo = (place.sbuf(part, [P, KD, SEQ], F32R) for part in ("hi", "lo"))
        place.sbuf("rest_of_h", [P, KF - 2 * KD, SEQ])
        project_out(nc, "ffn0_down", h, KF, k_rows(t["ffn_down0"]), x1, t["ln2_g"][0:1], t["ln2_b"][0:1],
                    ident, x2, x2_hi, x2_lo)

        with ExitStack() as next_h_ctx:
            with ExitStack() as x_ctx:
                hi, lo = odd_mixer(ident, upper, x2_hi, x2_lo, x2_ctx, x_ctx)
                h = Scope(nc, next_h_ctx, "ffn1").sbuf("h", [P, KF, SEQ])
                ffn_up(nc, "ffn1_up", hi, lo, t["ffn_up1"], t["ffn_taps1"], h)
            project_out(nc, "ffn1_down", h, KF, k_rows(t["ffn_down1"]), x3, t["ln2_g"][1:2], t["ln2_b"][1:2],
                        ident, out)


def load_constants(nc, pairs):
    with ExitStack() as ctx:
        loaded = Scope(nc, ctx, "const").sem("loaded")
        block = ctx.enter_context(nc.Block())

        @block.sync
        def _(sp):
            for dst, src in pairs:
                sp.dma_start(dst[:], src).then_inc(loaded, 16)
            sp.wait_ge(loaded, 16 * len(pairs))


def lay_out(inputs):
    given = {name: np.asarray(a) for name, a in inputs.items()}
    arrays = {
        "x": given["x"][0],
        "x_turned": given["x"][0].reshape(SEQ, KD, P).transpose(2, 1, 0),
        "positions": given["positions"][0].reshape(TT, P).T,
        "ev_w_in": given["ev_w_in"][0].reshape(KD, P, EV_IN // NB, NB).transpose(2, 1, 0, 3),
        "ev_w_out": given["ev_w_out"][0],
        "od_w_out": given["od_w_out"][0],
        "od_a_log": given["od_a_log"],
        "od_dt_bias": given["od_dt_bias"],
        "od_norm_w": given["od_norm_w"],
        "od_taps": given["od_conv_w"][0].reshape(GDN_CONV, 3 * GDN_W // P, P).transpose(2, 1, 0),
    }
    w = given["od_w_in"][0]
    arrays["od_w_qkv"] = w[:, :3 * GDN_W].reshape(KD, P, 3 * GDN_W // P, P).transpose(2, 1, 0, 3)
    arrays["od_w_gate"] = w[:, 3 * GDN_W:4 * GDN_W].reshape(KD, P, GDN_W // NB, NB).transpose(2, 1, 0, 3)
    arrays["od_w_ba"] = w[:, 4 * GDN_W:].reshape(KD, P, 2 * GDN_HEADS).transpose(1, 0, 2)
    for layer in range(2):
        taps = np.concatenate([given["ffn_conv_w"][layer], given["ffn_conv_b"][layer][None]], 0)
        arrays[f"ffn_taps{layer}"] = taps.reshape(FFN_CONV + 1, 2, KF, P).transpose(3, 2, 1, 0)
        arrays[f"ffn_up{layer}"] = given["ffn_w_up"][layer].reshape(KD, P, 2, KF, P).transpose(3, 1, 2, 0, 4)
        arrays[f"ffn_down{layer}"] = given["ffn_w_down"][layer]
    for name in ("ln1_g", "ln1_b", "ln2_g", "ln2_b"):
        arrays[name] = given[name]

    arrays["ident"] = np.eye(P, dtype=np.float32)
    arrays["upper"], arrays["delta_first"], arrays["delta_joins"] = delta_constants()
    arrays["ret_mask"], arrays["ret_factor"], _ = retention_constants()
    arrays["dil_masks"] = dilated_masks()
    arrays["inv_freq"] = inverse_frequencies()
    return {name: np.ascontiguousarray(array) for name, array in arrays.items()}


def kernel(**inputs):
    import concourse.bacc as bacc
    from concourse.bass_utils import run_bass_kernel_spmd

    nc = bacc.Bacc("TRN2", target_bir_lowering=False, num_devices=1)
    tensors, feeds = {}, {}
    for name, a in lay_out(inputs).items():
        feeds[f"in_{name}"] = a
        tensors[name] = nc.dram_tensor(f"in_{name}", a.shape, mybir.dt.from_np(a.dtype), kind="ExternalInput").ap()
    out = nc.dram_tensor("out_y", [SEQ, D], F32, kind="ExternalOutput").ap()
    build(nc, tensors, out)
    result = run_bass_kernel_spmd(nc, [feeds], core_ids=[0])
    return result.results[0]["out_y"].reshape(1, SEQ, D)
```
